# Optimizing a Trainium2 kernel written in Bass

```python
import math
import jax
import jax.numpy as jnp
from jax import lax
import numpy as np

D_MODEL = 2048
BATCH = 1
SEQ = 128
DEPTH = 2
DEC_BATCH = 1
DEC_SEQ = 128
PAST_LEN = 128

GRID_W = 64
ROPE_THETA = 10000.0
Q_BLOCK = 128
EPS = 1e-6
HEAD_DIM = 128
N_EVEN = (DEPTH + 1) // 2
N_ODD = DEPTH // 2

DA_HEADS = 8
DA_SUB = HEAD_DIM // 2
GQ_HEADS = 8
GQ_KV_HEADS = 2
GQ_REP = GQ_HEADS // GQ_KV_HEADS
ML_HEADS = 8
ML_DK = 128
ML_DV = 128
ML_CHUNK = 64
ML_CONV = 3
MLA_HEADS = 8
MLA_Q_RANK = 512
MLA_KV_RANK = 256
MLA_NOPE = 128
MLA_ROPE = 64
MLA_V = 128
D_FF = 5632
FFN_CONV = 3

EVEN_WIDTHS = (DA_HEADS * HEAD_DIM, DA_HEADS * HEAD_DIM, DA_HEADS * HEAD_DIM,
               GQ_HEADS * HEAD_DIM, GQ_KV_HEADS * HEAD_DIM, GQ_KV_HEADS * HEAD_DIM)
ODD_WIDTHS = (ML_HEADS * ML_DK, ML_HEADS * ML_DK, ML_HEADS * ML_DV, ML_HEADS * ML_DV,
              4 * ML_HEADS, MLA_Q_RANK, MLA_KV_RANK, MLA_ROPE)
EVEN_IN = sum(EVEN_WIDTHS)
ODD_IN = sum(ODD_WIDTHS)
EVEN_MIX = DA_HEADS * HEAD_DIM + GQ_HEADS * HEAD_DIM
ODD_MIX = ML_HEADS * ML_DV + MLA_HEADS * MLA_V

kernel_name = 'hybrid_diffusion_prefix_trunk_step'

def _split(x, widths):
    offs, acc = [], 0
    for w in widths[:-1]:
        acc += w
        offs.append(acc)
    return jnp.split(x, offs, axis=-1)

def _rms(x, g):
    xf = x.astype(jnp.float32)
    y = xf * lax.rsqrt(jnp.mean(xf * xf, axis=-1, keepdims=True) + EPS)
    return (y * g.astype(jnp.float32)).astype(x.dtype)

def _adaln(cvec, w, b):
    m = (jax.nn.silu(cvec) @ w + b)[:, None, :]
    return jnp.split(m, 6, axis=-1)

def _modulate(x, g, shift, scale):
    return _rms(x, g) * (1 + scale) + shift

def _dwconv(x, w, b):
    width = w.shape[0]
    pad = width // 2
    n = x.shape[1]
    xp = jnp.pad(x, ((0, 0), (pad, pad), (0, 0)))
    y = b
    for i in range(width):
        y = y + xp[:, i:i + n] * w[i]
    return y

def _rope_tables(grid_rows, dim):
    t = jnp.arange(grid_rows * GRID_W)
    r = (t // GRID_W).astype(jnp.float32)
    col = (t % GRID_W).astype(jnp.float32)
    quarter = dim // 4
    inv = ROPE_THETA ** (-jnp.arange(quarter, dtype=jnp.float32) / quarter)
    ang = jnp.stack([r[:, None] * inv, col[:, None] * inv], axis=1)
    return jnp.cos(ang), jnp.sin(ang)

def _rope(x, cos, sin):
    quarter = x.shape[-1] // 4
    xr = x.astype(jnp.float32).reshape(x.shape[:-1] + (2, 2, quarter))
    x1, x2 = xr[..., 0, :], xr[..., 1, :]
    out = jnp.stack([x1 * cos - x2 * sin, x1 * sin + x2 * cos], axis=-2)
    return out.reshape(x.shape).astype(x.dtype)

def _over_query_blocks(fn, queries):
    n_q = queries[0].shape[-2]
    nb = n_q // Q_BLOCK

    def split(a):
        a = a.reshape(a.shape[:-2] + (nb, Q_BLOCK, a.shape[-1]))
        return jnp.moveaxis(a, -3, 0)

    out = lax.map(lambda blk: fn(*blk), tuple(split(a) for a in queries))
    out = jnp.moveaxis(out, 0, -3)
    return out.reshape(out.shape[:-3] + (n_q, out.shape[-1]))

def _diff_attention(q, k, v, lam, ln_g, lam_init):
    scale = DA_SUB ** -0.5

    def block(qb):
        s = jnp.einsum('bhcqd,bhckd->bhcqk', qb, k, preferred_element_type=jnp.float32) * scale
        a = jax.nn.softmax(s, axis=-1)
        w = a[:, :, 0] - lam * a[:, :, 1]
        return jnp.einsum('bhqk,bhkd->bhqd', w.astype(v.dtype), v)

    o = _over_query_blocks(block, (q,))
    return _rms(o, ln_g) * (1.0 - lam_init)

def _gqa(q, k, v):
    scale = HEAD_DIM ** -0.5

    def block(qb):
        s = jnp.einsum('bgrqd,bgkd->bgrqk', qb, k, preferred_element_type=jnp.float32) * scale
        a = jax.nn.softmax(s, axis=-1)
        return jnp.einsum('bgrqk,bgkd->bgrqd', a.astype(v.dtype), v)

    return _over_query_blocks(block, (q,))

def _mla_attention(q_nope, q_pe, k_nope, k_pe, v):
    scale = (MLA_NOPE + MLA_ROPE) ** -0.5

    def block(qn, qp):
        s = (jnp.einsum('bhqd,bhkd->bhqk', qn, k_nope, preferred_element_type=jnp.float32)
             + jnp.einsum('bhqd,bkd->bhqk', qp, k_pe, preferred_element_type=jnp.float32)) * scale
        a = jax.nn.softmax(s, axis=-1)
        return jnp.einsum('bhqk,bhkd->bhqd', a.astype(v.dtype), v)

    return _over_query_blocks(block, (q_nope, q_pe))

def _mla_kv(ckv, w_ukv):
    b_, s_, _ = ckv.shape
    kv = (ckv @ w_ukv).reshape(b_, s_, MLA_HEADS, MLA_NOPE + MLA_V).transpose(0, 2, 1, 3)
    return kv[..., :MLA_NOPE], kv[..., MLA_NOPE:]

def _mlstm_scan(q, k, v, log_i, log_f, c0, n0, m0):
    b_, h_, n_tok, _ = q.shape
    nc = n_tok // ML_CHUNK
    f32 = jnp.float32

    def chunks(a):
        a = a.astype(f32)
        a = a.reshape(a.shape[:2] + (nc, ML_CHUNK) + a.shape[3:])
        return jnp.moveaxis(a, 2, 0)

    tril = jnp.tril(jnp.ones((ML_CHUNK, ML_CHUNK), dtype=bool))

    def step(carry, inp):
        cst, nst, mst = carry
        qc, kc, vc, li, lf = inp
        bcum = jnp.cumsum(lf, axis=-1)
        d_intra = jnp.where(tril, bcum[..., :, None] - bcum[..., None, :] + li[..., None, :], -jnp.inf)
        d_inter = bcum + mst[..., None]
        m_t = jnp.maximum(d_inter, jnp.max(d_intra, axis=-1))
        s = jnp.einsum('bhtd,bhsd->bhts', qc, kc) * jnp.exp(d_intra - m_t[..., None])
        a = jnp.exp(d_inter - m_t)
        num = jnp.einsum('bhts,bhsv->bhtv', s, vc) + a[..., None] * jnp.einsum('bhtd,bhdv->bhtv', qc, cst)
        den = jnp.sum(s, axis=-1) + a * jnp.einsum('bhtd,bhd->bht', qc, nst)
        h = num / jnp.maximum(jnp.abs(den), jnp.exp(-m_t))[..., None]
        b_end = bcum[..., -1]
        g = b_end[..., None] - bcum + li
        m_new = jnp.maximum(b_end + mst, jnp.max(g, axis=-1))
        wg = jnp.exp(g - m_new[..., None])
        decay = jnp.exp(b_end + mst - m_new)
        c_new = decay[..., None, None] * cst + jnp.einsum('bhs,bhsd,bhsv->bhdv', wg, kc, vc)
        n_new = decay[..., None] * nst + jnp.einsum('bhs,bhsd->bhd', wg, kc)
        return (c_new, n_new, m_new), h

    init = (c0.astype(f32), n0.astype(f32), m0.astype(f32))
    (c_fin, n_fin, m_fin), hs = lax.scan(step, init, (chunks(q), chunks(k), chunks(v), chunks(log_i), chunks(log_f)))
    h = jnp.moveaxis(hs, 0, 2).reshape(b_, h_, n_tok, hs.shape[-1])
    return h, c_fin, n_fin, m_fin

def _mlstm_mixer(qm, km, vm, om, gates, gate_b, norm_g, c0, n0, m0):
    b_, h_, n_tok, _ = qm.shape
    g = (gates + gate_b).astype(jnp.float32).reshape(b_, n_tok, 4, ML_HEADS).transpose(2, 0, 3, 1)
    i_f, lf_f = g[0], jax.nn.log_sigmoid(g[1])
    i_b, lf_b = g[2], jax.nn.log_sigmoid(g[3])
    h_f, c_f, n_f, m_f = _mlstm_scan(qm, km, vm, i_f, lf_f, c0[:, 0], n0[:, 0], m0[:, 0])

    def rev(a):
        return jnp.flip(a, axis=2)

    h_b, c_b, n_b, m_b = _mlstm_scan(rev(qm), rev(km), rev(vm), rev(i_b), rev(lf_b), c0[:, 1], n0[:, 1], m0[:, 1])
    h = _rms(h_f + rev(h_b), norm_g)
    h = h.transpose(0, 2, 1, 3).reshape(b_, n_tok, h_ * ML_DV).astype(om.dtype) * jax.nn.sigmoid(om)
    return h, (jnp.stack([c_f, c_b], axis=1), jnp.stack([n_f, n_b], axis=1), jnp.stack([m_f, m_b], axis=1))

def _even_heads(h, w_in, q_norm_g, k_norm_g):
    b_, n_tok, _ = h.shape
    qa, ka, va, qb, kb, vb = _split(h @ w_in, EVEN_WIDTHS)

    def sub(a):
        return a.reshape(b_, n_tok, DA_HEADS, 2, DA_SUB).transpose(0, 2, 3, 1, 4)

    qa, ka = sub(qa), sub(ka)
    va = va.reshape(b_, n_tok, DA_HEADS, HEAD_DIM).transpose(0, 2, 1, 3)
    qb = _rms(qb.reshape(b_, n_tok, GQ_KV_HEADS, GQ_REP, HEAD_DIM), q_norm_g).transpose(0, 2, 3, 1, 4)
    kb = _rms(kb.reshape(b_, n_tok, GQ_KV_HEADS, HEAD_DIM), k_norm_g).transpose(0, 2, 1, 3)
    vb = vb.reshape(b_, n_tok, GQ_KV_HEADS, HEAD_DIM).transpose(0, 2, 1, 3)
    return qa, ka, va, qb, kb, vb

def _even_merge(oa, ob, w_out):
    b_, _, n_tok, _ = oa.shape
    oa = oa.transpose(0, 2, 1, 3).reshape(b_, n_tok, DA_HEADS * HEAD_DIM)
    ob = ob.transpose(0, 3, 1, 2, 4).reshape(b_, n_tok, GQ_HEADS * HEAD_DIM)
    return jnp.concatenate([oa, ob], axis=-1) @ w_out

def _odd_heads(h, w_in, conv_w, conv_b, q_norm_g, w_uq, kv_norm_g):
    b_, n_tok, _ = h.shape
    qm, km, vm, om, gates, q_down, kv_down, k_pe = _split(h @ w_in, ODD_WIDTHS)
    qk = jax.nn.silu(_dwconv(jnp.concatenate([qm, km], axis=-1), conv_w, conv_b))
    qm, km = jnp.split(qk, 2, axis=-1)

    def heads(a, d):
        return a.reshape(b_, n_tok, ML_HEADS, d).transpose(0, 2, 1, 3)

    qm = heads(qm, ML_DK) * (ML_DK ** -0.5)
    km = heads(km, ML_DK)
    vm = heads(vm, ML_DV)
    cq = (_rms(q_down, q_norm_g) @ w_uq).reshape(b_, n_tok, MLA_HEADS, MLA_NOPE + MLA_ROPE).transpose(0, 2, 1, 3)
    ckv = _rms(kv_down, kv_norm_g)
    return qm, km, vm, om, gates, cq[..., :MLA_NOPE], cq[..., MLA_NOPE:], ckv, k_pe

def _odd_merge(h_ml, h_mla, w_out):
    b_, _, n_tok, _ = h_mla.shape
    h_mla = h_mla.transpose(0, 2, 1, 3).reshape(b_, n_tok, MLA_HEADS * MLA_V)
    return jnp.concatenate([h_ml, h_mla], axis=-1) @ w_out

def _conv_ffn(h, w_up, conv_w, conv_b, w_down):
    u = _dwconv(h @ w_up, conv_w, conv_b)
    g, up = jnp.split(u, 2, axis=-1)
    return (jax.nn.silu(g) * up) @ w_down

def setup_inputs(seed: int = 0) -> dict:
    key = jax.random.key(seed)
    keys = iter(jax.random.split(key, 64))

    def nrm(shape, scale=1.0):
        return scale * jax.random.normal(next(keys), shape, dtype=jnp.float32)

    def gain(shape):
        return 1.0 + 0.05 * nrm(shape)

    D = D_MODEL
    f_bias = jnp.linspace(3.0, 6.0, ML_HEADS, dtype=jnp.float32)
    i_bias = jnp.zeros((ML_HEADS,), jnp.float32)
    gate_base = jnp.concatenate([i_bias, f_bias, i_bias, f_bias])
    return dict(
        x_prompt=nrm((BATCH, SEQ, D)),
        x_sample=nrm((DEC_BATCH, DEC_SEQ, D)),
        cache_da_k=nrm((DEC_BATCH, N_EVEN, DA_HEADS, 2, PAST_LEN, DA_SUB)),
        cache_da_v=nrm((DEC_BATCH, N_EVEN, DA_HEADS, PAST_LEN, HEAD_DIM)),
        cache_gq_k=nrm((DEC_BATCH, N_EVEN, GQ_KV_HEADS, PAST_LEN, HEAD_DIM)),
        cache_gq_v=nrm((DEC_BATCH, N_EVEN, GQ_KV_HEADS, PAST_LEN, HEAD_DIM)),
        cache_mla_ckv=nrm((DEC_BATCH, N_ODD, PAST_LEN, MLA_KV_RANK)),
        cache_mla_kpe=nrm((DEC_BATCH, N_ODD, PAST_LEN, MLA_ROPE)),
        state_ml_C=nrm((DEC_BATCH, N_ODD, 2, ML_HEADS, ML_DK, ML_DV)),
        state_ml_n=nrm((DEC_BATCH, N_ODD, 2, ML_HEADS, ML_DK)),
        state_ml_m=nrm((DEC_BATCH, N_ODD, 2, ML_HEADS)),
        c=nrm((DEC_BATCH, D)),
        c_ctx=nrm((D,)),
        norm1_g=gain((DEPTH, D)),
        norm2_g=gain((DEPTH, D)),
        w_mod=nrm((DEPTH, D, 6 * D), 0.5 * D ** -0.5),
        b_mod=nrm((DEPTH, 6 * D), 0.02),
        even_w_in=nrm((N_EVEN, D, EVEN_IN), D ** -0.5),
        even_w_out=nrm((N_EVEN, EVEN_MIX, D), EVEN_MIX ** -0.5),
        da_lambda=nrm((N_EVEN, 4, DA_SUB), 0.1),
        da_subln_g=gain((N_EVEN, HEAD_DIM)),
        gq_q_norm_g=gain((N_EVEN, HEAD_DIM)),
        gq_k_norm_g=gain((N_EVEN, HEAD_DIM)),
        odd_w_in=nrm((N_ODD, D, ODD_IN), D ** -0.5),
        odd_w_out=nrm((N_ODD, ODD_MIX, D), ODD_MIX ** -0.5),
        ml_conv_w=nrm((N_ODD, ML_CONV, 2 * ML_HEADS * ML_DK), ML_CONV ** -0.5),
        ml_conv_b=nrm((N_ODD, 2 * ML_HEADS * ML_DK), 0.02),
        ml_gate_b=gate_base[None, :] + nrm((N_ODD, 4 * ML_HEADS), 0.1),
        ml_norm_g=gain((N_ODD, ML_DV)),
        mla_q_norm_g=gain((N_ODD, MLA_Q_RANK)),
        mla_w_uq=nrm((N_ODD, MLA_Q_RANK, MLA_HEADS * (MLA_NOPE + MLA_ROPE)), MLA_Q_RANK ** -0.5),
        mla_kv_norm_g=gain((N_ODD, MLA_KV_RANK)),
        mla_w_ukv=nrm((N_ODD, MLA_KV_RANK, MLA_HEADS * (MLA_NOPE + MLA_V)), MLA_KV_RANK ** -0.5),
        ffn_w_up=nrm((DEPTH, D, 2 * D_FF), D ** -0.5),
        ffn_conv_w=nrm((DEPTH, FFN_CONV, 2 * D_FF), FFN_CONV ** -0.5),
        ffn_conv_b=nrm((DEPTH, 2 * D_FF), 0.02),
        ffn_w_down=nrm((DEPTH, D_FF, D), D_FF ** -0.5),
        final_norm_g=gain((D,)),
    )

def reference(x_prompt, x_sample, cache_da_k, cache_da_v, cache_gq_k, cache_gq_v,
              cache_mla_ckv, cache_mla_kpe, state_ml_C, state_ml_n, state_ml_m,
              c, c_ctx, norm1_g, norm2_g, w_mod, b_mod, even_w_in, even_w_out,
              da_lambda, da_subln_g, gq_q_norm_g, gq_k_norm_g, odd_w_in, odd_w_out,
              ml_conv_w, ml_conv_b, ml_gate_b, ml_norm_g, mla_q_norm_g, mla_w_uq,
              mla_kv_norm_g, mla_w_ukv, ffn_w_up, ffn_conv_w, ffn_conv_b, ffn_w_down,
              final_norm_g):
    grid_rows = x_sample.shape[1] // GRID_W
    cos_sub, sin_sub = _rope_tables(grid_rows, DA_SUB)
    cos_hd, sin_hd = _rope_tables(grid_rows, HEAD_DIM)
    cos_pe, sin_pe = _rope_tables(grid_rows, MLA_ROPE)
    b_ctx = x_prompt.shape[0]
    cond_ctx = c_ctx[None, :]
    xp, xs = x_prompt, x_sample
    da_k_l, da_v_l, gq_k_l, gq_v_l = [], [], [], []
    ckv_l, kpe_l, mC_l, mn_l, mm_l = [], [], [], [], []
    for l in range(DEPTH):
        mod_p = _adaln(cond_ctx, w_mod[l], b_mod[l])
        mod_s = _adaln(c, w_mod[l], b_mod[l])
        hp = _modulate(xp, norm1_g[l], mod_p[0], mod_p[1])
        hs = _modulate(xs, norm1_g[l], mod_s[0], mod_s[1])
        j = l // 2
        if l % 2 == 0:
            lam_init = 0.8 - 0.6 * math.exp(-0.3 * l)
            lq1, lk1, lq2, lk2 = da_lambda[j].astype(jnp.float32)
            lam = jnp.exp(jnp.sum(lq1 * lk1)) - jnp.exp(jnp.sum(lq2 * lk2)) + lam_init
            qa, ka, va, qb, kb, vb = _even_heads(hp, even_w_in[j], gq_q_norm_g[j], gq_k_norm_g[j])
            out_p = _even_merge(_diff_attention(qa, ka, va, lam, da_subln_g[j], lam_init),
                                _gqa(qb, kb, vb), even_w_out[j])
            da_k_l.append(ka)
            da_v_l.append(va)
            gq_k_l.append(kb)
            gq_v_l.append(vb)
            qa, ka, va, qb, kb, vb = _even_heads(hs, even_w_in[j], gq_q_norm_g[j], gq_k_norm_g[j])
            ka = jnp.concatenate([cache_da_k[:, j], _rope(ka, cos_sub, sin_sub)], axis=3)
            va = jnp.concatenate([cache_da_v[:, j], va], axis=2)
            kb = jnp.concatenate([cache_gq_k[:, j], _rope(kb, cos_hd, sin_hd)], axis=2)
            vb = jnp.concatenate([cache_gq_v[:, j], vb], axis=2)
            out_s = _even_merge(_diff_attention(_rope(qa, cos_sub, sin_sub), ka, va, lam, da_subln_g[j], lam_init),
                                _gqa(_rope(qb, cos_hd, sin_hd), kb, vb), even_w_out[j])
        else:
            qm, km, vm, om, gates, q_nope, q_pe, ckv, k_pe = _odd_heads(
                hp, odd_w_in[j], ml_conv_w[j], ml_conv_b[j], mla_q_norm_g[j], mla_w_uq[j], mla_kv_norm_g[j])
            zc = jnp.zeros((b_ctx, 2, ML_HEADS, ML_DK, ML_DV), jnp.float32)
            zn = jnp.zeros((b_ctx, 2, ML_HEADS, ML_DK), jnp.float32)
            zm = jnp.zeros((b_ctx, 2, ML_HEADS), jnp.float32)
            h_ml, (st_c, st_n, st_m) = _mlstm_mixer(qm, km, vm, om, gates, ml_gate_b[j], ml_norm_g[j], zc, zn, zm)
            k_nope, v = _mla_kv(ckv, mla_w_ukv[j])
            out_p = _odd_merge(h_ml, _mla_attention(q_nope, q_pe, k_nope, k_pe, v), odd_w_out[j])
            ckv_l.append(ckv)
            kpe_l.append(k_pe)
            mC_l.append(st_c)
            mn_l.append(st_n)
            mm_l.append(st_m)
            qm, km, vm, om, gates, q_nope, q_pe, ckv, k_pe = _odd_heads(
                hs, odd_w_in[j], ml_conv_w[j], ml_conv_b[j], mla_q_norm_g[j], mla_w_uq[j], mla_kv_norm_g[j])
            h_ml = _mlstm_mixer(qm, km, vm, om, gates, ml_gate_b[j], ml_norm_g[j],
                                state_ml_C[:, j], state_ml_n[:, j], state_ml_m[:, j])[0]
            ckv_all = jnp.concatenate([cache_mla_ckv[:, j], ckv], axis=1)
            kpe_all = jnp.concatenate([cache_mla_kpe[:, j], _rope(k_pe, cos_pe, sin_pe)], axis=1)
            k_nope, v = _mla_kv(ckv_all, mla_w_ukv[j])
            out_s = _odd_merge(h_ml, _mla_attention(q_nope, _rope(q_pe, cos_pe, sin_pe), k_nope, kpe_all, v),
                               odd_w_out[j])
        xp = xp + mod_p[2] * out_p
        xs = xs + mod_s[2] * out_s
        hp = _modulate(xp, norm2_g[l], mod_p[3], mod_p[4])
        hs = _modulate(xs, norm2_g[l], mod_s[3], mod_s[4])
        xp = xp + mod_p[5] * _conv_ffn(hp, ffn_w_up[l], ffn_conv_w[l], ffn_conv_b[l], ffn_w_down[l])
        xs = xs + mod_s[5] * _conv_ffn(hs, ffn_w_up[l], ffn_conv_w[l], ffn_conv_b[l], ffn_w_down[l])
    y_prompt = _rms(xp, final_norm_g)
    y_sample = _rms(xs, final_norm_g)
    new_da_k = jnp.stack(da_k_l, axis=1)
    new_da_v = jnp.stack(da_v_l, axis=1)
    new_gq_k = jnp.stack(gq_k_l, axis=1)
    new_gq_v = jnp.stack(gq_v_l, axis=1)
    new_mla_ckv = jnp.stack(ckv_l, axis=1)
    new_mla_kpe = jnp.stack(kpe_l, axis=1)
    new_ml_C = jnp.stack(mC_l, axis=1)
    new_ml_n = jnp.stack(mn_l, axis=1)
    new_ml_m = jnp.stack(mm_l, axis=1)
    return (y_prompt, y_sample, new_da_k, new_da_v, new_gq_k, new_gq_v, new_mla_ckv, new_mla_kpe, new_ml_C, new_ml_n, new_ml_m)


_drawn_inputs = setup_inputs


def setup_inputs(seed=0):
    import zlib

    import numpy as np

    out = dict(_drawn_inputs(seed))
    spreads = {}
    factors = {'cache_gq_k': 4.724,
     'cache_gq_v': 3.764,
     'cache_mla_ckv': 3.994,
     'cache_mla_kpe': 7.241,
     'state_ml_C': 3.078,
     'state_ml_n': 8.0,
     'state_ml_m': 4.488,
     'da_lambda': 3.278,
     'da_subln_g': 2.97,
     'gq_q_norm_g': 8.0,
     'ml_norm_g': 8.0,
     'mla_q_norm_g': 8.0,
     'ffn_conv_b': 6.33}
    for name, (base, spread) in spreads.items():
        noise = np.random.default_rng([zlib.crc32(name.encode()), seed]).standard_normal(out[name].shape)
        drawn = base * np.exp(spread * noise) if base else spread * noise
        out[name] = jnp.asarray(drawn.astype(out[name].dtype))
    for name, factor in factors.items():
        out[name] = (out[name] * factor).astype(out[name].dtype)
    return out
```

```python
from contextlib import ExitStack

import concourse.bass as bass
import numpy as np
from concourse import mybir

F32 = mybir.dt.float32
F32R = mybir.dt.float32r
ALU = mybir.AluOpType
ACT = mybir.ActivationFunctionType
X_AXIS = mybir.AxisListType.X

P = 128
D = 2048
KD = D // P
T = 128
NT = 2 * T
DEPTH = 2
GRID_W = 64
EPS = 1e-6
HEADS = 8
KV_HEADS = 2
SUB = 64
Q_RANK, KV_RANK = 512, 256
NOPE = 128
D_FF = 5632
KF = D_FF // P
EVEN_TILES = 36
LAM_INIT = 0.8 - 0.6
MASKED = -1.0e30

RAW = 4
SPLIT = 2
CHUNKS = 4
SLABW = 512
GROUP = SLABW // P

C_IDENT, C_ONES, C_ROT_SUB, C_ROT_HD = 0, 128, 256, 384
C_COS_SUB, C_SIN_SUB, C_COS_HD, C_SIN_HD = 512, 640, 768, 896
C_MASK = 1024
C_SEL = 1280
C_SUM = 1408
NCONST = 1410


def constants():
    c = np.zeros((P, NCONST), np.float32)
    c[:, C_IDENT:C_IDENT + P] = np.eye(P)
    c[:, C_ONES:C_ONES + P] = 1.0
    t = np.arange(T)
    for width, rot, cos, sin in ((SUB, C_ROT_SUB, C_COS_SUB, C_SIN_SUB), (P, C_ROT_HD, C_COS_HD, C_SIN_HD)):
        quarter = width // 4
        inv = np.float32(10000.0) ** (-np.arange(quarter, dtype=np.float32) / quarter)
        for f in range(P):
            g = f % width
            axis, half, j = g // (2 * quarter), (g // quarter) % 2, g % quarter
            pos = (t // GRID_W if axis == 0 else t % GRID_W).astype(np.float32)
            angle = pos * inv[j]
            c[f, cos:cos + T] = np.cos(angle)
            c[f, sin:sin + T] = np.sin(angle)
            if half == 0:
                c[f + quarter, rot + f] = -1.0
            else:
                c[f - quarter, rot + f] = 1.0
    c[:, C_MASK:C_MASK + T] = np.where(t[:, None] <= t[None, :], 0.0, MASKED)
    c[:, C_MASK + T:C_MASK + 2 * T] = np.where(t[:, None] >= t[None, :], 0.0, MASKED)
    for direction in range(2):
        for kind in range(2):
            for stream in range(2):
                for h in range(HEADS):
                    col = C_SEL + 16 * (4 * direction + 2 * kind + stream) + 8 * stream + h
                    c[16 * direction + 8 * kind + h, col] = 1.0
    for stream in range(2):
        c[stream, C_SUM + stream] = 1.0
        c[2 + stream, C_SUM + stream] = 1.0
    return c


PARAMS = (
    ("b_mod", DEPTH * 6 * KD), ("norm1_g", DEPTH * KD), ("norm2_g", DEPTH * KD), ("final_norm_g", KD),
    ("ffn_conv_w", DEPTH * 3 * 2 * KF), ("ffn_conv_b", DEPTH * 2 * KF), ("ml_conv_w", 3 * 2 * HEADS),
    ("ml_conv_b", 2 * HEADS), ("c_ctx", KD), ("c", KD), ("da_subln_g", 1), ("gq_q_norm_g", 1),
    ("gq_k_norm_g", 1), ("ml_norm_g", 1), ("mla_q_norm_g", Q_RANK // P), ("mla_kv_norm_g", KV_RANK // P),
    ("state_ml_n", 2 * HEADS),
)
PCOL = {}
_at = 0
for _name, _rows in PARAMS:
    PCOL[_name] = _at
    _at += _rows
NPAR = _at
PAR_TILES = -(-NPAR // P)


class Tally:

    def __init__(self, sem):
        self.sem, self.base = sem, 0

    def at(self, n):
        return self.base + n

    def advance(self, n):
        self.base += n


def wait(eng, sem, value):
    if not isinstance(value, int) or value > 0:
        eng.wait_ge(sem, value)


class Phase:

    def __init__(self, load, iters, slabs, groups):
        self.load, self.iters, self.slabs, self.groups = load, iters, slabs, groups
        self.per_group = slabs // groups
        self.slab0 = self.group0 = 0
        self.slot0 = [0] * RAW
        self.before = [0] * RAW
        self.next = None

    def slab(self, i, s):
        return self.slab0 + i * self.slabs + s

    def group(self, i, g):
        return self.group0 + i * self.groups + g

    def loads_of(self, slot):
        return (self.slabs - slot + RAW - 1) // RAW if self.slabs > slot else 0


def plan(phases):
    slab = group = 0
    held, last = [0] * RAW, [0] * RAW
    for n, ph in enumerate(phases):
        ph.slab0, ph.group0, ph.slot0, ph.before = slab, group, list(held), list(last)
        for slot in range(RAW):
            k = ph.loads_of(slot)
            held[slot] += k * ph.iters
            if k:
                last[slot] = slab + (ph.iters - 1) * ph.slabs + slot + RAW * (k - 1) + 1
        slab += ph.iters * ph.slabs
        group += ph.iters * ph.groups
        ph.next = phases[n + 1] if n + 1 < len(phases) else None


def rolled(eng, iters, body):
    if iters == 1:
        body(0, True, True)
        return
    body(0, True, False)
    if iters > 2:
        with eng.Fori(1, iters - 1) as i:
            body(i, False, False)
    body(iters - 1, False, True)


def over(ap, n):
    return ap.unsqueeze(len(ap.shape)).broadcast_to([*ap.shape, n])


def trunk(nc, ins, outs):
    ctx = ExitStack()
    with ctx:
        def sb(name, shape, dt=F32, scope=ctx):
            return scope.enter_context(nc.sbuf_tensor(name, shape, dt))

        def tally(name):
            return Tally(ctx.enter_context(nc.semaphore(name)))

        raw = sb("raw", [P, RAW, CHUNKS, SLABW])
        w_hi = sb("w_hi", [P, SPLIT, CHUNKS, SLABW], F32R)
        w_lo = sb("w_lo", [P, SPLIT, CHUNKS, SLABW], F32R)
        x = sb("x", [P, KD, NT])
        const = sb("const", [P, NCONST])
        par = sb("par", [P, NPAR])
        mod = sb("mod", [P, DEPTH, 6 * KD, 2])
        norm_gain = sb("norm_gain", [P, DEPTH, 2, KD, 2])
        lam = sb("lam", [P, 1])
        gate_b = sb("gate_b", [4 * HEADS, 1])
        m0 = sb("m0", [2 * HEADS, 2])
        banks = ctx.enter_context(nc.psum_tensor("banks", [P, 8, 512], F32))

        ident = const[:, C_IDENT:C_IDENT + P]
        ones = const[:, C_ONES:C_ONES + P]

        landed = [tally(f"landed{s}") for s in range(RAW)]
        hi_done = tally("hi_done")
        lo_done = tally("lo_done")
        slab_used = tally("slab_used")
        part_copied = tally("part_copied")
        summed = tally("summed")
        gated = tally("gated")
        resid = tally("resid")
        rows_out = tally("rows_out")
        rows_turned = tally("rows_turned")
        mod_done = tally("mod_done")
        tap = [tally(f"tap{n}") for n in range(3)]
        silu_done = tally("silu_done")
        act_done = tally("act_done")
        mov_hi = tally("mov_hi")
        mov_lo = tally("mov_lo")
        small_in = tally("small_in")
        tokens_in = tally("tokens_in")
        lam_in = tally("lam_in")
        state_in = tally("state_in")
        pool_step = tally("pool_step")
        stored = tally("stored")
        pe_step = tally("pe_step")
        act_step = tally("act_step")
        dve_step = tally("dve_step")

        def columns(w, first, width=SLABW):
            v = w.rearrange("(s c p) n -> s p c n", c=CHUNKS, p=P)
            return lambda s, n0: v[s, :, :, bass.ds(n0, width) if not isinstance(n0, int) else slice(n0, n0 + width)]

        def plain(w, first, groups_per_iter, per_group):
            get = columns(w, first)

            def load(sp, slot, i, s):
                src = get(s % per_group, first + SLABW * (i * groups_per_iter + s // per_group))
                return sp.dma_start(raw[:, slot], src)
            return load

        def ffn_up_load(w):
            get = columns(w, 0)

            def load(sp, slot, i, s):
                return sp.dma_start(raw[:, slot], get(s % 4, SLABW * i + D_FF * (s // 4)))
            return load

        def odd_tail_load(w):
            def load(sp, slot, i, s):
                n0, width = ((4 * D // 2, 416), (4 * D // 2 + 416, 448))[s // 4]
                v = w.rearrange("(s c p) n -> s p c n", c=CHUNKS, p=P)
                return sp.dma_start(raw[:, slot, :, 0:width], v[s % 4, :, :, n0:n0 + width])
            return load

        def uq_load(sp, slot, i, s):
            v = ins["mla_w_uq"][0].rearrange("(c p) n -> p c n", p=P)
            return sp.dma_start(raw[:, slot, :, 0:384], v[:, :, 384 * s:384 * s + 384])

        def ukv_view(t):
            return t.rearrange("p c n -> p (c n)").rearrange("p (c n) -> p c n", c=KV_RANK // P)

        def ukv_load(sp, slot, i, s):
            v = ins["mla_w_ukv"][0].rearrange("(c p) n -> p c n", p=P)
            return sp.dma_start(ukv_view(raw[:, slot]), v[:, :, 1024 * s:1024 * s + 1024])

        ph = {}
        for l in range(DEPTH):
            ph["mod", l] = Phase(plain(ins["w_mod"][l], 0, 2, 4), 12, 8, 2)
        ph["even_in"] = Phase(plain(ins["even_w_in"][0], 0, 2, 4), 4, 8, 2)
        ph["even_in_end"] = Phase(plain(ins["even_w_in"][0], 8 * SLABW, 1, 4), 1, 4, 1)
        ph["out", 0] = Phase(plain(ins["even_w_out"][0], 0, 2, 4), 2, 8, 2)
        ph["odd_qk"] = Phase(plain(ins["odd_w_in"][0], 0, 2, 4), 2, 8, 2)
        ph["odd_vo"] = Phase(plain(ins["odd_w_in"][0], 4 * SLABW, 2, 4), 2, 8, 2)
        ph["odd_tail"] = Phase(odd_tail_load(ins["odd_w_in"][0]), 1, 8, 2)
        ph["uq"] = Phase(uq_load, 1, 4, 4)
        ph["ukv"] = Phase(ukv_load, 1, 2, 2)
        ph["out", 1] = Phase(plain(ins["odd_w_out"][0], 0, 2, 4), 2, 8, 2)
        for l in range(DEPTH):
            ph["up", l] = Phase(ffn_up_load(ins["ffn_w_up"][l]), 11, 8, 2)
            ph["down", l] = Phase(plain(ins["ffn_w_down"][l], 0, 2, 11), 2, 22, 2)
        order = [("mod", 0), ("mod", 1), "even_in", "even_in_end", ("out", 0), ("up", 0), ("down", 0),
                 "odd_qk", "odd_vo", "odd_tail", "uq", "ukv", ("out", 1), ("up", 1), ("down", 1)]
        plan([ph[k] for k in order])

        def load_slab(sp, f, i, s, in_slot_before):
            slot = s % RAW
            wait(sp, hi_done.sem, in_slot_before)
            wait(sp, lo_done.sem, in_slot_before)
            f.load(sp, slot, i, s).then_inc(landed[slot].sem, 16)

        def sp_first(sp, f):
            if f is not None:
                for s in range(min(RAW, f.slabs)):
                    load_slab(sp, f, 0, s, f.before[s])

        def sp_stream(sp, f):
            def body(i, first, last):
                for s in range(RAW, f.slabs):
                    load_slab(sp, f, i, s, f.slab(i, s - RAW) + 1)
                if last:
                    sp_first(sp, f.next)
                else:
                    for s in range(RAW):
                        newest = s + RAW * (f.loads_of(s) - 1)
                        load_slab(sp, f, i + 1, s, f.slab(i, newest) + 1)
            rolled(sp, f.iters, body)

        def slab_landed(f, i, s):
            slot = s % RAW
            return landed[slot].sem, 16 * (f.slot0[slot] + i * f.loads_of(slot) + s // RAW + 1)

        def split_hi(act, f, i, s):
            q = f.slab(i, s)
            act.wait_ge(*slab_landed(f, i, s))
            wait(act, slab_used.sem, q - SPLIT + 1)
            act.activation(w_hi[:, s % SPLIT], raw[:, s % RAW], ACT.Copy).then_inc(hi_done.sem, 1)

        def split_lo(dve, f, i, s):
            q = f.slab(i, s)
            dve.wait_ge(hi_done.sem, q + 1)
            wait(dve, slab_used.sem, q - SPLIT + 1)
            dve.tensor_tensor(w_lo[:, s % SPLIT], raw[:, s % RAW], w_hi[:, s % SPLIT].bitcast(F32),
                              ALU.subtract).then_inc(lo_done.sem, 1)

        def split_stream(eng, f, split, pieces, also=None):
            def body(i, first, last):
                for s in range(f.slabs):
                    ahead = s + SPLIT
                    if ahead < f.slabs:
                        split(eng, f, i, ahead)
                        if also:
                            also(i, ahead)
                    elif not last:
                        split(eng, f, i + 1, ahead - f.slabs)
                        if also:
                            also(i + 1, ahead - f.slabs)
                    elif f.next is not None:
                        split(eng, f.next, 0, ahead - f.slabs)
                    run_pieces(f, pieces, i, s, first)
            rolled(eng, f.iters, body)
            finish_pieces(f, pieces)

        def run_pieces(f, pieces, i, s, first):
            for g in range(f.groups):
                for d, piece in enumerate(pieces):
                    at = (g + 1) * f.per_group - 1 + d
                    if piece is not None and at == s:
                        piece(i, g)
                    elif piece is not None and at == s + f.slabs and not first:
                        piece(i - 1, g)

        def finish_pieces(f, pieces):
            for s in range(f.slabs, 2 * f.slabs):
                for g in range(f.groups):
                    for d, piece in enumerate(pieces):
                        if piece is not None and (g + 1) * f.per_group - 1 + d == s:
                            piece(f.iters - 1, g)

        def product_stream(pe, f, slab_products, pieces=()):
            def body(i, first, last):
                for s in range(f.slabs):
                    g = s // f.per_group
                    pe.wait_ge(lo_done.sem, f.slab(i, s) + 1)
                    if s % f.per_group == 0:
                        wait(pe, summed.sem, f.group(i, g) - 1)
                    slab_products(i, s, g).then_inc(slab_used.sem, 1)
                    run_pieces(f, pieces, i, s, first)
            rolled(pe, f.iters, body)
            finish_pieces(f, pieces)

        def tile_products(pe, slot, first_bank, moving, start, stop):
            for c in range(CHUNKS):
                for t in range(GROUP):
                    bank = banks[:, first_bank + t]
                    cols = slice(P * t, P * t + P)
                    pe.matmul(bank, w_hi[:, slot, c, cols], moving[:, c, :], start=start and c == 0, stop=False)
                    mm = pe.matmul(bank[:, 0:NT], w_lo[:, slot, c, cols], moving[:, c, 0:NT],
                                   start=False, stop=stop and c == CHUNKS - 1)
            return mm

        def group_banks(g):
            return slice(GROUP * (g % 2), GROUP * (g % 2) + GROUP)

        def split_products(pe, f, operand, moving_ready=None):
            def one(i, s, g):
                k = s % f.per_group
                if moving_ready is not None:
                    moving_ready(i, s)
                return tile_products(pe, s % SPLIT, GROUP * (g % 2), operand(s, k), k == 0, k == f.per_group - 1)
            product_stream(pe, f, one)

        cond = ExitStack()
        ctx.enter_context(cond)
        cond_split = sb("cond_split", [P, KD, 4], F32R, cond)
        with ExitStack() as scope:
            rows = sb("rows", [P, PAR_TILES, P], scope=scope)
            tokens = sb("tokens", [P, 2, D], scope=scope)
            cond_f = sb("cond_f", [P, KD, 2], scope=scope)
            lam_rows = sb("lam_rows", [P, 4 * SUB], scope=scope)
            lam_prod = sb("lam_prod", [P, 2 * SUB], scope=scope)
            lam_sum = sb("lam_sum", [P, 2], scope=scope)
            first = ph[order[0]]

            pieces_in = []
            for name, n in PARAMS:
                flat = ins[name].rearrange(
                    {1: "(n p) -> n p", 2: "a (n p) -> (a n) p", 3: "a b (n p) -> (a b n) p",
                     4: "a b c (n p) -> (a b c n) p", 5: "a b c d (n p) -> (a b c d n) p"}[len(ins[name].shape)], p=P)
                r = 0
                while r < n:
                    tile, row = divmod(PCOL[name] + r, P)
                    k = min(n - r, P - row)
                    pieces_in.append((rows[row:row + k, tile, :], flat[r:r + k, :]))
                    r += k
            with nc.Block() as block:
                @block.sync
                def _(sp):
                    sp.dma_start(const[:], ins["constants"]).then_inc(small_in.sem, 16)
                    for dst, src in pieces_in:
                        sp.dma_start(dst, src).then_inc(small_in.sem, 16)
                    sp_first(sp, first)

                @block.gpsimd
                def _(pool):
                    pool.memset(m0[:], 0.0).then_inc(pool_step.sem, 1)
                    pool.wait_ge(pool_step.sem, 1)
                    pool.dma_start(m0[HEADS:2 * HEADS, :], ins["state_ml_m"][0, 0].rearrange("d h -> h d"),
                                   allow_slow_non_contiguous=True).then_inc(state_in.sem, 16)
                    pool.dma_start(gate_b[:], ins["ml_gate_b"].rearrange("a n -> n a"),
                                   allow_slow_non_contiguous=True).then_inc(state_in.sem, 16)
                    pool.wait_ge(state_in.sem, 32)

                @block.scalar
                def _(act):
                    act.dma_start(tokens[:, 0, :], ins["x_prompt"][0]).then_inc(tokens_in.sem, 16)
                    act.dma_start(tokens[:, 1, :], ins["x_sample"][0]).then_inc(tokens_in.sem, 16)
                    act.dma_start(lam_rows[:], ins["da_lambda"].rearrange("a b c -> a (b c)")
                                  .broadcast_to([P, 4 * SUB])).then_inc(lam_in.sem, 16)
                    act.wait_ge(dve_step.sem, 1)
                    act.activation(cond_f[:], par[:, PCOL["c_ctx"]:PCOL["c_ctx"] + 2 * KD]
                                   .rearrange("p (s k) -> p k s", s=2), ACT.Silu).then_inc(act_step.sem, 1)
                    act.wait_ge(act_step.sem, 1)
                    act.activation(cond_split[:, :, 0:2], cond_f[:], ACT.Copy).then_inc(act_step.sem, 1)
                    act.wait_ge(dve_step.sem, 4)
                    act.activation(lam_sum[:], lam_sum[:], ACT.Exp).then_inc(act_step.sem, 1)
                    for s in range(SPLIT):
                        split_hi(act, first, 0, s)

                @block.vector
                def _(dve):
                    dve.wait_ge(pe_step.sem, 1)
                    for b in range(0, PAR_TILES, 4):
                        k = min(4, PAR_TILES - b) * P
                        k = min(k, NPAR - b * P)
                        cp = dve.tensor_copy(par[:, b * P:b * P + k], banks[:, b // 4, 0:k])
                    cp.then_inc(dve_step.sem, 1)
                    dve.wait_ge(act_step.sem, 2)
                    dve.tensor_tensor(cond_split[:, :, 2:4], cond_f[:], cond_split[:, :, 0:2].bitcast(F32),
                                      ALU.subtract).then_inc(dve_step.sem, 1)
                    dve.wait_ge(lam_in.sem, 16)
                    lr = lam_rows[:].rearrange("p (a b c) -> p a b c", a=2, b=2)
                    dve.tensor_tensor(lam_prod[:].rearrange("p (a c) -> p a c", a=2), lr[:, :, 0], lr[:, :, 1],
                                      ALU.mult).then_inc(dve_step.sem, 1)
                    dve.wait_ge(dve_step.sem, 3)
                    dve.tensor_reduce(lam_sum[:], lam_prod[:].rearrange("p (a c) -> p a c", a=2), X_AXIS,
                                      ALU.add).then_inc(dve_step.sem, 1)
                    for s in range(2):
                        for b in range(4):
                            dve.wait_ge(pe_step.sem, 2 + 4 * s + b)
                            dve.tensor_copy(x[:, 4 * b:4 * b + 4, T * s:T * s + T],
                                            banks[:, 3 + (4 * s + b) % 4, :].rearrange("p (k t) -> p k t", k=4)
                                            ).then_inc(dve_step.sem, 1)
                    dve.wait_ge(act_step.sem, 3)
                    dve.tensor_tensor(lam[:], lam_sum[:, 0:1], lam_sum[:, 1:2], ALU.subtract
                                      ).then_inc(dve_step.sem, 1)
                    dve.wait_ge(dve_step.sem, 13)
                    dve.tensor_scalar(lam[:], lam[:], LAM_INIT, None, ALU.add).then_inc(dve_step.sem, 1)
                    for s in range(SPLIT):
                        split_lo(dve, first, 0, s)

                @block.tensor
                def _(pe):
                    pe.wait_ge(small_in.sem, 16 * (1 + len(pieces_in)))
                    for b in range(PAR_TILES):
                        k = min(P, NPAR - b * P)
                        tr = pe.transpose(banks[:, b // 4, P * (b % 4):P * (b % 4) + k], rows[0:k, b, :],
                                          ident[0:k, 0:k])
                    tr.then_inc(pe_step.sem, 1)
                    pe.wait_ge(tokens_in.sem, 32)
                    for s in range(2):
                        for b in range(4):
                            if s:
                                pe.wait_ge(dve_step.sem, 5 + b)
                            for k in range(4):
                                tr = pe.transpose(banks[:, 3 + (4 * s + b) % 4, P * k:P * k + P],
                                                  tokens[:, s, P * (4 * b + k):P * (4 * b + k) + P], ident)
                            tr.then_inc(pe_step.sem, 1)
            small_in.advance(16 * (1 + len(pieces_in)))
            pool_step.advance(1)
            pe_step.advance(9)
            act_step.advance(3)
            dve_step.advance(14)

        def modulation(l):
            f = ph["mod", l]
            G = 2
            mod_rows = sb(f"mod_rows{l}", [4, G, SLABW], scope=scope)
            out_row, out_col = 0, 2
            bias = par[:, PCOL["b_mod"] + l * 6 * KD:PCOL["b_mod"] + (l + 1) * 6 * KD]
            r_out = rows_out
            turned, m_done = rows_turned, mod_done
            with nc.Block() as block:
                @block.sync
                def _(sp):
                    sp_stream(sp, f)

                @block.scalar
                def _(act):
                    def copy_rows(i, g):
                        n = f.group(i, g)
                        act.wait_ge(slab_used.sem, f.slab(i, 4 * g + 3) + 1)
                        wait(act, turned.sem, n - 1)
                        act.activation(mod_rows[:, g, :], banks[0:4, out_row + g, :], ACT.Copy
                                       ).then_inc(r_out.sem, 1)
                    split_stream(act, f, split_hi, [copy_rows])

                @block.vector
                def _(dve):
                    def add_bias(i, g):
                        n = f.group(i, g)
                        dve.wait_ge(turned.sem, n + 1)
                        first_tile = GROUP * (i * G + g)
                        tiles = (slice(first_tile, first_tile + GROUP) if isinstance(first_tile, int)
                                 else bass.ds(first_tile, GROUP))
                        dve.tensor_tensor(mod[:, l, tiles, :],
                                          banks[:, out_col + g, 0:2 * GROUP].rearrange("p (t s) -> p t s", s=2),
                                          over(bias[:, tiles], 2), ALU.add).then_inc(m_done.sem, 1)
                    split_stream(dve, f, split_lo, [None, None, None, add_bias])
                    dve.wait_ge(m_done.sem, f.group(f.iters - 1, G - 1) + 1)
                    for n, name in enumerate(("norm1_g", "norm2_g")):
                        gain = par[:, PCOL[name] + l * KD:PCOL[name] + (l + 1) * KD]
                        dve.scalar_tensor_tensor(norm_gain[:, l, n], mod[:, l, (3 * n + 1) * KD:(3 * n + 2) * KD, :],
                                                 1.0, over(gain, 2), ALU.add, ALU.mult)

                @block.tensor
                def _(pe):
                    def rows_product(i, s, g):
                        k0 = CHUNKS * (s % 4)
                        for c in range(CHUNKS):
                            for n, half in enumerate((w_hi, w_lo)):
                                mm = pe.matmul(banks[0:4, out_row + g, :], cond_split[:, k0 + c, :],
                                               half[:, s % SPLIT, c, :], start=(k0 + c == 0 and n == 0),
                                               stop=(k0 + c == KD - 1 and n == 1))
                        return mm

                    def stream_product(i, s, g):
                        if s % 4 == 0:
                            wait(pe, r_out.sem, f.group(i, g) - 1)
                        return rows_product(i, s, g)

                    def turn(i, g):
                        n = f.group(i, g)
                        pe.wait_ge(r_out.sem, n + 1)
                        wait(pe, m_done.sem, n - 1)
                        for t in range(GROUP):
                            mm = pe.matmul(banks[:, out_col + g, 2 * t:2 * t + 2], mod_rows[:, g, P * t:P * t + P],
                                           const[0:4, C_SUM:C_SUM + 2], start=True, stop=True)
                        mm.then_inc(turned.sem, 1)

                    def body(i, first, last):
                        for s in range(f.slabs):
                            pe.wait_ge(lo_done.sem, f.slab(i, s) + 1)
                            stream_product(i, s, s // 4).then_inc(slab_used.sem, 1)
                            run_pieces(f, [None, None, turn], i, s, first)
                    rolled(pe, f.iters, body)
                    finish_pieces(f, [None, None, turn])

        with ExitStack() as scope:
            for l in range(DEPTH):
                modulation(l)
        cond.close()
        mod_groups = sum(ph["mod", l].iters * ph["mod", l].groups for l in range(DEPTH))
        for f in ph.values():
            f.group0 -= mod_groups

        def norm_stage(xs, gains, shifts, tag):
            with ExitStack() as scope:
                h = sb(f"h_{tag}", [P, KD, NT], scope=scope)
                r = sb(f"r_{tag}", [P, NT], scope=scope)
                A, V, E = act_step, dve_step, pe_step
                with nc.Block() as block:
                    @block.scalar
                    def _(act):
                        for b in range(4):
                            act.activation(h[:, 4 * b:4 * b + 4], x[:, 4 * b:4 * b + 4], ACT.Square
                                           ).then_inc(A.sem, 1)
                        act.wait_ge(V.sem, V.at(1))
                        act.activation(r[:], r[:], ACT.Sqrt).then_inc(A.sem, 1)
                        for b in range(4):
                            act.wait_ge(V.sem, V.at(7 + b))
                            act.activation(xs[:, 4 * b:4 * b + 4, 0:NT], h[:, 4 * b:4 * b + 4], ACT.Copy
                                           ).then_inc(A.sem, 1)

                    @block.tensor
                    def _(pe):
                        for b in range(4):
                            pe.wait_ge(A.sem, A.at(1 + b))
                            for k in range(4 * b, 4 * b + 4):
                                mm = pe.matmul(banks[:, 0, 0:NT], ones, h[:, k, :], start=k == 0, stop=k == KD - 1)
                        mm.then_inc(E.sem, 1)

                    @block.vector
                    def _(dve):
                        dve.wait_ge(E.sem, E.at(1))
                        dve.tensor_scalar(r[:], banks[:, 0, 0:NT], 1.0 / D, EPS, ALU.mult, ALU.add
                                          ).then_inc(V.sem, 1)
                        dve.wait_ge(A.sem, A.at(5))
                        dve.reciprocal(r[:], r[:]).then_inc(V.sem, 1)
                        dve.wait_ge(V.sem, V.at(2))
                        for b in range(4):
                            dve.tensor_tensor(h[:, 4 * b:4 * b + 4], x[:, 4 * b:4 * b + 4],
                                              r[:].unsqueeze(1).broadcast_to([P, 4, NT]), ALU.mult
                                              ).then_inc(V.sem, 1)
                        for b in range(4):
                            dve.wait_ge(V.sem, V.at(3 + b))
                            for k in range(4 * b, 4 * b + 4):
                                for s in range(2):
                                    part = h[:, k, T * s:T * s + T]
                                    ts = dve.tensor_scalar(part, part, gains[:, k, s:s + 1], shifts[:, k, s:s + 1],
                                                           ALU.mult, ALU.add)
                            ts.then_inc(V.sem, 1)
                        for b in range(4):
                            dve.wait_ge(A.sem, A.at(6 + b))
                            dve.tensor_tensor(xs[:, 4 * b:4 * b + 4, NT:2 * NT], h[:, 4 * b:4 * b + 4],
                                              xs[:, 4 * b:4 * b + 4, 0:NT].bitcast(F32), ALU.subtract)
                A.advance(9)
                V.advance(10)
                E.advance(1)

        def norm_of(l, n, xs):
            norm_stage(xs, norm_gain[:, l, n], mod[:, l, 3 * n * KD:(3 * n + 1) * KD, :], f"{l}{n}")

        def project(phases, operand, act_pieces, dve_pieces, act_also=None, dve_also=None, moving_ready=None,
                    products=None):
            with nc.Block() as block:
                @block.sync
                def _(sp):
                    for f in phases:
                        sp_stream(sp, f)

                @block.scalar
                def _(act):
                    for n, f in enumerate(phases):
                        split_stream(act, f, split_hi, [(lambda i, g, p=p, f=f: p(act, f, i, g)) if p else None
                                                        for p in act_pieces[n]],
                                     also=(lambda i, s, f=f: act_also(act, f, i, s)) if act_also else None)

                @block.vector
                def _(dve):
                    for n, f in enumerate(phases):
                        split_stream(dve, f, split_lo, [(lambda i, g, p=p, f=f: p(dve, f, i, g)) if p else None
                                                        for p in dve_pieces[n]],
                                     also=(lambda i, s, f=f: dve_also(dve, f, i, s)) if dve_also else None)

                @block.tensor
                def _(pe):
                    for n, f in enumerate(phases):
                        own = products and products[n]
                        if own:
                            product_stream(pe, f, lambda i, s, g, f=f, own=own: own(pe, f, i, s, g))
                        else:
                            split_products(pe, f, operand, moving_ready and (
                                lambda i, s, f=f: moving_ready(pe, f, i, s)))

        def group_used(f, i, g):
            return f.slab(i, (g + 1) * f.per_group - 1) + 1

        def copy_part(tb):
            def piece(act, f, i, g):
                act.wait_ge(slab_used.sem, group_used(f, i, g))
                wait(act, summed.sem, f.group(i, g))
                act.activation(tb[:], banks[:, group_banks(g), NT:2 * NT], ACT.Copy).then_inc(part_copied.sem, 1)
            return piece

        def tiles_at(n, k):
            return slice(n, n + k) if isinstance(n, int) else bass.ds(n, k)

        def add_parts(tb, dst, first=0):
            def piece(dve, f, i, g):
                dve.wait_ge(part_copied.sem, f.group(i, g) + 1)
                n = first + GROUP * (i * f.groups + g)
                dve.tensor_tensor(dst[:, tiles_at(n, GROUP), :], banks[:, group_banks(g), 0:NT], tb[:], ALU.add
                                  ).then_inc(summed.sem, 1)
            return piece

        def residual_pieces(tb, gate):
            def act_piece(act, f, i, g):
                act.wait_ge(slab_used.sem, group_used(f, i, g))
                wait(act, resid.sem, f.group(i, g) - resid_skip[0])
                act.activation(tb[:], banks[:, group_banks(g), NT:2 * NT], ACT.Copy).then_inc(part_copied.sem, 1)

            def dve_piece(dve, f, i, g):
                n = f.group(i, g)
                dve.wait_ge(part_copied.sem, n + 1)
                dve.tensor_tensor(tb[:], banks[:, group_banks(g), 0:NT], tb[:], ALU.add).then_inc(summed.sem, 1)
                dve.wait_ge(summed.sem, n + 1)
                tile0 = GROUP * (i * f.groups + g)
                four = tb[:].rearrange("p t (s n) -> p (t s) n", s=2)
                dve.tensor_tensor(four, four, over(gate[:, tiles_at(tile0, GROUP), :].rearrange("p t s -> p (t s)"), T),
                                  ALU.mult).then_inc(gated.sem, 1)
                dve.wait_ge(gated.sem, n - resid_skip[0] + 1)
                xt = x[:, tiles_at(tile0, GROUP), :]
                dve.tensor_tensor(xt, xt, tb[:], ALU.add).then_inc(resid.sem, 1)
            return act_piece, dve_piece

        resid_skip = [0]

        def three_taps(dve, u, y, weight, bias, n):
            for t in range(GROUP):
                ins_ = dve.tensor_scalar(y[:, t], u[:, t], weight(1, t), bias(t), ALU.mult, ALU.add)
            ins_.then_inc(tap[0].sem, 1)
            for which, to, frm in ((0, 1, 0), (2, 0, 1)):
                before, after = (tap[0], tap[1]) if which == 0 else (tap[1], tap[2])
                dve.wait_ge(before.sem, before.at(n + 1))
                for t in range(GROUP):
                    yt = y[:, t].rearrange("p (s n) -> p s n", s=2)[:, :, to:to + T - 1]
                    ut = u[:, t].rearrange("p (s n) -> p s n", s=2)[:, :, frm:frm + T - 1]
                    ins_ = dve.scalar_tensor_tensor(yt, ut, weight(which, t), yt, ALU.mult, ALU.add)
                ins_.then_inc(after.sem, 1)

        def ffn(l):
            up, down = ph["up", l], ph["down", l]
            with ExitStack() as scope:
                acts = sb(f"acts{l}", [P, KF, NT], scope=scope)
                xs = sb(f"xs_ffn{l}", [P, KD, 2 * NT], F32R, scope)
                norm_of(l, 1, xs)
                tb = sb(f"tb{l}", [P, GROUP, NT], scope=scope)
                u = sb(f"u{l}", [P, GROUP, NT], scope=scope)
                y = sb(f"y{l}", [P, GROUP, NT], scope=scope)
                gate = sb(f"gate{l}", [P, GROUP, NT], scope=scope)
                conv_col = PCOL["ffn_conv_w"] + l * 3 * 2 * KF
                bias_col = PCOL["ffn_conv_b"] + l * 2 * KF
                g_up0 = up.group0

                def count(f, i, g):
                    return f.group(i, g) - g_up0

                def conv(dve, f, i, g):
                    n = count(f, i, g)
                    dve.wait_ge(part_copied.sem, f.group(i, g) + 1)
                    if g == 0:
                        wait(dve, act_done.sem, act_done.at(i))
                    else:
                        dve.wait_ge(silu_done.sem, silu_done.at(i + 1))
                    dve.tensor_tensor(u[:], banks[:, group_banks(g), 0:NT], tb[:], ALU.add).then_inc(summed.sem, 1)
                    dve.wait_ge(summed.sem, f.group(i, g) + 1)

                    def col(base, t):
                        return par[:, tiles_at(base + g * KF + t + GROUP * i, 1)]

                    three_taps(dve, u, y, lambda which, t: col(conv_col + which * 2 * KF, t),
                               lambda t: col(bias_col, t), n)

                def silu(act, f, i, g):
                    if g == 0:
                        act.wait_ge(tap[2].sem, tap[2].at(count(f, i, g) + 1))
                        wait(act, act_done.sem, act_done.at(i))
                        act.activation(gate[:], y[:], ACT.Silu).then_inc(silu_done.sem, 1)

                def multiply(dve, f, i, g):
                    if g == 1:
                        dve.wait_ge(tap[2].sem, tap[2].at(count(f, i, g) + 1))
                        dve.tensor_tensor(acts[:, tiles_at(GROUP * i, GROUP), :], gate[:], y[:], ALU.mult
                                          ).then_inc(act_done.sem, 1)

                project([up], lambda s, k: xs[:, CHUNKS * k:CHUNKS * k + CHUNKS],
                        [[copy_part(tb), silu]], [[conv, multiply]])
                groups = up.iters * up.groups
                for t in tap:
                    t.advance(groups)
                for t in (silu_done, act_done):
                    t.advance(up.iters)
                resid_skip[0] += groups

                def chunk0(s):
                    return CHUNKS * (s % down.per_group)

                def slot_of(s):
                    return slice(CHUNKS * (s % SPLIT), CHUNKS * (s % SPLIT) + CHUNKS)

                def moving_hi(act, f, i, s):
                    act.activation(xs[:, slot_of(s), 0:NT], acts[:, chunk0(s):chunk0(s) + CHUNKS], ACT.Copy
                                   ).then_inc(mov_hi.sem, 1)

                def moving_lo(dve, f, i, s):
                    dve.wait_ge(mov_hi.sem, mov_hi.at(i * f.slabs + s + 1))
                    dve.tensor_tensor(xs[:, slot_of(s), NT:2 * NT], acts[:, chunk0(s):chunk0(s) + CHUNKS],
                                      xs[:, slot_of(s), 0:NT].bitcast(F32), ALU.subtract).then_inc(mov_lo.sem, 1)

                act_piece, dve_piece = residual_pieces(tb, mod[:, l, 5 * KD:6 * KD, :])
                with nc.Block() as block:
                    @block.scalar
                    def _(act):
                        for s in range(SPLIT):
                            moving_hi(act, down, 0, s)

                    @block.vector
                    def _(dve):
                        for s in range(SPLIT):
                            moving_lo(dve, down, 0, s)
                project([down], lambda s, k: xs[:, slot_of(s)], [[act_piece]], [[dve_piece]],
                        act_also=moving_hi, dve_also=moving_lo,
                        moving_ready=lambda pe, f, i, s: pe.wait_ge(mov_lo.sem, mov_lo.at(i * f.slabs + s + 1)))
                mov_hi.advance(down.iters * down.slabs)
                mov_lo.advance(down.iters * down.slabs)

        def out_projection(l, mix):
            f = ph["out", l]
            with ExitStack() as scope:
                xs = sb(f"xs_out{l}", [P, KD, 2 * NT], F32R, scope)
                tb = sb(f"tb_out{l}", [P, GROUP, NT], scope=scope)
                A = act_step
                with nc.Block() as block:
                    @block.scalar
                    def _(act):
                        for b in range(4):
                            act.activation(xs[:, 4 * b:4 * b + 4, 0:NT], mix[:, 4 * b:4 * b + 4], ACT.Copy
                                           ).then_inc(A.sem, 1)

                    @block.vector
                    def _(dve):
                        for b in range(4):
                            dve.wait_ge(A.sem, A.at(1 + b))
                            dve.tensor_tensor(xs[:, 4 * b:4 * b + 4, NT:2 * NT], mix[:, 4 * b:4 * b + 4],
                                              xs[:, 4 * b:4 * b + 4, 0:NT].bitcast(F32), ALU.subtract)
                A.advance(4)
                act_piece, dve_piece = residual_pieces(tb, mod[:, l, 2 * KD:3 * KD, :])
                project([f], lambda s, k: xs[:, CHUNKS * k:CHUNKS * k + CHUNKS], [[act_piece]], [[dve_piece]])

        A, V, E = act_step, dve_step, pe_step

        def feature_rms(src, work, gains, together=False):
            n = src.shape[1]
            count = 1 if together else n
            flat = work.rearrange("p n t -> p (n t)")
            sq, r = flat[:, 0:n * NT], flat[:, 0:count * NT]
            with nc.Block() as block:
                @block.scalar
                def _(act):
                    act.activation(sq.rearrange("p (n t) -> p n t", n=n), src, ACT.Square).then_inc(A.sem, 1)
                    act.wait_ge(V.sem, V.at(1))
                    act.activation(r, r, ACT.Sqrt).then_inc(A.sem, 1)

                @block.tensor
                def _(pe):
                    pe.wait_ge(A.sem, A.at(1))
                    if together:
                        for k in range(n):
                            mm = pe.matmul(banks[:, 0, 0:NT], ones, sq[:, k * NT:k * NT + NT],
                                           start=k == 0, stop=k == n - 1)
                    else:
                        for b in range(0, n, 2):
                            mm = pe.matmul(banks[:, b // 2, :], ones, sq[:, b * NT:(b + 2) * NT], start=True, stop=True)
                    mm.then_inc(E.sem, 1)

                @block.vector
                def _(dve):
                    dve.wait_ge(E.sem, E.at(1))
                    sums = banks[:].rearrange("p b n -> p (b n)")[:, 0:count * NT]
                    dve.tensor_scalar(r, sums, 1.0 / (P * n if together else P), EPS, ALU.mult, ALU.add
                                      ).then_inc(V.sem, 1)
                    dve.wait_ge(A.sem, A.at(2))
                    dve.reciprocal(r, r).then_inc(V.sem, 1)
                    dve.wait_ge(V.sem, V.at(2))
                    scale = (r.unsqueeze(1).broadcast_to([P, n, NT]) if together
                             else r.rearrange("p (n t) -> p n t", n=n))
                    dve.tensor_tensor(src, src, scale, ALU.mult).then_inc(V.sem, 1)
                    dve.wait_ge(V.sem, V.at(3))
                    for tiles, gain, factor in gains:
                        dve.tensor_scalar(src[:, tiles], src[:, tiles], gain, factor, ALU.mult, ALU.mult)
            A.advance(2)
            V.advance(3)
            E.advance(1)

        def rotate(src, rot_col, cos_col, sin_col, work):
            R, n = src.shape[0:2]
            tmp = work.rearrange("p n t -> p (n t)")[0:R, 0:n * T].rearrange("p (n t) -> p n t", n=n)
            with nc.Block() as block:
                @block.tensor
                def _(pe):
                    for b in range(0, n, 4):
                        k = min(4, n - b)
                        mm = pe.matmul(banks[0:R, b // 4, 0:k * T], const[0:R, rot_col:rot_col + R], src[:, b:b + k, :],
                                       start=True, stop=True)
                    mm.then_inc(E.sem, 1)

                @block.vector
                def _(dve):
                    def table(c):
                        return const[0:R, c:c + T].unsqueeze(1).broadcast_to([R, n, T])
                    dve.wait_ge(E.sem, E.at(1))
                    turned = banks[0:R].rearrange("p b n -> p (b n)")[:, 0:n * T].rearrange("p (n t) -> p n t", n=n)
                    dve.tensor_tensor(tmp, turned, table(sin_col), ALU.mult)
                    dve.tensor_tensor(src, src, table(cos_col), ALU.mult).then_inc(V.sem, 1)
                    dve.wait_ge(V.sem, V.at(1))
                    dve.tensor_tensor(src, src, tmp, ALU.add)
            V.advance(1)
            E.advance(1)

        def turn_tiles(srcs, dst):
            with nc.Block() as block:
                batches = [srcs[b:b + 4] for b in range(0, len(srcs), 4)]

                @block.tensor
                def _(pe):
                    for b, batch in enumerate(batches):
                        wait(pe, A.sem, A.at(b - 7) if b >= 8 else 0)
                        for j, s in enumerate(batch):
                            rows, cols = s.shape
                            tr = pe.transpose(banks[0:cols, b % 8, P * j:P * j + rows], s, ident[0:rows, 0:rows])
                        tr.then_inc(E.sem, 1)

                @block.scalar
                def _(act):
                    for b, batch in enumerate(batches):
                        act.wait_ge(E.sem, E.at(b + 1))
                        cols, rows = batch[0].shape[1], batch[0].shape[0]
                        act.activation(dst[0:cols, 4 * b:4 * b + len(batch), 0:rows],
                                       banks[0:cols, b % 8, 0:P * len(batch)].rearrange("p (n r) -> p n r", r=P)[:, :, 0:rows],
                                       ACT.Copy).then_inc(A.sem, 1)
            A.advance(len(batches))
            E.advance(len(batches))

        scores_in = tally("scores_in")
        scores_out = tally("scores_out")
        row_max = tally("row_max")
        exped = tally("exped")
        row_sum = tally("row_sum")
        row_inv = tally("row_inv")
        inv_signed = tally("inv_signed")
        scaled = tally("scaled")
        weights_in = tally("weights_in")
        w_turned = tally("w_turned")
        w_copied = tally("w_copied")
        mixed = tally("mixed")
        mixed_out = tally("mixed_out")

        def attention(blocks, tag):
            with ExitStack() as scope:
                e = sb(f"e_{tag}", [P, 2, 2048], scope=scope)
                wt = sb(f"wt_{tag}", [P, 2, 8, P], scope=scope)
                mx = sb(f"mx_{tag}", [P, 2, 16], scope=scope)
                inv = sb(f"inv_{tag}", [P, 2, 16], scope=scope)
                scores = banks[:, 0:4].rearrange("p b n -> p (b n)")
                rounds, at = [], 0
                for b, k in enumerate(blocks):
                    heads = k["rows"] // (2 if k["diff"] else 1)
                    chunks = k["keys"] // T
                    per = 8 // chunks
                    rounds.append([(at + j, per * j, per, chunks) for j in range(heads // per)])
                    at += heads // per

                def rows_of(buf, k):
                    return buf[:, 0:k["rows"] * k["keys"]].rearrange("p (r l) -> p r l", r=k["rows"])

                with nc.Block() as block:
                    @block.tensor
                    def _(pe):
                        def score(b):
                            k = blocks[b]
                            wait(pe, scores_out.sem, scores_out.at(b) if b else 0)
                            out = rows_of(scores, k)
                            for row in range(k["rows"]):
                                mm = k["score"](pe, row, out[:, row])
                            mm.then_inc(scores_in.sem, 1)

                        def mix_values(b):
                            k = blocks[b]
                            w = rows_of(e[:, b % 2], k)
                            pe.wait_ge(weights_in.sem, weights_in.at(b + 1))
                            for n, h0, per, chunks in rounds[b]:
                                wait(pe, w_copied.sem, w_copied.at(n) if n else 0)
                                for j in range(per):
                                    for c in range(chunks):
                                        m = j * chunks + c
                                        tr = pe.transpose(banks[:, 4 + m // 4, P * (m % 4):P * (m % 4) + P],
                                                          w[:, h0 + j, T * c:T * c + T], ident)
                                tr.then_inc(w_turned.sem, 1)
                                pe.wait_ge(w_copied.sem, w_copied.at(n + 1))
                                wait(pe, mixed_out.sem, mixed_out.at(n) if n else 0)
                                for j in range(per):
                                    for c in range(chunks):
                                        mm = pe.matmul(banks[:, 6 + j // 4, P * (j % 4):P * (j % 4) + P],
                                                       k["value"](h0 + j, c), wt[:, n % 2, j * chunks + c],
                                                       start=c == 0, stop=c == chunks - 1)
                                mm.then_inc(mixed.sem, 1)
                        score(0)
                        for b in range(len(blocks)):
                            if b + 1 < len(blocks):
                                score(b + 1)
                            mix_values(b)

                    @block.vector
                    def _(dve):
                        def prepare(b):
                            k = blocks[b]
                            s, w = rows_of(scores, k), rows_of(e[:, b % 2], k)
                            dve.wait_ge(scores_in.sem, scores_in.at(b + 1))
                            top = mx[:, b % 2, 0:k["rows"]]
                            dve.tensor_reduce(top, s, X_AXIS, ALU.max).then_inc(row_max.sem, 1)
                            dve.wait_ge(row_max.sem, row_max.at(b + 1))
                            if b >= 2:
                                dve.wait_ge(w_turned.sem, w_turned.at(rounds[b - 2][-1][0] + 1))
                            dve.tensor_tensor(w, s, over(top, k["keys"]), ALU.subtract).then_inc(scores_out.sem, 1)

                        def normalise(b):
                            k = blocks[b]
                            w = rows_of(e[:, b % 2], k)
                            r = inv[:, b % 2, 0:k["rows"]]
                            dve.wait_ge(exped.sem, exped.at(b + 1))
                            dve.tensor_reduce(r, w, X_AXIS, ALU.add).then_inc(row_sum.sem, 1)
                            dve.wait_ge(row_sum.sem, row_sum.at(b + 1))
                            dve.reciprocal(r, r).then_inc(row_inv.sem, 1)
                            dve.wait_ge(row_inv.sem, row_inv.at(b + 1))
                            if k["diff"]:
                                second = r[:, k["rows"] // 2:]
                                dve.tensor_scalar(second, second, lam[:], -1.0, ALU.mult, ALU.mult
                                                  ).then_inc(inv_signed.sem, 1)
                                dve.wait_ge(inv_signed.sem, inv_signed.at(b + 1))
                                dve.tensor_tensor(w, w, over(r, k["keys"]), ALU.mult).then_inc(scaled.sem, 1)
                                dve.wait_ge(scaled.sem, scaled.at(b + 1))
                                w1, w2 = w[:, 0:k["rows"] // 2], w[:, k["rows"] // 2:]
                                dve.tensor_tensor(w1, w1, w2, ALU.add).then_inc(weights_in.sem, 1)
                            else:
                                dve.tensor_tensor(w, w, over(r, k["keys"]), ALU.mult).then_inc(weights_in.sem, 1)
                        prepare(0)
                        for b in range(len(blocks)):
                            if b + 1 < len(blocks):
                                prepare(b + 1)
                            normalise(b)

                    @block.scalar
                    def _(act):
                        def exponentials(b):
                            k = blocks[b]
                            w = rows_of(e[:, b % 2], k)
                            act.wait_ge(scores_out.sem, scores_out.at(b + 1))
                            act.activation(w, w, ACT.Exp, scale=k["scale"]).then_inc(exped.sem, 1)

                        def carry(b):
                            for n, h0, per, chunks in rounds[b]:
                                act.wait_ge(w_turned.sem, w_turned.at(n + 1))
                                if n >= 2:
                                    act.wait_ge(mixed.sem, mixed.at(n - 1))
                                act.activation(wt[:, n % 2], banks[:, 4:6].rearrange("p b (n t) -> p (b n) t", t=P),
                                               ACT.Copy).then_inc(w_copied.sem, 1)
                                act.wait_ge(mixed.sem, mixed.at(n + 1))
                                out = banks[:, 6:8].rearrange("p b (n t) -> p (b n) t", t=P)
                                act.activation(blocks[b]["dst"](h0, per), out[:, 0:per], ACT.Copy
                                               ).then_inc(mixed_out.sem, 1)
                        exponentials(0)
                        for b in range(len(blocks)):
                            if b + 1 < len(blocks):
                                exponentials(b + 1)
                            carry(b)
                diffs = sum(k["diff"] for k in blocks)
                assert all(k["diff"] for k in blocks[:diffs])
                for t in (scores_in, scores_out, row_max, exped, row_sum, row_inv, weights_in):
                    t.advance(len(blocks))
                for t in (inv_signed, scaled):
                    t.advance(diffs)
                for t in (w_turned, w_copied, mixed, mixed_out):
                    t.advance(at)

        def even_layer(l):
            with ExitStack() as outer:
                mix = sb("mix0", [P, 2 * HEADS, NT], scope=outer)
                with ExitStack() as scope:
                    qkv = sb("qkv", [P, EVEN_TILES, NT], scope=scope)
                    with ExitStack() as inner:
                        xs = sb("xs_even", [P, KD, 2 * NT], F32R, inner)
                        norm_of(l, 0, xs)
                        tb = sb("tb_even", [P, GROUP, NT], scope=inner)
                        a, b = ph["even_in"], ph["even_in_end"]
                        project([a, b], lambda s, k: xs[:, CHUNKS * k:CHUNKS * k + CHUNKS],
                                [[copy_part(tb)], [copy_part(tb)]],
                                [[add_parts(tb, qkv)], [add_parts(tb, qkv, GROUP * a.iters * a.groups)]])
                        resid_skip[0] += EVEN_TILES // GROUP
                    QA, KA, VA, QB, KB, VB = 0, 8, 16, 24, 32, 34
                    kv_cache = sb("kv_cache", [P, 2, 10, P], scope=scope)
                    turned = sb("turned0", [P, 40, P], scope=scope)
                    with nc.Block() as block:
                        @block.sync
                        def _(sp):
                            for c in range(2):
                                sp.dma_start(kv_cache[:, 0, 0:HEADS].rearrange("t h (c d) -> t h c d", c=2)[:, :, c],
                                             ins["cache_da_k"][0, 0, :, c].rearrange("h t d -> t h d")
                                             ).then_inc(small_in.sem, 16)
                            sp.dma_start(kv_cache[:, 1, 0:HEADS], ins["cache_da_v"][0, 0].rearrange("h t d -> t h d")
                                         ).then_inc(small_in.sem, 16)
                            for n, name in enumerate(("cache_gq_k", "cache_gq_v")):
                                sp.dma_start(kv_cache[:, n, HEADS:10], ins[name][0, 0].rearrange("h t d -> t h d")
                                             ).then_inc(small_in.sem, 16)
                            sp.wait_ge(small_in.sem, small_in.at(80))
                    small_in.advance(80)
                    with ExitStack() as inner:
                        work = sb("work0", [P, 10, NT], scope=inner)
                        feature_rms(qkv[:, QB:KB + KV_HEADS], work,
                                    [(slice(0, HEADS), par[:, PCOL["gq_q_norm_g"]:PCOL["gq_q_norm_g"] + 1], 1.0),
                                     (slice(HEADS, HEADS + KV_HEADS),
                                      par[:, PCOL["gq_k_norm_g"]:PCOL["gq_k_norm_g"] + 1], 1.0)])
                        rotate(qkv[:, 0:2 * HEADS, T:NT], C_ROT_SUB, C_COS_SUB, C_SIN_SUB, work)
                        rotate(qkv[:, QB:KB + KV_HEADS, T:NT], C_ROT_HD, C_COS_HD, C_SIN_HD, work)
                    prompt = [qkv[:, t, 0:T] for t in (*range(KA, KA + 8), *range(VA, VA + 8), 32, 33, 34, 35)]
                    sample = [qkv[:, t, T:NT] for t in (*range(VA, VA + 8), 34, 35)]
                    turn_tiles(prompt + sample + [kv_cache[:, 0, h] for h in range(10)], turned)
                    KA_P, VA_P, KB_P, VB_P, VA_S, VB_S, K_CACHE = 0, 8, 16, 18, 20, 28, 30
                    with nc.Block() as block:
                        @block.sync
                        def _(sp):
                            for c in range(2):
                                sp.dma_start(outs["new_da_k"][0, 0, :, c].rearrange("h t d -> t h d"),
                                             turned[:, KA_P:KA_P + 8].rearrange("t h (c d) -> t h c d", c=2)[:, :, c]
                                             ).then_inc(stored.sem, 16)
                            for name, t0, n in (("new_da_v", VA_P, 8), ("new_gq_k", KB_P, 2), ("new_gq_v", VB_P, 2)):
                                sp.dma_start(outs[name][0, 0].rearrange("h t d -> t h d"), turned[:, t0:t0 + n]
                                             ).then_inc(stored.sem, 16)
                    stored.advance(80)

                    def sub(c):
                        return slice(SUB * c, SUB * c + SUB)

                    def da_prompt(pe, row, out):
                        c, h = divmod(row, HEADS)
                        return pe.matmul(out, qkv[sub(c), QA + h, 0:T], qkv[sub(c), KA + h, 0:T], start=True, stop=True)

                    def da_sample(h0):
                        def score(pe, row, out):
                            c, h = row // 4, h0 + row % 4
                            q = qkv[sub(c), QA + h, T:NT]
                            pe.matmul(out[:, 0:T], q, turned[sub(c), K_CACHE + h], start=True, stop=True)
                            return pe.matmul(out[:, T:2 * T], q, qkv[sub(c), KA + h, T:NT], start=True, stop=True)
                        return score

                    def gq_prompt(pe, row, out):
                        return pe.matmul(out, qkv[:, QB + row, 0:T], qkv[:, KB + row // 4, 0:T], start=True, stop=True)

                    def gq_sample(pe, row, out):
                        g = row // 4
                        pe.matmul(out[:, 0:T], qkv[:, QB + row, T:NT], turned[:, K_CACHE + 8 + g], start=True, stop=True)
                        return pe.matmul(out[:, T:2 * T], qkv[:, QB + row, T:NT], qkv[:, KB + g, T:NT],
                                         start=True, stop=True)

                    def dst(first, stream):
                        return lambda h0, n: mix[:, first + h0:first + h0 + n, T * stream:T * stream + T]

                    def cached(v_cache, v_own, share=1):
                        return lambda h, c: kv_cache[:, 1, v_cache + h // share] if c == 0 else turned[:, v_own + h // share]

                    da = dict(diff=True, scale=SUB ** -0.5)
                    gq = dict(diff=False, scale=P ** -0.5)
                    attention([
                        dict(da, rows=16, keys=T, score=da_prompt, dst=dst(0, 0), value=lambda h, c: turned[:, VA_P + h]),
                        dict(da, rows=8, keys=2 * T, score=da_sample(0), dst=dst(0, 1), value=cached(0, VA_S)),
                        dict(da, rows=8, keys=2 * T, score=da_sample(4), dst=dst(4, 1), value=lambda h, c: cached(4, VA_S + 4)(h, c)),
                        dict(gq, rows=8, keys=T, score=gq_prompt, dst=dst(8, 0), value=lambda h, c: turned[:, VB_P + h // 4]),
                        dict(gq, rows=8, keys=2 * T, score=gq_sample, dst=dst(8, 1), value=cached(8, VB_S, 4)),
                    ], "even")
                    with ExitStack() as inner:
                        work = sb("work1", [P, HEADS, NT], scope=inner)
                        feature_rms(mix[:, 0:HEADS], work,
                                    [(slice(0, HEADS), par[:, PCOL["da_subln_g"]:PCOL["da_subln_g"] + 1], 1.0 - LAM_INIT)])
                out_projection(l, mix)
            ffn(l)

        VM, OM, QD, KV, PE_T = 0, 8, 16, 20, 22

        def mlstm(kq, prj, gates, mix):
            R = 2 * HEADS
            NEG_M, Z, A_, EM, WG = range(5)
            with ExitStack() as scope:
                ee = sb("ee", [P, 4 * HEADS, T], scope=scope)
                va = sb("va", [P, R, P + 1], scope=scope)
                c0 = sb("c0", [P, R, P + 1], scope=scope)
                k_tok = sb("k_tok", [P, HEADS, P], scope=scope)
                qa = sb("qa", [P, R, T], scope=scope)
                sc = sb("sc", [R, 5, 2, T], scope=scope)
                turned = sb("sc_turned", [P, 4, R], scope=scope)
                den = sb("den", [P, 2, HEADS], scope=scope)
                state_n = sb("state_n", [R, 1, P], scope=scope)
                hbuf = mix[:, HEADS:2 * HEADS].rearrange("p a (b t) -> p (a b) t", t=T)

                def ordered(kind, d):
                    return sc[:, kind, d, :] if d == 0 else sc[:, kind, d, ::-1]

                with ExitStack() as inner:
                    gs = sb("gs", [R, 4, T], scope=inner)
                    ex = sb("ex", [R, 2, T], scope=inner)
                    lf = sb("lf", [R, 2, T], scope=inner)
                    bs = sb("bs", [R, 2, T], scope=inner)
                    zz = sb("zz", [R, 2, T], scope=inner)
                    mm_ = sb("mm", [R, 2, T], scope=inner)
                    ms = sb("ms", [R, 2, T], scope=inner)
                    zero = sb("zero", [R, T], scope=inner)
                    n_end = sb("n_end", [R, 2], scope=inner)
                    f_rows = gs[:].rearrange("r (d k) t -> r d k t", k=2)[:, :, 1]
                    i_rows = gs[:].rearrange("r (d k) t -> r d k t", k=2)[:, :, 0]
                    with nc.Block() as block:
                        @block.sync
                        def _(sp):
                            for d in range(2):
                                sp.dma_start(c0[:, HEADS * d:HEADS * d + HEADS, 0:P],
                                             ins["state_ml_C"][0, 0, d].rearrange("h k v -> k h v")
                                             ).then_inc(small_in.sem, 16)
                            sp.wait_ge(V.sem, V.at(9))
                            sp.dma_start(outs["new_ml_m"][0, 0].rearrange("d h -> h d"), ms[0:HEADS, :, T - 1],
                                         allow_slow_non_contiguous=True).then_inc(stored.sem, 16)
                            sp.wait_ge(stored.sem, stored.at(16))

                        @block.gpsimd
                        def _(pool):
                            pool.memset(zero[:], 0.0).then_inc(pool_step.sem, 1)
                            pool.memset(va[:, :, P:P + 1], 1.0)

                        @block.vector
                        def _(dve):
                            dve.tensor_scalar(gates[:], gates[:], gate_b[:], None, ALU.add).then_inc(V.sem, 1)
                            dve.tensor_scalar(kq[:, 0:HEADS], kq[:, 0:HEADS], P ** -0.5, None, ALU.mult)
                            dve.tensor_copy(c0[:, :, P:P + 1],
                                            par[:, PCOL["state_ml_n"]:PCOL["state_ml_n"] + R].unsqueeze(2))
                            dve.wait_ge(E.sem, E.at(1))
                            dve.tensor_copy(gs[:], banks[0:R, 0, :].rearrange("r (k t) -> r k t", k=4)
                                            ).then_inc(V.sem, 1)
                            dve.wait_ge(V.sem, V.at(2))
                            dve.scalar_tensor_tensor(ex[:], f_rows, -1.0, f_rows, ALU.mult, ALU.min
                                                     ).then_inc(V.sem, 1)
                            dve.tensor_scalar(lf[:], f_rows, 0.0, None, ALU.min).then_inc(V.sem, 1)
                            dve.wait_ge(A.sem, A.at(2))
                            dve.wait_ge(V.sem, V.at(4))
                            dve.tensor_tensor(lf[:], lf[:], ex[:], ALU.subtract).then_inc(V.sem, 1)
                            dve.wait_ge(V.sem, V.at(5))
                            dve.wait_ge(pool_step.sem, pool_step.at(1))
                            for d in range(2):
                                sn = dve.tensor_tensor_scan(bs[:, d], lf[:, d], zero[:], 0.0, ALU.add, ALU.add)
                            sn.then_inc(V.sem, 1)
                            dve.wait_ge(V.sem, V.at(6))
                            dve.tensor_tensor(zz[:], i_rows, bs[:], ALU.subtract).then_inc(V.sem, 1)
                            dve.wait_ge(V.sem, V.at(7))
                            for d in range(2):
                                sn = dve.tensor_tensor_scan(mm_[:, d], zz[:, d], zz[:, d], m0[:, d:d + 1],
                                                            ALU.max, ALU.max)
                            sn.then_inc(V.sem, 1)
                            dve.wait_ge(V.sem, V.at(8))
                            dve.tensor_tensor(ms[:], bs[:], mm_[:], ALU.add).then_inc(V.sem, 1)
                            dve.tensor_scalar(n_end[:].unsqueeze(2), mm_[:, :, T - 1:T], -1.0, None, ALU.mult
                                              ).then_inc(V.sem, 1)
                            for d in range(2):
                                dve.tensor_scalar(ordered(NEG_M, d), mm_[:, d], -1.0, None, ALU.mult)
                                dve.tensor_copy(ordered(Z, d), zz[:, d])

                        @block.scalar
                        def _(act):
                            act.wait_ge(V.sem, V.at(3))
                            act.activation(ex[:], ex[:], ACT.Exp).then_inc(A.sem, 1)
                            act.wait_ge(A.sem, A.at(1))
                            act.activation(ex[:], ex[:], ACT.Ln, bias=1.0).then_inc(A.sem, 1)
                            act.wait_ge(V.sem, V.at(10))
                            for d in range(2):
                                act.activation(ordered(A_, d), mm_[:, d], ACT.Exp, bias=m0[:, d:d + 1], scale=-1.0)
                                act.activation(ordered(EM, d), ms[:, d], ACT.Exp, scale=-1.0)
                                act.activation(ordered(WG, d), zz[:, d], ACT.Exp, bias=n_end[:, d:d + 1])

                        @block.tensor
                        def _(pe):
                            pe.wait_ge(V.sem, V.at(1))
                            for d in range(2):
                                for kind in range(2):
                                    for s in range(2):
                                        tok = gates[:, T * s:T * s + T]
                                        col = C_SEL + 16 * (4 * d + 2 * kind + s)
                                        mm = pe.matmul(banks[0:R, 0, T * (2 * d + kind):T * (2 * d + kind) + T],
                                                       const[0:4 * HEADS, col:col + R], tok if d == 0 else tok[:, ::-1],
                                                       start=s == 0, stop=s == 1)
                            mm.then_inc(E.sem, 1)
                    V.advance(10)
                    A.advance(2)
                    E.advance(1)
                    pool_step.advance(1)
                    stored.advance(16)
                turn_tiles([prj[:, VM + h, T * s:T * s + T] for s in range(2) for h in range(HEADS)], va[:])
                turn_tiles([kq[:, HEADS + h, 0:T] for h in range(HEADS)], k_tok[:])
                turn_tiles([sc[:, kind, d, :] for kind in (EM, WG) for d in range(2)], turned[:])

                def row(n):
                    return const[0:R, C_IDENT + n:C_IDENT + n + 1].broadcast_to([R, P])
                with nc.Block() as block:
                    @block.sync
                    def _(sp):
                        sp.wait_ge(small_in.sem, small_in.at(32))

                    @block.tensor
                    def _(pe):
                        for j in range(8):
                            d = j // 4
                            pe.matmul(banks[:, j, :], ident, const[:, C_MASK + T * d:C_MASK + T * d + T]
                                      .unsqueeze(1).broadcast_to([P, 4, T]), start=True, stop=False)
                            for m in range(4):
                                n = (4 * j + m) % R
                                out = banks[:, j, T * m:T * m + T]
                                pe.matmul(out, row(n), sc[:, NEG_M, d, :], start=False, stop=False)
                                mm = pe.matmul(out, sc[:, Z, d, :], row(n), start=False, stop=m == 3)
                            mm.then_inc(E.sem, 1)
                        for b in range(4):
                            pe.wait_ge(A.sem, A.at(b + 1))
                            for m in range(4):
                                s, h = divmod(4 * b + m, HEADS)
                                mm = pe.matmul(banks[:, b, T * m:T * m + T], kq[:, HEADS + h, T * s:T * s + T],
                                               kq[:, h, T * s:T * s + T], start=True, stop=True)
                        mm.then_inc(E.sem, 1)
                        for b in range(4):
                            pe.wait_ge(A.sem, A.at(b + 5))
                            for m in range(4):
                                d, h = divmod(4 * b + m, HEADS)
                                mm = pe.matmul(banks[:, 4 + b, T * m:T * m + T], row(HEADS + h), sc[:, A_, d, :],
                                               start=True, stop=True)
                        mm.then_inc(E.sem, 1)

                    @block.scalar
                    def _(act):
                        for j in range(8):
                            act.wait_ge(E.sem, E.at(1 + j))
                            act.activation(ee[:, 4 * j:4 * j + 4], banks[:, j, :].rearrange("p (m t) -> p m t", m=4),
                                           ACT.Exp).then_inc(A.sem, 1)

                    @block.vector
                    def _(dve):
                        dve.wait_ge(E.sem, E.at(9))
                        dve.wait_ge(A.sem, A.at(8))
                        for d in range(2):
                            part = ee[:, R * d:R * d + R]
                            dve.tensor_tensor(part, banks[:, 0:4].rearrange("p b (m t) -> p (b m) t", t=T), part, ALU.mult)
                        dve.wait_ge(E.sem, E.at(10))
                        for d in range(2):
                            dve.tensor_tensor(qa[:, HEADS * d:HEADS * d + HEADS],
                                              banks[:, 4 + 2 * d:6 + 2 * d].rearrange("p b (m t) -> p (b m) t", t=T),
                                              kq[:, 0:HEADS, T:NT], ALU.mult)
                small_in.advance(32)
                E.advance(10)
                A.advance(8)

                def pair_banks(n):
                    return banks[:, 4 * (n % 2):4 * (n % 2) + 4].rearrange("p b (j w) -> p (b j) w", j=2)
                with nc.Block() as block:
                    @block.tensor
                    def _(pe):
                        for n in range(4):
                            d, s = divmod(n, 2)
                            wait(pe, V.sem, V.at(3 * (n - 2) + 3) if n >= 2 else 0)
                            for h in range(HEADS):
                                out = pair_banks(n)[:, h, 0:P + 1]
                                mm = pe.matmul(out, ee[:, R * d + HEADS * s + h], va[:, HEADS * s + h],
                                               start=True, stop=s == 0)
                                if s == 1:
                                    mm = pe.matmul(out, qa[:, HEADS * d + h], c0[:, HEADS * d + h],
                                                   start=False, stop=True)
                            mm.then_inc(E.sem, 1)

                    @block.scalar
                    def _(act):
                        for n in range(4):
                            act.wait_ge(E.sem, E.at(n + 1))
                            if n >= 2:
                                act.wait_ge(V.sem, V.at(3 * (n - 2) + 3))
                            act.activation(den[:, n % 2].unsqueeze(2), pair_banks(n)[:, :, P:P + 1], ACT.Abs
                                           ).then_inc(A.sem, 1)

                    @block.vector
                    def _(dve):
                        for n in range(4):
                            d, s = divmod(n, 2)
                            dn = den[:, n % 2]
                            dve.wait_ge(A.sem, A.at(n + 1))
                            dve.tensor_tensor(dn, dn, turned[:, d, HEADS * s:HEADS * s + HEADS], ALU.max
                                              ).then_inc(V.sem, 1)
                            dve.wait_ge(V.sem, V.at(3 * n + 1))
                            dve.reciprocal(dn, dn).then_inc(V.sem, 1)
                            dve.wait_ge(V.sem, V.at(3 * n + 2))
                            hs = hbuf[:, HEADS * s:HEADS * s + HEADS]
                            dst = hs if d == 0 else ee[:, HEADS * s:HEADS * s + HEADS]
                            dve.tensor_tensor(dst, pair_banks(n)[:, :, 0:P], over(dn, P), ALU.mult
                                              ).then_inc(V.sem, 1)
                        for s in range(2):
                            dve.wait_ge(V.sem, V.at(9 + 3 * s))
                            hs = hbuf[:, HEADS * s:HEADS * s + HEADS]
                            dve.tensor_tensor(hs, hs, ee[:, HEADS * s:HEADS * s + HEADS], ALU.add)
                V.advance(12)
                A.advance(4)
                E.advance(4)

                kw = ee[:, 0:R]
                new_c = c0
                with nc.Block() as block:
                    @block.vector
                    def _(dve):
                        for d in range(2):
                            dve.tensor_tensor(kw[:, HEADS * d:HEADS * d + HEADS], k_tok[:],
                                              over(turned[:, 2 + d, 0:HEADS], P), ALU.mult).then_inc(V.sem, 1)
                        for d in range(2):
                            dve.wait_ge(E.sem, E.at(d + 1))
                            dve.tensor_copy(new_c[:, HEADS * d:HEADS * d + HEADS], pair_banks(d)[:, :, 0:P + 1]
                                            ).then_inc(V.sem, 1)
                        dve.wait_ge(A.sem, A.at(1))
                        r = den[:].rearrange("p a b -> p (a b)")
                        dve.tensor_reduce(r, qa[:], X_AXIS, ALU.add).then_inc(V.sem, 1)
                        dve.wait_ge(V.sem, V.at(5))
                        dve.tensor_scalar(r, r, 1.0 / P, EPS, ALU.mult, ALU.add).then_inc(V.sem, 1)
                        dve.wait_ge(A.sem, A.at(2))
                        dve.reciprocal(r, r).then_inc(V.sem, 1)
                        dve.wait_ge(V.sem, V.at(7))
                        dve.tensor_tensor(hbuf, hbuf, over(r, P), ALU.mult).then_inc(V.sem, 1)
                        for b in range(4):
                            dve.wait_ge(E.sem, E.at(3 + b))
                            s, h = divmod(4 * b, HEADS)
                            dve.scalar_tensor_tensor(
                                mix[:, h:h + 4, T * s:T * s + T], banks[:, b, :].rearrange("p (n t) -> p n t", t=T),
                                par[:, PCOL["ml_norm_g"]:PCOL["ml_norm_g"] + 1], prj[:, OM + h:OM + h + 4, T * s:T * s + T],
                                ALU.mult, ALU.mult)

                    @block.scalar
                    def _(act):
                        act.activation(qa[:], hbuf, ACT.Square).then_inc(A.sem, 1)
                        act.wait_ge(V.sem, V.at(6))
                        r = den[:].rearrange("p a b -> p (a b)")
                        act.activation(r, r, ACT.Sqrt).then_inc(A.sem, 1)
                        act.activation(prj[:, OM:OM + HEADS], prj[:, OM:OM + HEADS], ACT.Sigmoid).then_inc(A.sem, 1)

                    @block.tensor
                    def _(pe):
                        for d in range(2):
                            pe.wait_ge(V.sem, V.at(d + 1))
                            for h in range(HEADS):
                                mm = pe.matmul(pair_banks(d)[:, h, 0:P + 1], kw[:, HEADS * d + h], va[:, h],
                                               start=True, stop=True)
                            mm.then_inc(E.sem, 1)
                        pe.wait_ge(V.sem, V.at(8))
                        pe.wait_ge(A.sem, A.at(3))
                        for b in range(4):
                            for m in range(4):
                                tr = pe.transpose(banks[:, b, P * m:P * m + P], hbuf[:, 4 * b + m], ident)
                            tr.then_inc(E.sem, 1)
                V.advance(8)
                A.advance(3)
                E.advance(6)
                turn_tiles([new_c[:, :, P]], state_n[:])
                with nc.Block() as block:
                    @block.sync
                    def _(sp):
                        for d in range(2):
                            sp.dma_start(outs["new_ml_C"][0, 0, d].rearrange("h k v -> k h v"),
                                         new_c[:, HEADS * d:HEADS * d + HEADS, 0:P]).then_inc(stored.sem, 16)
                        sp.dma_start(outs["new_ml_n"][0, 0].rearrange("d h k -> (d h) k"), state_n[:, 0]
                                     ).then_inc(stored.sem, 16)
                        sp.wait_ge(stored.sem, stored.at(48))
                stored.advance(48)

        def latent_attention(prj, mix):
            KEYS = 3 * T
            with ExitStack() as scope:
                qn = sb("qn", [P, HEADS, NT], scope=scope)
                qp = sb("qp", [SUB, HEADS, NT], scope=scope)
                kn = sb("kn", [P, HEADS, KEYS], scope=scope)
                vt = sb("vt", [P, 3, HEADS, P], scope=scope)
                kp = sb("kp", [SUB, KEYS], scope=scope)
                with ExitStack() as inner:
                    work = sb("work2", [P, 4, NT], scope=inner)
                    cached = sb("cached", [P, 2, P], scope=inner)
                    cached_kpe = sb("cached_kpe", [P, SUB], scope=inner)
                    turned = sb("turned1", [P, 4, P], scope=inner)
                    kpe_turned = sb("kpe_turned", [SUB, 1, P], scope=inner)
                    kpe_tok = sb("kpe_tok", [P, 1, SUB], scope=inner)
                    cq = sb("cq", [P, Q_RANK // P, 2 * NT], F32R, inner)
                    ckv_hi = sb("ckv_hi", [P, 2, KEYS], F32R, inner)
                    ckv_lo = sb("ckv_lo", [P, 2, KEYS], F32R, inner)
                    tb = sb("tb_uq", [P, 4, NT], scope=inner)
                    with nc.Block() as block:
                        @block.sync
                        def _(sp):
                            sp.dma_start(cached[:, 0:2].rearrange("t a b -> t (a b)"), ins["cache_mla_ckv"][0, 0]
                                         ).then_inc(small_in.sem, 16)
                            sp.dma_start(cached_kpe[:], ins["cache_mla_kpe"][0, 0]).then_inc(small_in.sem, 16)
                            sp.wait_ge(small_in.sem, small_in.at(32))
                    small_in.advance(32)
                    for first, n, name in ((QD, 4, "mla_q_norm_g"), (KV, 2, "mla_kv_norm_g")):
                        feature_rms(prj[:, first:first + n], work,
                                    [(slice(k, k + 1), par[:, PCOL[name] + k:PCOL[name] + k + 1], 1.0)
                                     for k in range(n)], together=True)
                    turn_tiles([prj[:, KV, 0:T], prj[:, KV + 1, 0:T], cached[:, 0], cached[:, 1]],
                               turned[:])
                    turn_tiles([cached_kpe[:]], kpe_turned[:])
                    turn_tiles([prj[0:SUB, PE_T, 0:T]], kpe_tok[:])
                    rotate(prj[0:SUB, PE_T:PE_T + 1, T:NT], C_ROT_SUB, C_COS_SUB, C_SIN_SUB, work)
                    with nc.Block() as block:
                        @block.sync
                        def _(sp):
                            sp.dma_start(outs["new_mla_ckv"][0, 0], turned[:, 0:2].rearrange("t a b -> t (a b)")
                                         ).then_inc(stored.sem, 16)
                            sp.dma_start(outs["new_mla_kpe"][0, 0], kpe_tok[:, 0]).then_inc(stored.sem, 16)
                            sp.wait_ge(stored.sem, stored.at(32))

                        @block.scalar
                        def _(act):
                            act.activation(cq[:, :, 0:NT], prj[:, QD:QD + 4], ACT.Copy).then_inc(A.sem, 1)
                            act.activation(ckv_hi[:, :, 0:NT], prj[:, KV:KV + 2], ACT.Copy).then_inc(A.sem, 1)
                            act.activation(ckv_hi[:, :, NT:KEYS], turned[:, 2:4], ACT.Copy).then_inc(A.sem, 1)

                        @block.vector
                        def _(dve):
                            dve.tensor_copy(kp[:, 0:NT], prj[0:SUB, PE_T])
                            dve.tensor_copy(kp[:, NT:KEYS], kpe_turned[:, 0])
                            dve.wait_ge(A.sem, A.at(3))
                            dve.tensor_tensor(cq[:, :, NT:2 * NT], prj[:, QD:QD + 4], cq[:, :, 0:NT].bitcast(F32),
                                              ALU.subtract)
                            dve.tensor_tensor(ckv_lo[:, :, 0:NT], prj[:, KV:KV + 2], ckv_hi[:, :, 0:NT].bitcast(F32),
                                              ALU.subtract)
                            dve.tensor_tensor(ckv_lo[:, :, NT:KEYS], turned[:, 2:4],
                                              ckv_hi[:, :, NT:KEYS].bitcast(F32), ALU.subtract)
                    A.advance(3)
                    stored.advance(32)

                    def uq_products(pe, f, i, s, g):
                        def tile(half, c, t):
                            first = (NOPE + SUB) * (t % 2) + (0 if t < 2 else NOPE)
                            return half[:, s % SPLIT, c, first:first + (NOPE if t < 2 else SUB)]
                        for c in range(CHUNKS):
                            for t in range(4):
                                bank = banks[0:NOPE if t < 2 else SUB, GROUP * (g % 2) + t]
                                pe.matmul(bank, tile(w_hi, c, t), cq[:, c], start=c == 0, stop=False)
                                mm = pe.matmul(bank[:, 0:NT], tile(w_lo, c, t), cq[:, c, 0:NT], start=False,
                                               stop=c == CHUNKS - 1)
                        return mm

                    def uq_copy(act, f, i, g):
                        act.wait_ge(slab_used.sem, group_used(f, i, g))
                        wait(act, summed.sem, f.group(i, g))
                        b = GROUP * (g % 2)
                        act.activation(tb[0:SUB, 2:4], banks[0:SUB, b + 2:b + 4, NT:2 * NT], ACT.Copy)
                        act.activation(tb[:, 0:2], banks[:, b:b + 2, NT:2 * NT], ACT.Copy).then_inc(part_copied.sem, 1)

                    def uq_add(dve, f, i, g):
                        dve.wait_ge(part_copied.sem, f.group(i, g) + 1)
                        b = GROUP * (g % 2)
                        dve.tensor_tensor(qp[:, 2 * g:2 * g + 2], banks[0:SUB, b + 2:b + 4, 0:NT], tb[0:SUB, 2:4], ALU.add)
                        dve.tensor_tensor(qn[:, 2 * g:2 * g + 2], banks[:, b:b + 2, 0:NT], tb[:, 0:2], ALU.add
                                          ).then_inc(summed.sem, 1)

                    def ukv_products(pe, f, i, s, g):
                        wait(pe, summed.sem, f.group(i, g))
                        hi4, lo4 = (ukv_view(w[:, s % SPLIT]).rearrange("p c (h n) -> p c h n", h=4) for w in (w_hi, w_lo))
                        for c in range(2):
                            for h in range(4):
                                for n, (w, a) in enumerate(((hi4, ckv_hi), (hi4, ckv_lo), (lo4, ckv_hi))):
                                    pe.matmul(banks[:, h, 0:KEYS], w[:, c, h, 0:NOPE], a[:, c, :],
                                              start=c == 0 and n == 0, stop=c == 1 and n == 2)
                            for t in range(3):
                                for n, (w, a) in enumerate(((hi4, ckv_hi), (hi4, ckv_lo), (lo4, ckv_hi))):
                                    mm = pe.matmul(banks[:, 4 + t], a[:, c, T * t:T * t + T], w[:, c, :, NOPE:NOPE + P],
                                                   start=c == 0 and n == 0, stop=c == 1 and n == 2)
                        return mm

                    def ukv_keys(act, f, i, g):
                        act.wait_ge(slab_used.sem, group_used(f, i, g))
                        act.activation(kn[:, 4 * g:4 * g + 4], banks[:, 0:4, 0:KEYS], ACT.Copy).then_inc(part_copied.sem, 1)

                    def ukv_values(dve, f, i, g):
                        dve.wait_ge(part_copied.sem, f.group(i, g) + 1)
                        dve.tensor_copy(vt[:, :, 4 * g:4 * g + 4], banks[:, 4:7, :].rearrange("p t (h n) -> p t h n", h=4)
                                        ).then_inc(summed.sem, 1)

                    project([ph["uq"], ph["ukv"]], None, [[uq_copy], [ukv_keys]], [[uq_add], [ukv_values]],
                            products=[uq_products, ukv_products])
                    resid_skip[0] += 6
                    rotate(qp[:, :, T:NT], C_ROT_SUB, C_COS_SUB, C_SIN_SUB, work)

                def score(stream):
                    cols = slice(0, T) if stream == 0 else slice(T, KEYS)

                    def one(pe, h, out):
                        tok = slice(T * stream, T * stream + T)
                        pe.matmul(out, qn[:, h, tok], kn[:, h, cols], start=True, stop=False)
                        return pe.matmul(out, qp[:, h, tok], kp[:, cols], start=False, stop=True)
                    return one

                common = dict(diff=False, rows=HEADS, scale=(NOPE + SUB) ** -0.5)
                attention([
                    dict(common, keys=T, score=score(0), value=lambda h, c: vt[:, 0, h],
                         dst=lambda h0, n: mix[:, HEADS + h0:HEADS + h0 + n, 0:T]),
                    dict(common, keys=2 * T, score=score(1), value=lambda h, c: vt[:, 1 + c, h],
                         dst=lambda h0, n: mix[:, HEADS + h0:HEADS + h0 + n, T:NT]),
                ], "odd")

        def odd_layer(l):
            with ExitStack() as outer:
                mix = sb("mix1", [P, 2 * HEADS, NT], scope=outer)
                with ExitStack() as scope:
                    prj = sb("prj", [P, 23, NT], scope=scope)
                    gates = sb("gates", [4 * HEADS, NT], scope=scope)
                    with ExitStack() as rec:
                        kq = sb("kq", [P, 2 * HEADS, NT], scope=rec)
                        with ExitStack() as inner:
                            xs = sb("xs_odd", [P, KD, 2 * NT], F32R, inner)
                            norm_of(l, 0, xs)
                            tb = sb("tb_odd", [P, GROUP, NT], scope=inner)
                            u = sb("u_odd", [P, GROUP, NT], scope=inner)
                            y = sb("y_odd", [P, GROUP, NT], scope=inner)
                            fq = ph["odd_qk"]

                            def conv(dve, f, i, g):
                                n = f.group(i, g) - fq.group0
                                dve.wait_ge(part_copied.sem, f.group(i, g) + 1)
                                dve.tensor_tensor(u[:], banks[:, group_banks(g), 0:NT], tb[:], ALU.add
                                                  ).then_inc(summed.sem, 1)
                                dve.wait_ge(summed.sem, f.group(i, g) + 1)
                                wait(dve, silu_done.sem, silu_done.at(n))
                                tile0 = GROUP * (i * f.groups + g)
                                three_taps(dve, u, y, lambda which, t: par[:, PCOL["ml_conv_w"] + which * 2 * HEADS + tile0 + t:][:, 0:1],
                                           lambda t: par[:, PCOL["ml_conv_b"] + tile0 + t:][:, 0:1], n)

                            def silu(act, f, i, g):
                                n = f.group(i, g) - fq.group0
                                act.wait_ge(tap[2].sem, tap[2].at(n + 1))
                                act.activation(kq[:, GROUP * n:GROUP * n + GROUP], y[:], ACT.Silu).then_inc(silu_done.sem, 1)

                            def tail_products(pe, f, i, s, g):
                                spans = ((0, 32), (32, 160), (160, 288), (288, 416)) if g == 0 else \
                                    ((0, 128), (128, 256), (256, 384), (384, 448))
                                for c in range(CHUNKS):
                                    k = CHUNKS * (s % 4) + c
                                    for t, (a, b) in enumerate(spans):
                                        hi, lo = w_hi[:, s % SPLIT, c, a:b], w_lo[:, s % SPLIT, c, a:b]
                                        bank = banks[0:b - a, GROUP * (g % 2) + t]
                                        pe.matmul(bank, hi, xs[:, k], start=k == 0, stop=False)
                                        mm = pe.matmul(bank[:, 0:NT], lo, xs[:, k, 0:NT], start=False, stop=k == KD - 1)
                                return mm

                            def tail_copy(act, f, i, g):
                                act.wait_ge(slab_used.sem, group_used(f, i, g))
                                wait(act, summed.sem, f.group(i, g))
                                if g == 0:
                                    act.activation(tb[0:32, 0], banks[0:32, 0, NT:2 * NT], ACT.Copy)
                                    act.activation(tb[:, 1:4], banks[:, 1:4, NT:2 * NT], ACT.Copy).then_inc(part_copied.sem, 1)
                                else:
                                    act.activation(tb[0:SUB, 3], banks[0:SUB, 7, NT:2 * NT], ACT.Copy)
                                    act.activation(tb[:, 0:3], banks[:, 4:7, NT:2 * NT], ACT.Copy).then_inc(part_copied.sem, 1)

                            def tail_add(dve, f, i, g):
                                dve.wait_ge(part_copied.sem, f.group(i, g) + 1)
                                if g == 0:
                                    dve.tensor_tensor(gates[:], banks[0:32, 0, 0:NT], tb[0:32, 0], ALU.add)
                                    dve.tensor_tensor(prj[:, QD:QD + 3], banks[:, 1:4, 0:NT], tb[:, 1:4], ALU.add
                                                      ).then_inc(summed.sem, 1)
                                else:
                                    dve.tensor_tensor(prj[0:SUB, PE_T], banks[0:SUB, 7, 0:NT], tb[0:SUB, 3], ALU.add)
                                    dve.tensor_tensor(prj[:, QD + 3:QD + 6], banks[:, 4:7, 0:NT], tb[:, 0:3], ALU.add
                                                      ).then_inc(summed.sem, 1)

                            project([fq, ph["odd_vo"], ph["odd_tail"]],
                                    lambda s, k: xs[:, CHUNKS * k:CHUNKS * k + CHUNKS],
                                    [[copy_part(tb), silu], [copy_part(tb)], [tail_copy]],
                                    [[conv], [add_parts(tb, prj)], [tail_add]],
                                    products=[None, None, tail_products])
                            for t in (*tap, silu_done):
                                t.advance(4)
                            resid_skip[0] += 10
                        mlstm(kq, prj, gates, mix)
                    latent_attention(prj, mix)
                out_projection(l, mix)
            ffn(l)

        even_layer(0)
        odd_layer(1)

        with ExitStack() as scope:
            work = sb("work_end", [P, KD, NT], scope=scope)
            y_tok = sb("y_tok", [P, 2 * KD, P], scope=scope)
            g0 = PCOL["final_norm_g"]
            feature_rms(x[:], work, [(slice(k, k + 1), par[:, g0 + k:g0 + k + 1], 1.0) for k in range(KD)], together=True)
            turn_tiles([x[:, k, T * s:T * s + T] for s in range(2) for k in range(KD)], y_tok[:])
            with nc.Block() as block:
                @block.sync
                def _(sp):
                    for s, name in enumerate(("y_prompt", "y_sample")):
                        sp.dma_start(outs[name][0], y_tok[:, KD * s:KD * s + KD].rearrange("t k p -> t (k p)")
                                     ).then_inc(stored.sem, 16)
                    sp.wait_ge(stored.sem, stored.at(32))


INPUTS = ("x_prompt", "x_sample", "cache_da_k", "cache_da_v", "cache_gq_k", "cache_gq_v", "cache_mla_ckv",
          "cache_mla_kpe", "state_ml_C", "state_ml_n", "state_ml_m", "c", "c_ctx", "norm1_g", "norm2_g", "w_mod",
          "b_mod", "even_w_in", "even_w_out", "da_lambda", "da_subln_g", "gq_q_norm_g", "gq_k_norm_g", "odd_w_in",
          "odd_w_out", "ml_conv_w", "ml_conv_b", "ml_gate_b", "ml_norm_g", "mla_q_norm_g", "mla_w_uq",
          "mla_kv_norm_g", "mla_w_ukv", "ffn_w_up", "ffn_conv_w", "ffn_conv_b", "ffn_w_down", "final_norm_g")
OUTPUTS = (("y_prompt", (1, T, D)), ("y_sample", (1, T, D)), ("new_da_k", (1, 1, HEADS, 2, T, SUB)),
           ("new_da_v", (1, 1, HEADS, T, P)), ("new_gq_k", (1, 1, KV_HEADS, T, P)),
           ("new_gq_v", (1, 1, KV_HEADS, T, P)), ("new_mla_ckv", (1, 1, T, KV_RANK)),
           ("new_mla_kpe", (1, 1, T, SUB)), ("new_ml_C", (1, 1, 2, HEADS, P, P)), ("new_ml_n", (1, 1, 2, HEADS, P)),
           ("new_ml_m", (1, 1, 2, HEADS)))


def kernel(**inputs):
    import concourse.bacc as bacc
    from concourse.bass_utils import run_bass_kernel_spmd

    nc = bacc.Bacc("TRN2", target_bir_lowering=False, num_devices=1)
    arrays, ins, outs = {}, {}, {}
    given = {name: np.ascontiguousarray(inputs[name]) for name in INPUTS}
    given["constants"] = constants()
    for name, a in given.items():
        arrays[f"in_{name}"] = a
        ins[name] = nc.dram_tensor(f"in_{name}", a.shape, mybir.dt.from_np(a.dtype), kind="ExternalInput").ap()
    for name, shape in OUTPUTS:
        outs[name] = nc.dram_tensor(f"out_{name}", shape, F32, kind="ExternalOutput").ap()
    trunk(nc, ins, outs)
    r = run_bass_kernel_spmd(nc, [arrays], core_ids=[0])
    return tuple(r.results[0][f"out_{name}"] for name, _ in OUTPUTS)
```

```python
from contextlib import ExitStack

import concourse.bass as bass
import numpy as np
from concourse import mybir

F32 = mybir.dt.float32
F32R = mybir.dt.float32r
ALU = mybir.AluOpType
ACT = mybir.ActivationFunctionType
X_AXIS = mybir.AxisListType.X

P = 128
D = 2048
KD = D // P
T = 128
NT = 2 * T
DEPTH = 2
GRID_W = 64
EPS = 1e-6
HEADS = 8
KV_HEADS = 2
SUB = 64
Q_RANK, KV_RANK = 512, 256
NOPE = 128
D_FF = 5632
KF = D_FF // P
EVEN_TILES = 36
LAM_INIT = 0.8 - 0.6
MASKED = -1.0e30

RAW = 8
SPLIT = 4
CHUNKS = 2
SLABW = 512
GROUP = SLABW // P
MOD_SLABS = KD // CHUNKS
MOD_GROUPS = 6 * D // SLABW
MOD_ROWS, MOD_COLS = 4, 6

C_IDENT, C_ONES, C_ROT_SUB, C_ROT_HD = 0, 128, 256, 384
C_COS_SUB, C_SIN_SUB, C_COS_HD, C_SIN_HD = 512, 640, 768, 896
C_MASK = 1024
C_SEL = 1280
C_SUM = 1408
NCONST = 1410


def constants():
    c = np.zeros((P, NCONST), np.float32)
    c[:, C_IDENT:C_IDENT + P] = np.eye(P)
    c[:, C_ONES:C_ONES + P] = 1.0
    t = np.arange(T)
    for width, rot, cos, sin in ((SUB, C_ROT_SUB, C_COS_SUB, C_SIN_SUB), (P, C_ROT_HD, C_COS_HD, C_SIN_HD)):
        quarter = width // 4
        inv = np.float32(10000.0) ** (-np.arange(quarter, dtype=np.float32) / quarter)
        for f in range(P):
            g = f % width
            axis, half, j = g // (2 * quarter), (g // quarter) % 2, g % quarter
            pos = (t // GRID_W if axis == 0 else t % GRID_W).astype(np.float32)
            angle = pos * inv[j]
            c[f, cos:cos + T] = np.cos(angle)
            c[f, sin:sin + T] = np.sin(angle)
            if half == 0:
                c[f + quarter, rot + f] = -1.0
            else:
                c[f - quarter, rot + f] = 1.0
    c[:, C_MASK:C_MASK + T] = np.where(t[:, None] <= t[None, :], 0.0, MASKED)
    c[:, C_MASK + T:C_MASK + 2 * T] = np.where(t[:, None] >= t[None, :], 0.0, MASKED)
    for direction in range(2):
        for kind in range(2):
            for stream in range(2):
                for h in range(HEADS):
                    col = C_SEL + 16 * (4 * direction + 2 * kind + stream) + 8 * stream + h
                    c[16 * direction + 8 * kind + h, col] = 1.0
    for stream in range(2):
        c[stream, C_SUM + stream] = 1.0
        c[2 + stream, C_SUM + stream] = 1.0
    return c


PARAMS = (
    ("b_mod", DEPTH * 6 * KD), ("norm1_g", DEPTH * KD), ("norm2_g", DEPTH * KD), ("final_norm_g", KD),
    ("ffn_conv_w", DEPTH * 3 * 2 * KF), ("ffn_conv_b", DEPTH * 2 * KF), ("ml_conv_w", 3 * 2 * HEADS),
    ("ml_conv_b", 2 * HEADS), ("c_ctx", KD), ("c", KD), ("da_subln_g", 1), ("gq_q_norm_g", 1),
    ("gq_k_norm_g", 1), ("ml_norm_g", 1), ("mla_q_norm_g", Q_RANK // P), ("mla_kv_norm_g", KV_RANK // P),
    ("state_ml_n", 2 * HEADS),
)
PCOL = {}
_at = 0
for _name, _rows in PARAMS:
    PCOL[_name] = _at
    _at += _rows
NPAR = _at
PAR_TILES = -(-NPAR // P)


class Tally:

    def __init__(self, sem):
        self.sem, self.base = sem, 0

    def at(self, n):
        return self.base + n

    def advance(self, n):
        self.base += n


def wait(eng, sem, value):
    if not isinstance(value, int) or value > 0:
        eng.wait_ge(sem, value)


class Phase:

    def __init__(self, load, iters, groups, per_group, mods=0, iter0=0):
        self.load, self.iters, self.groups, self.per_group, self.mods, self.iter0 = \
            load, iters, groups, per_group, mods, iter0
        self.seq = []
        for g in range(max(groups, mods)):
            own = [("own", g, k) for k in range(per_group)] if g < groups else []
            mod = [("mod", g, k) for k in range(MOD_SLABS)] if g < mods else []
            if own and mod:
                self.seq += [own[0], *(slab for pair in zip(own[1:], mod) for slab in pair), mod[-1]]
            else:
                self.seq += own + mod
        self.slabs = len(self.seq)
        self.ends = [self.seq.index(("own", g, per_group - 1)) for g in range(groups)]
        self.mod_ends = [self.seq.index(("mod", j, MOD_SLABS - 1)) for j in range(mods)]
        self.slab0 = self.group0 = self.mod0 = 0
        self.slot0 = [0] * RAW
        self.before = [0] * RAW
        self.next = None

    def slab(self, i, s):
        return self.slab0 + i * self.slabs + s

    def group(self, i, g):
        return self.group0 + i * self.groups + g

    def mod_group(self, i, j):
        return self.mod0 + i * self.mods + j

    def loads_of(self, slot):
        return (self.slabs - slot + RAW - 1) // RAW if self.slabs > slot else 0

    def first_bank(self, g):
        return 0 if self.mods else GROUP * (g % 2)


def plan(phases):
    slab = group = mod = 0
    held, last = [0] * RAW, [0] * RAW
    for n, ph in enumerate(phases):
        ph.slab0, ph.group0, ph.mod0, ph.slot0, ph.before = slab, group, mod, list(held), list(last)
        for slot in range(RAW):
            k = ph.loads_of(slot)
            held[slot] += k * ph.iters
            if k:
                last[slot] = slab + (ph.iters - 1) * ph.slabs + slot + RAW * (k - 1) + 1
        slab += ph.iters * ph.slabs
        group += ph.iters * ph.groups
        mod += ph.iters * ph.mods
        ph.next = phases[n + 1] if n + 1 < len(phases) else None
    assert mod == DEPTH * MOD_GROUPS


def rolled(eng, iters, body):
    if iters == 1:
        body(0, True, True)
        return
    body(0, True, False)
    if iters > 2:
        with eng.Fori(1, iters - 1) as i:
            body(i, False, False)
    body(iters - 1, False, True)


def over(ap, n):
    return ap.unsqueeze(len(ap.shape)).broadcast_to([*ap.shape, n])


def trunk(nc, ins, outs):
    ctx = ExitStack()
    with ctx:
        def sb(name, shape, dt=F32, scope=ctx):
            return scope.enter_context(nc.sbuf_tensor(name, shape, dt))

        def tally(name):
            return Tally(ctx.enter_context(nc.semaphore(name)))

        raw = sb("raw", [P, RAW, CHUNKS, SLABW])
        w_hi = sb("w_hi", [P, SPLIT, CHUNKS, SLABW], F32R)
        w_lo = sb("w_lo", [P, SPLIT, CHUNKS, SLABW], F32R)
        x = sb("x", [P, KD, NT])
        const = sb("const", [P, NCONST])
        par = sb("par", [P, NPAR])
        mod = sb("mod", [P, DEPTH, 6 * KD, 2])
        norm_gain = sb("norm_gain", [P, DEPTH, 2, KD, 2])
        cond_split = sb("cond_split", [P, KD, 4], F32R)
        mod_rows = sb("mod_rows", [4, 2, SLABW])
        lam = sb("lam", [P, 1])
        gate_b = sb("gate_b", [4 * HEADS, 1])
        m0 = sb("m0", [2 * HEADS, 2])
        banks = ctx.enter_context(nc.psum_tensor("banks", [P, 8, 512], F32))

        ident = const[:, C_IDENT:C_IDENT + P]
        ones = const[:, C_ONES:C_ONES + P]

        landed = [tally(f"landed{s}") for s in range(RAW)]
        hi_done = tally("hi_done")
        lo_done = tally("lo_done")
        slab_used = tally("slab_used")
        part_copied = tally("part_copied")
        summed = tally("summed")
        gated = tally("gated")
        resid = tally("resid")
        rows_out = tally("rows_out")
        rows_turned = tally("rows_turned")
        mod_done = tally("mod_done")
        tap = [tally(f"tap{n}") for n in range(3)]
        silu_done = tally("silu_done")
        act_done = tally("act_done")
        mov_hi = tally("mov_hi")
        mov_lo = tally("mov_lo")
        small_in = tally("small_in")
        tokens_in = tally("tokens_in")
        lam_in = tally("lam_in")
        state_in = tally("state_in")
        pool_step = tally("pool_step")
        stored = tally("stored")
        pe_step = tally("pe_step")
        act_step = tally("act_step")
        dve_step = tally("dve_step")

        def columns(w, first, width=SLABW):
            v = w.rearrange("(s c p) n -> s p c n", c=CHUNKS, p=P)
            return lambda s, n0: v[s, :, :, bass.ds(n0, width) if not isinstance(n0, int) else slice(n0, n0 + width)]

        def plain(w, first, groups_per_iter):
            get = columns(w, first)

            def load(sp, slot, i, g, k):
                return sp.dma_start(raw[:, slot], get(k, first + SLABW * (i * groups_per_iter + g)))
            return load

        def ffn_up_load(w, iter0):
            get = columns(w, 0)

            def load(sp, slot, i, g, k):
                return sp.dma_start(raw[:, slot], get(k, SLABW * (i + iter0) + D_FF * g))
            return load

        def odd_tail_load(w):
            def load(sp, slot, i, g, k):
                n0, width = ((4 * D // 2, 416), (4 * D // 2 + 416, 448))[g]
                v = w.rearrange("(s c p) n -> s p c n", c=CHUNKS, p=P)
                return sp.dma_start(raw[:, slot, :, 0:width], v[k, :, :, n0:n0 + width])
            return load

        def uq_load(sp, slot, i, g, k):
            v = ins["mla_w_uq"][0].rearrange("(s c p) n -> s p c n", c=CHUNKS, p=P)
            return sp.dma_start(raw[:, slot, :, 0:384], v[k, :, :, 384 * g:384 * g + 384])

        def ukv_load(sp, slot, i, g, k):
            v = ins["mla_w_ukv"][0].rearrange("(c p) n -> p c n", p=P)
            return sp.dma_start(raw[:, slot], v[:, :, SLABW * (2 * g + k):SLABW * (2 * g + k + 1)])

        KS = KD // CHUNKS
        ph = {
            "mod": Phase(None, 4, 0, 0, mods=2),
            "even_in": Phase(plain(ins["even_w_in"][0], 0, 2), 4, 2, KS, mods=2),
            "even_in_end": Phase(plain(ins["even_w_in"][0], 8 * SLABW, 1), 1, 1, KS),
            ("out", 0): Phase(plain(ins["even_w_out"][0], 0, 2), 2, 2, KS, mods=2),
            ("up", 0): Phase(ffn_up_load(ins["ffn_w_up"][0], 0), 2, 2, KS, mods=2),
            ("up_end", 0): Phase(ffn_up_load(ins["ffn_w_up"][0], 2), 9, 2, KS, mods=2, iter0=2),
            "odd_qk": Phase(plain(ins["odd_w_in"][0], 0, 2), 2, 2, KS, mods=2),
            "odd_vo": Phase(plain(ins["odd_w_in"][0], 4 * SLABW, 4), 1, 4, KS, mods=2),
            "odd_tail": Phase(odd_tail_load(ins["odd_w_in"][0]), 1, 2, KS),
            "uq": Phase(uq_load, 1, 4, Q_RANK // (P * CHUNKS)),
            "ukv": Phase(ukv_load, 1, 2, 2),
            ("out", 1): Phase(plain(ins["odd_w_out"][0], 0, 2), 2, 2, KS),
            ("up", 1): Phase(ffn_up_load(ins["ffn_w_up"][1], 0), 11, 2, KS),
        }
        for l in range(DEPTH):
            ph["down", l] = Phase(plain(ins["ffn_w_down"][l], 0, 2), 2, 2, KF // CHUNKS)
        order = ["mod", "even_in", "even_in_end", ("out", 0), ("up", 0), ("up_end", 0), ("down", 0),
                 "odd_qk", "odd_vo", "odd_tail", "uq", "ukv", ("out", 1), ("up", 1), ("down", 1)]
        plan([ph[k] for k in order])

        def mod_columns(f, i, j):
            l = f.mod0 // MOD_GROUPS
            return l, GROUP * (f.mod_group(i, j) - l * MOD_GROUPS)

        def mod_load(sp, f, slot, i, j, k):
            l, tile = mod_columns(f, i, j)
            return sp.dma_start(raw[:, slot], columns(ins["w_mod"][l], 0)(k, P * tile))

        def load_slab(sp, f, i, s, in_slot_before):
            slot = s % RAW
            wait(sp, hi_done.sem, in_slot_before)
            wait(sp, lo_done.sem, in_slot_before)
            kind, g, k = f.seq[s]
            dma = f.load(sp, slot, i, g, k) if kind == "own" else mod_load(sp, f, slot, i, g, k)
            dma.then_inc(landed[slot].sem, 16)

        def sp_first(sp, f):
            if f is not None:
                for s in range(min(RAW, f.slabs)):
                    load_slab(sp, f, 0, s, f.before[s])

        def sp_stream(sp, f):
            def body(i, first, last):
                for s in range(RAW, f.slabs):
                    load_slab(sp, f, i, s, f.slab(i, s - RAW) + 1)
                if last:
                    sp_first(sp, f.next)
                else:
                    for s in range(RAW):
                        newest = s + RAW * (f.loads_of(s) - 1)
                        load_slab(sp, f, i + 1, s, f.slab(i, newest) + 1)
            rolled(sp, f.iters, body)

        def slab_landed(f, i, s):
            slot = s % RAW
            return landed[slot].sem, 16 * (f.slot0[slot] + i * f.loads_of(slot) + s // RAW + 1)

        def split_hi(act, f, i, s):
            q = f.slab(i, s)
            act.wait_ge(*slab_landed(f, i, s))
            wait(act, slab_used.sem, q - SPLIT + 1)
            act.activation(w_hi[:, s % SPLIT], raw[:, s % RAW], ACT.Copy).then_inc(hi_done.sem, 1)

        def split_lo(dve, f, i, s):
            q = f.slab(i, s)
            dve.wait_ge(hi_done.sem, q + 1)
            wait(dve, slab_used.sem, q - SPLIT + 1)
            dve.tensor_tensor(w_lo[:, s % SPLIT], raw[:, s % RAW], w_hi[:, s % SPLIT].bitcast(F32),
                              ALU.subtract).then_inc(lo_done.sem, 1)

        def split_stream(eng, f, split, places, also=None):
            def body(i, first, last):
                for s in range(f.slabs):
                    run_pieces(f, places, i, s, first)
                    ahead = s + SPLIT
                    if ahead < f.slabs:
                        split(eng, f, i, ahead)
                        if also:
                            also(i, ahead)
                    elif not last:
                        split(eng, f, i + 1, ahead - f.slabs)
                        if also:
                            also(i + 1, ahead - f.slabs)
                    elif f.next is not None:
                        split(eng, f.next, 0, ahead - f.slabs)
            rolled(eng, f.iters, body)
            finish_pieces(f, places)

        def placed(f, pieces, mod_pieces):
            return [(end + d, piece, g)
                    for ends, all_ in ((f.ends, pieces), (f.mod_ends, mod_pieces))
                    for g, end in enumerate(ends) for d, piece in enumerate(all_) if piece is not None]

        def run_pieces(f, places, i, s, first):
            for at, piece, g in places:
                if at == s:
                    piece(i, g)
                elif at == s + f.slabs and not first:
                    piece(i - 1, g)

        def finish_pieces(f, places):
            for s in range(f.slabs, 2 * f.slabs):
                for at, piece, g in places:
                    if at == s:
                        piece(f.iters - 1, g)

        def product_stream(pe, f, slab_products):
            places = placed(f, [], [None] * 3 + [lambda i, j: turn_mod(pe, f, i, j)])

            def body(i, first, last):
                for s, (kind, g, k) in enumerate(f.seq):
                    pe.wait_ge(lo_done.sem, f.slab(i, s) + 1)
                    if kind == "mod":
                        products = mod_products(pe, f, i, s, g, k)
                    else:
                        if k == 0:
                            alternating = not f.mods and not (first and g == 0)
                            wait(pe, summed.sem, f.group(i, g) - (1 if alternating else 0))
                            if first and g == 1 and not f.mods:
                                wait(pe, mod_done.sem, f.mod0)
                        products = slab_products(i, s, g, k)
                    products.then_inc(slab_used.sem, 1)
                    run_pieces(f, places, i, s, first)
            rolled(pe, f.iters, body)
            finish_pieces(f, places)

        def mod_products(pe, f, i, s, j, k):
            if k == 0:
                wait(pe, rows_out.sem, f.mod_group(i, j) - 1)
            for c in range(CHUNKS):
                for n, half in enumerate((w_hi, w_lo)):
                    mm = pe.matmul(banks[0:4, MOD_ROWS + j % 2, :], cond_split[:, CHUNKS * k + c, :],
                                   half[:, s % SPLIT, c, :], start=(k == 0 and c == 0 and n == 0),
                                   stop=(k == MOD_SLABS - 1 and c == CHUNKS - 1 and n == 1))
            return mm

        def copy_mod_rows(act, f, i, j):
            n = f.mod_group(i, j)
            act.wait_ge(slab_used.sem, f.slab(i, f.mod_ends[j]) + 1)
            wait(act, rows_turned.sem, n - 1)
            act.activation(mod_rows[:, j % 2, :], banks[0:4, MOD_ROWS + j % 2, :], ACT.Copy).then_inc(rows_out.sem, 1)

        def turn_mod(pe, f, i, j):
            n = f.mod_group(i, j)
            pe.wait_ge(rows_out.sem, n + 1)
            wait(pe, mod_done.sem, n - 1)
            for t in range(GROUP):
                mm = pe.matmul(banks[:, MOD_COLS + j % 2, 2 * t:2 * t + 2], mod_rows[:, j % 2, P * t:P * t + P],
                               const[0:4, C_SUM:C_SUM + 2], start=True, stop=True)
            mm.then_inc(rows_turned.sem, 1)

        def add_mod_bias(dve, f, i, j):
            dve.wait_ge(rows_turned.sem, f.mod_group(i, j) + 1)
            l, tile = mod_columns(f, i, j)
            bias = par[:, PCOL["b_mod"] + l * 6 * KD:PCOL["b_mod"] + (l + 1) * 6 * KD]
            dve.tensor_tensor(mod[:, l, tiles_at(tile, GROUP), :],
                              banks[:, MOD_COLS + j % 2, 0:2 * GROUP].rearrange("p (t s) -> p t s", s=2),
                              over(bias[:, tiles_at(tile, GROUP)], 2), ALU.add).then_inc(mod_done.sem, 1)

        def tiles_at(n, k):
            return slice(n, n + k) if isinstance(n, int) else bass.ds(n, k)

        def tile_products(pe, slot, first_bank, moving, start, stop):
            for c in range(CHUNKS):
                for t in range(GROUP):
                    bank = banks[:, first_bank + t]
                    cols = slice(P * t, P * t + P)
                    pe.matmul(bank, w_hi[:, slot, c, cols], moving[:, c, :], start=start and c == 0, stop=False)
                    mm = pe.matmul(bank[:, 0:NT], w_lo[:, slot, c, cols], moving[:, c, 0:NT],
                                   start=False, stop=stop and c == CHUNKS - 1)
            return mm

        def group_banks(f, g):
            return slice(f.first_bank(g), f.first_bank(g) + GROUP)

        def split_products(pe, f, operand, moving_ready=None):
            def one(i, s, g, k):
                if moving_ready is not None:
                    moving_ready(i, s)
                return tile_products(pe, s % SPLIT, f.first_bank(g), operand(s, k), k == 0, k == f.per_group - 1)
            product_stream(pe, f, one)

        with ExitStack() as scope:
            rows = sb("rows", [P, PAR_TILES, P], scope=scope)
            tokens = sb("tokens", [P, 2, D], scope=scope)
            cond_f = sb("cond_f", [P, KD, 2], scope=scope)
            lam_rows = sb("lam_rows", [P, 4 * SUB], scope=scope)
            lam_prod = sb("lam_prod", [P, 2 * SUB], scope=scope)
            lam_sum = sb("lam_sum", [P, 2], scope=scope)
            first = ph[order[0]]

            pieces_in = []
            for name, n in PARAMS:
                flat = ins[name].rearrange(
                    {1: "(n p) -> n p", 2: "a (n p) -> (a n) p", 3: "a b (n p) -> (a b n) p",
                     4: "a b c (n p) -> (a b c n) p", 5: "a b c d (n p) -> (a b c d n) p"}[len(ins[name].shape)], p=P)
                r = 0
                while r < n:
                    tile, row = divmod(PCOL[name] + r, P)
                    k = min(n - r, P - row)
                    pieces_in.append((rows[row:row + k, tile, :], flat[r:r + k, :]))
                    r += k
            with nc.Block() as block:
                @block.sync
                def _(sp):
                    sp.dma_start(const[:], ins["constants"]).then_inc(small_in.sem, 16)
                    for dst, src in pieces_in:
                        sp.dma_start(dst, src).then_inc(small_in.sem, 16)
                    sp_first(sp, first)

                @block.gpsimd
                def _(pool):
                    pool.memset(m0[:], 0.0).then_inc(pool_step.sem, 1)
                    pool.wait_ge(pool_step.sem, 1)
                    pool.dma_start(m0[HEADS:2 * HEADS, :], ins["state_ml_m"][0, 0].rearrange("d h -> h d"),
                                   allow_slow_non_contiguous=True).then_inc(state_in.sem, 16)
                    pool.dma_start(gate_b[:], ins["ml_gate_b"].rearrange("a n -> n a"),
                                   allow_slow_non_contiguous=True).then_inc(state_in.sem, 16)
                    pool.wait_ge(state_in.sem, 32)

                @block.scalar
                def _(act):
                    act.dma_start(tokens[:, 0, :], ins["x_prompt"][0]).then_inc(tokens_in.sem, 16)
                    act.dma_start(tokens[:, 1, :], ins["x_sample"][0]).then_inc(tokens_in.sem, 16)
                    act.dma_start(lam_rows[:], ins["da_lambda"].rearrange("a b c -> a (b c)")
                                  .broadcast_to([P, 4 * SUB])).then_inc(lam_in.sem, 16)
                    act.wait_ge(dve_step.sem, 1)
                    act.activation(cond_f[:], par[:, PCOL["c_ctx"]:PCOL["c_ctx"] + 2 * KD]
                                   .rearrange("p (s k) -> p k s", s=2), ACT.Silu).then_inc(act_step.sem, 1)
                    act.wait_ge(act_step.sem, 1)
                    act.activation(cond_split[:, :, 0:2], cond_f[:], ACT.Copy).then_inc(act_step.sem, 1)
                    act.wait_ge(dve_step.sem, 4)
                    act.activation(lam_sum[:], lam_sum[:], ACT.Exp).then_inc(act_step.sem, 1)
                    for s in range(SPLIT):
                        split_hi(act, first, 0, s)

                @block.vector
                def _(dve):
                    dve.wait_ge(pe_step.sem, 1)
                    for b in range(0, PAR_TILES, 4):
                        k = min(4, PAR_TILES - b) * P
                        k = min(k, NPAR - b * P)
                        cp = dve.tensor_copy(par[:, b * P:b * P + k], banks[:, b // 4, 0:k])
                    cp.then_inc(dve_step.sem, 1)
                    dve.wait_ge(act_step.sem, 2)
                    dve.tensor_tensor(cond_split[:, :, 2:4], cond_f[:], cond_split[:, :, 0:2].bitcast(F32),
                                      ALU.subtract).then_inc(dve_step.sem, 1)
                    dve.wait_ge(lam_in.sem, 16)
                    lr = lam_rows[:].rearrange("p (a b c) -> p a b c", a=2, b=2)
                    dve.tensor_tensor(lam_prod[:].rearrange("p (a c) -> p a c", a=2), lr[:, :, 0], lr[:, :, 1],
                                      ALU.mult).then_inc(dve_step.sem, 1)
                    dve.wait_ge(dve_step.sem, 3)
                    dve.tensor_reduce(lam_sum[:], lam_prod[:].rearrange("p (a c) -> p a c", a=2), X_AXIS,
                                      ALU.add).then_inc(dve_step.sem, 1)
                    for s in range(2):
                        for b in range(4):
                            dve.wait_ge(pe_step.sem, 2 + 4 * s + b)
                            dve.tensor_copy(x[:, 4 * b:4 * b + 4, T * s:T * s + T],
                                            banks[:, 3 + (4 * s + b) % 4, :].rearrange("p (k t) -> p k t", k=4)
                                            ).then_inc(dve_step.sem, 1)
                    dve.wait_ge(act_step.sem, 3)
                    dve.tensor_tensor(lam[:], lam_sum[:, 0:1], lam_sum[:, 1:2], ALU.subtract
                                      ).then_inc(dve_step.sem, 1)
                    dve.wait_ge(dve_step.sem, 13)
                    dve.tensor_scalar(lam[:], lam[:], LAM_INIT, None, ALU.add).then_inc(dve_step.sem, 1)
                    for s in range(SPLIT):
                        split_lo(dve, first, 0, s)

                @block.tensor
                def _(pe):
                    pe.wait_ge(small_in.sem, 16 * (1 + len(pieces_in)))
                    for b in range(PAR_TILES):
                        k = min(P, NPAR - b * P)
                        tr = pe.transpose(banks[:, b // 4, P * (b % 4):P * (b % 4) + k], rows[0:k, b, :],
                                          ident[0:k, 0:k])
                    tr.then_inc(pe_step.sem, 1)
                    pe.wait_ge(tokens_in.sem, 32)
                    for s in range(2):
                        for b in range(4):
                            if s:
                                pe.wait_ge(dve_step.sem, 5 + b)
                            for k in range(4):
                                tr = pe.transpose(banks[:, 3 + (4 * s + b) % 4, P * k:P * k + P],
                                                  tokens[:, s, P * (4 * b + k):P * (4 * b + k) + P], ident)
                            tr.then_inc(pe_step.sem, 1)
            small_in.advance(16 * (1 + len(pieces_in)))
            pool_step.advance(1)
            pe_step.advance(9)
            act_step.advance(3)
            dve_step.advance(14)

        def norm_stage(xs, gains, scales, gain, shifts, tag):
            with ExitStack() as scope:
                h = sb(f"h_{tag}", [P, KD, NT], scope=scope)
                r = sb(f"r_{tag}", [P, NT], scope=scope)
                A, V, E = act_step, dve_step, pe_step
                with nc.Block() as block:
                    @block.scalar
                    def _(act):
                        for b in range(4):
                            act.activation(h[:, 4 * b:4 * b + 4], x[:, 4 * b:4 * b + 4], ACT.Square
                                           ).then_inc(A.sem, 1)
                        act.wait_ge(V.sem, V.at(1))
                        act.activation(r[:], r[:], ACT.Sqrt).then_inc(A.sem, 1)
                        for b in range(4):
                            act.wait_ge(V.sem, V.at(7 + b))
                            act.activation(xs[:, 4 * b:4 * b + 4, 0:NT], h[:, 4 * b:4 * b + 4], ACT.Copy
                                           ).then_inc(A.sem, 1)

                    @block.tensor
                    def _(pe):
                        for b in range(4):
                            pe.wait_ge(A.sem, A.at(1 + b))
                            for k in range(4 * b, 4 * b + 4):
                                mm = pe.matmul(banks[:, 0, 0:NT], ones, h[:, k, :], start=k == 0, stop=k == KD - 1)
                        mm.then_inc(E.sem, 1)

                    @block.vector
                    def _(dve):
                        dve.scalar_tensor_tensor(gains, scales, 1.0, over(gain, 2), ALU.add, ALU.mult)
                        dve.wait_ge(E.sem, E.at(1))
                        dve.tensor_scalar(r[:], banks[:, 0, 0:NT], 1.0 / D, EPS, ALU.mult, ALU.add
                                          ).then_inc(V.sem, 1)
                        dve.wait_ge(A.sem, A.at(5))
                        dve.reciprocal(r[:], r[:]).then_inc(V.sem, 1)
                        dve.wait_ge(V.sem, V.at(2))
                        for b in range(4):
                            dve.tensor_tensor(h[:, 4 * b:4 * b + 4], x[:, 4 * b:4 * b + 4],
                                              r[:].unsqueeze(1).broadcast_to([P, 4, NT]), ALU.mult
                                              ).then_inc(V.sem, 1)
                        for b in range(4):
                            dve.wait_ge(V.sem, V.at(3 + b))
                            for k in range(4 * b, 4 * b + 4):
                                for s in range(2):
                                    part = h[:, k, T * s:T * s + T]
                                    ts = dve.tensor_scalar(part, part, gains[:, k, s:s + 1], shifts[:, k, s:s + 1],
                                                           ALU.mult, ALU.add)
                            ts.then_inc(V.sem, 1)
                        for b in range(4):
                            dve.wait_ge(A.sem, A.at(6 + b))
                            dve.tensor_tensor(xs[:, 4 * b:4 * b + 4, NT:2 * NT], h[:, 4 * b:4 * b + 4],
                                              xs[:, 4 * b:4 * b + 4, 0:NT].bitcast(F32), ALU.subtract)
                A.advance(9)
                V.advance(10)
                E.advance(1)

        def norm_of(l, n, xs):
            norm_stage(xs, norm_gain[:, l, n], mod[:, l, (3 * n + 1) * KD:(3 * n + 2) * KD, :],
                       par[:, PCOL[f"norm{n + 1}_g"] + l * KD:PCOL[f"norm{n + 1}_g"] + (l + 1) * KD],
                       mod[:, l, 3 * n * KD:(3 * n + 1) * KD, :], f"{l}{n}")

        def project(phases, operand, act_pieces, dve_pieces, act_also=None, dve_also=None, moving_ready=None,
                    products=None):
            def bound(eng, f, pieces):
                return [p and (lambda i, g, p=p: p(eng, f, i, g)) for p in pieces]

            with nc.Block() as block:
                @block.sync
                def _(sp):
                    for f in phases:
                        sp_stream(sp, f)

                @block.scalar
                def _(act):
                    for n, f in enumerate(phases):
                        split_stream(act, f, split_hi, placed(f, bound(act, f, act_pieces[n]),
                                                              bound(act, f, [copy_mod_rows])),
                                     also=(lambda i, s, f=f: act_also(act, f, i, s)) if act_also else None)

                @block.vector
                def _(dve):
                    for n, f in enumerate(phases):
                        split_stream(dve, f, split_lo, placed(f, bound(dve, f, dve_pieces[n]),
                                                              bound(dve, f, [None] * 5 + [add_mod_bias])),
                                     also=(lambda i, s, f=f: dve_also(dve, f, i, s)) if dve_also else None)

                @block.tensor
                def _(pe):
                    for n, f in enumerate(phases):
                        own = products and products[n]
                        if own:
                            product_stream(pe, f, lambda i, s, g, k, f=f, own=own: own(pe, f, i, s, g, k))
                        else:
                            split_products(pe, f, operand, moving_ready and (
                                lambda i, s, f=f: moving_ready(pe, f, i, s)))

        def group_used(f, i, g):
            return f.slab(i, f.ends[g]) + 1

        def copy_part(tb):
            def piece(act, f, i, g):
                act.wait_ge(slab_used.sem, group_used(f, i, g))
                wait(act, summed.sem, f.group(i, g))
                act.activation(tb[:], banks[:, group_banks(f, g), NT:2 * NT], ACT.Copy).then_inc(part_copied.sem, 1)
            return piece

        def add_parts(tb, dst, first=0):
            def piece(dve, f, i, g):
                dve.wait_ge(part_copied.sem, f.group(i, g) + 1)
                n = first + GROUP * (i * f.groups + g)
                dve.tensor_tensor(dst[:, tiles_at(n, GROUP), :], banks[:, group_banks(f, g), 0:NT], tb[:], ALU.add
                                  ).then_inc(summed.sem, 1)
            return piece

        def residual_pieces(tb, gate):
            def act_piece(act, f, i, g):
                act.wait_ge(slab_used.sem, group_used(f, i, g))
                wait(act, resid.sem, f.group(i, g) - resid_skip[0])
                act.activation(tb[:], banks[:, group_banks(f, g), NT:2 * NT], ACT.Copy).then_inc(part_copied.sem, 1)

            def add(dve, f, i, g):
                dve.wait_ge(part_copied.sem, f.group(i, g) + 1)
                dve.tensor_tensor(tb[:], banks[:, group_banks(f, g), 0:NT], tb[:], ALU.add).then_inc(summed.sem, 1)

            def multiply(dve, f, i, g):
                dve.wait_ge(summed.sem, f.group(i, g) + 1)
                tile0 = GROUP * (i * f.groups + g)
                four = tb[:].rearrange("p t (s n) -> p (t s) n", s=2)
                dve.tensor_tensor(four, four, over(gate[:, tiles_at(tile0, GROUP), :].rearrange("p t s -> p (t s)"), T),
                                  ALU.mult).then_inc(gated.sem, 1)

            def update(dve, f, i, g):
                dve.wait_ge(gated.sem, f.group(i, g) - resid_skip[0] + 1)
                xt = x[:, tiles_at(GROUP * (i * f.groups + g), GROUP), :]
                dve.tensor_tensor(xt, xt, tb[:], ALU.add).then_inc(resid.sem, 1)
            return [act_piece], [add, multiply, update]

        resid_skip = [0]

        def convolution(tb, u, y, weight, bias, count, y_free):
            def add(dve, f, i, g):
                dve.wait_ge(part_copied.sem, f.group(i, g) + 1)
                wait(dve, tap[2].sem, tap[2].at(count(f, i, g)))
                dve.tensor_tensor(u[:], banks[:, group_banks(f, g), 0:NT], tb[:], ALU.add).then_inc(summed.sem, 1)

            def middle(act, f, i, g):
                act.wait_ge(summed.sem, f.group(i, g) + 1)
                y_free(act, f, i, g)
                for t in range(GROUP):
                    mid = act.activation(y[:, g % 2, t], u[:, t], ACT.Identity, bias=bias(f, i, g, t),
                                         scale=weight(f, i, g, 1, t))
                mid.then_inc(tap[0].sem, 1)

            def neighbour(which):
                to, frm = ((1, 0), None, (0, 1))[which]
                before, after = (tap[0], tap[1]) if which == 0 else (tap[1], tap[2])

                def piece(dve, f, i, g):
                    dve.wait_ge(before.sem, before.at(count(f, i, g) + 1))
                    for t in range(GROUP):
                        yt = y[:, g % 2, t].rearrange("p (s n) -> p s n", s=2)[:, :, to:to + T - 1]
                        ut = u[:, t].rearrange("p (s n) -> p s n", s=2)[:, :, frm:frm + T - 1]
                        added = dve.scalar_tensor_tensor(yt, ut, weight(f, i, g, which, t), yt, ALU.mult, ALU.add)
                    added.then_inc(after.sem, 1)
                return piece
            return [copy_part(tb), middle], [add, None, neighbour(0), neighbour(2)]

        project([ph["mod"]], None, [[]], [[]])

        def ffn(l):
            ups, down = [ph[k, l] for k in ("up", "up_end") if (k, l) in ph], ph["down", l]
            with ExitStack() as scope:
                acts = sb(f"acts{l}", [P, KF, NT], scope=scope)
                xs = sb(f"xs_ffn{l}", [P, KD, 2 * NT], F32R, scope)
                norm_of(l, 1, xs)
                tb = sb(f"tb{l}", [P, GROUP, NT], scope=scope)
                u = sb(f"u{l}", [P, GROUP, NT], scope=scope)
                y = sb(f"y{l}", [P, 2, GROUP, NT], scope=scope)
                conv_col = PCOL["ffn_conv_w"] + l * 3 * 2 * KF
                bias_col = PCOL["ffn_conv_b"] + l * 2 * KF

                def column(base):
                    return lambda f, i, g, t: par[:, tiles_at(base + g * KF + t + GROUP * (i + f.iter0), 1)]

                def weight(f, i, g, which, t):
                    return column(conv_col + which * 2 * KF)(f, i, g, t)

                def y_free(act, f, i, g):
                    wait(act, act_done.sem, act_done.at(i + f.iter0))

                def silu(act, f, i, g):
                    if g == 0:
                        act.wait_ge(tap[2].sem, tap[2].at(f.group(i, g) - ups[0].group0 + 1))
                        act.activation(y[:, 0], y[:, 0], ACT.Silu).then_inc(silu_done.sem, 1)

                def multiply(dve, f, i, g):
                    if g == 1:
                        dve.wait_ge(tap[2].sem, tap[2].at(f.group(i, g) - ups[0].group0 + 1))
                        dve.wait_ge(silu_done.sem, silu_done.at(i + f.iter0 + 1))
                        dve.tensor_tensor(acts[:, tiles_at(GROUP * (i + f.iter0), GROUP), :], y[:, 0], y[:, 1], ALU.mult
                                          ).then_inc(act_done.sem, 1)

                act_pieces, dve_pieces = convolution(tb, u, y, weight, column(bias_col),
                                                     lambda f, i, g: f.group(i, g) - ups[0].group0, y_free)
                project(ups, lambda s, k: xs[:, CHUNKS * k:CHUNKS * k + CHUNKS],
                        [[*act_pieces, None, None, silu]] * len(ups), [[*dve_pieces, multiply]] * len(ups))
                iters = sum(f.iters for f in ups)
                for t in tap:
                    t.advance(2 * iters)
                for t in (silu_done, act_done):
                    t.advance(iters)
                resid_skip[0] += 2 * iters

                def chunk0(s):
                    return CHUNKS * (s % down.per_group)

                def slot_of(s):
                    return slice(CHUNKS * (s % SPLIT), CHUNKS * (s % SPLIT) + CHUNKS)

                def moving_hi(act, f, i, s):
                    act.activation(xs[:, slot_of(s), 0:NT], acts[:, chunk0(s):chunk0(s) + CHUNKS], ACT.Copy
                                   ).then_inc(mov_hi.sem, 1)

                def moving_lo(dve, f, i, s):
                    dve.wait_ge(mov_hi.sem, mov_hi.at(i * f.slabs + s + 1))
                    dve.tensor_tensor(xs[:, slot_of(s), NT:2 * NT], acts[:, chunk0(s):chunk0(s) + CHUNKS],
                                      xs[:, slot_of(s), 0:NT].bitcast(F32), ALU.subtract).then_inc(mov_lo.sem, 1)

                act_pieces, dve_pieces = residual_pieces(tb, mod[:, l, 5 * KD:6 * KD, :])
                with nc.Block() as block:
                    @block.scalar
                    def _(act):
                        for s in range(SPLIT):
                            moving_hi(act, down, 0, s)

                    @block.vector
                    def _(dve):
                        for s in range(SPLIT):
                            moving_lo(dve, down, 0, s)
                project([down], lambda s, k: xs[:, slot_of(s)], [act_pieces], [dve_pieces],
                        act_also=moving_hi, dve_also=moving_lo,
                        moving_ready=lambda pe, f, i, s: pe.wait_ge(mov_lo.sem, mov_lo.at(i * f.slabs + s + 1)))
                mov_hi.advance(down.iters * down.slabs)
                mov_lo.advance(down.iters * down.slabs)

        def out_projection(l, mix):
            f = ph["out", l]
            with ExitStack() as scope:
                xs = sb(f"xs_out{l}", [P, KD, 2 * NT], F32R, scope)
                tb = sb(f"tb_out{l}", [P, GROUP, NT], scope=scope)
                A = act_step
                with nc.Block() as block:
                    @block.scalar
                    def _(act):
                        for b in range(4):
                            act.activation(xs[:, 4 * b:4 * b + 4, 0:NT], mix[:, 4 * b:4 * b + 4], ACT.Copy
                                           ).then_inc(A.sem, 1)

                    @block.vector
                    def _(dve):
                        for b in range(4):
                            dve.wait_ge(A.sem, A.at(1 + b))
                            dve.tensor_tensor(xs[:, 4 * b:4 * b + 4, NT:2 * NT], mix[:, 4 * b:4 * b + 4],
                                              xs[:, 4 * b:4 * b + 4, 0:NT].bitcast(F32), ALU.subtract)
                A.advance(4)
                act_pieces, dve_pieces = residual_pieces(tb, mod[:, l, 2 * KD:3 * KD, :])
                project([f], lambda s, k: xs[:, CHUNKS * k:CHUNKS * k + CHUNKS], [act_pieces], [dve_pieces])

        A, V, E = act_step, dve_step, pe_step

        def feature_rms(src, work, gains, together=False):
            n = src.shape[1]
            count = 1 if together else n
            flat = work.rearrange("p n t -> p (n t)")
            sq, r = flat[:, 0:n * NT], flat[:, 0:count * NT]
            with nc.Block() as block:
                @block.scalar
                def _(act):
                    act.activation(sq.rearrange("p (n t) -> p n t", n=n), src, ACT.Square).then_inc(A.sem, 1)
                    act.wait_ge(V.sem, V.at(1))
                    act.activation(r, r, ACT.Sqrt).then_inc(A.sem, 1)

                @block.tensor
                def _(pe):
                    pe.wait_ge(A.sem, A.at(1))
                    if together:
                        for k in range(n):
                            mm = pe.matmul(banks[:, 0, 0:NT], ones, sq[:, k * NT:k * NT + NT],
                                           start=k == 0, stop=k == n - 1)
                    else:
                        for b in range(0, n, 2):
                            mm = pe.matmul(banks[:, b // 2, :], ones, sq[:, b * NT:(b + 2) * NT], start=True, stop=True)
                    mm.then_inc(E.sem, 1)

                @block.vector
                def _(dve):
                    dve.wait_ge(E.sem, E.at(1))
                    sums = banks[:].rearrange("p b n -> p (b n)")[:, 0:count * NT]
                    dve.tensor_scalar(r, sums, 1.0 / (P * n if together else P), EPS, ALU.mult, ALU.add
                                      ).then_inc(V.sem, 1)
                    dve.wait_ge(A.sem, A.at(2))
                    dve.reciprocal(r, r).then_inc(V.sem, 1)
                    dve.wait_ge(V.sem, V.at(2))
                    scale = (r.unsqueeze(1).broadcast_to([P, n, NT]) if together
                             else r.rearrange("p (n t) -> p n t", n=n))
                    dve.tensor_tensor(src, src, scale, ALU.mult).then_inc(V.sem, 1)
                    dve.wait_ge(V.sem, V.at(3))
                    for tiles, gain, factor in gains:
                        dve.tensor_scalar(src[:, tiles], src[:, tiles], gain, factor, ALU.mult, ALU.mult)
            A.advance(2)
            V.advance(3)
            E.advance(1)

        def rotate(src, rot_col, cos_col, sin_col, work):
            R, n = src.shape[0:2]
            tmp = work.rearrange("p n t -> p (n t)")[0:R, 0:n * T].rearrange("p (n t) -> p n t", n=n)
            with nc.Block() as block:
                @block.tensor
                def _(pe):
                    for b in range(0, n, 4):
                        k = min(4, n - b)
                        mm = pe.matmul(banks[0:R, b // 4, 0:k * T], const[0:R, rot_col:rot_col + R], src[:, b:b + k, :],
                                       start=True, stop=True)
                    mm.then_inc(E.sem, 1)

                @block.vector
                def _(dve):
                    def table(c):
                        return const[0:R, c:c + T].unsqueeze(1).broadcast_to([R, n, T])
                    dve.wait_ge(E.sem, E.at(1))
                    turned = banks[0:R].rearrange("p b n -> p (b n)")[:, 0:n * T].rearrange("p (n t) -> p n t", n=n)
                    dve.tensor_tensor(tmp, turned, table(sin_col), ALU.mult)
                    dve.tensor_tensor(src, src, table(cos_col), ALU.mult).then_inc(V.sem, 1)
                    dve.wait_ge(V.sem, V.at(1))
                    dve.tensor_tensor(src, src, tmp, ALU.add)
            V.advance(1)
            E.advance(1)

        def turn_tiles(srcs, dst):
            with nc.Block() as block:
                batches = [srcs[b:b + 4] for b in range(0, len(srcs), 4)]

                @block.tensor
                def _(pe):
                    for b, batch in enumerate(batches):
                        wait(pe, A.sem, A.at(b - 7) if b >= 8 else 0)
                        for j, s in enumerate(batch):
                            rows, cols = s.shape
                            tr = pe.transpose(banks[0:cols, b % 8, P * j:P * j + rows], s, ident[0:rows, 0:rows])
                        tr.then_inc(E.sem, 1)

                @block.scalar
                def _(act):
                    for b, batch in enumerate(batches):
                        act.wait_ge(E.sem, E.at(b + 1))
                        cols, rows = batch[0].shape[1], batch[0].shape[0]
                        act.activation(dst[0:cols, 4 * b:4 * b + len(batch), 0:rows],
                                       banks[0:cols, b % 8, 0:P * len(batch)].rearrange("p (n r) -> p n r", r=P)[:, :, 0:rows],
                                       ACT.Copy).then_inc(A.sem, 1)
            A.advance(len(batches))
            E.advance(len(batches))

        scores_in = tally("scores_in")
        scores_out = tally("scores_out")
        row_max = tally("row_max")
        exped = tally("exped")
        row_sum = tally("row_sum")
        row_inv = tally("row_inv")
        inv_signed = tally("inv_signed")
        scaled = tally("scaled")
        weights_in = tally("weights_in")
        w_turned = tally("w_turned")
        w_copied = tally("w_copied")
        mixed = tally("mixed")
        mixed_out = tally("mixed_out")

        def attention(blocks, tag):
            with ExitStack() as scope:
                e = sb(f"e_{tag}", [P, 2, 2048], scope=scope)
                wt = sb(f"wt_{tag}", [P, 2, 8, P], scope=scope)
                mx = sb(f"mx_{tag}", [P, 2, 16], scope=scope)
                inv = sb(f"inv_{tag}", [P, 2, 16], scope=scope)
                scores = banks[:, 0:4].rearrange("p b n -> p (b n)")
                rounds, at = [], 0
                for b, k in enumerate(blocks):
                    heads = k["rows"] // (2 if k["diff"] else 1)
                    chunks = k["keys"] // T
                    per = 8 // chunks
                    rounds.append([(at + j, per * j, per, chunks) for j in range(heads // per)])
                    at += heads // per

                def rows_of(buf, k):
                    return buf[:, 0:k["rows"] * k["keys"]].rearrange("p (r l) -> p r l", r=k["rows"])

                with nc.Block() as block:
                    @block.tensor
                    def _(pe):
                        def score(b):
                            k = blocks[b]
                            wait(pe, scores_out.sem, scores_out.at(b) if b else 0)
                            out = rows_of(scores, k)
                            for row in range(k["rows"]):
                                mm = k["score"](pe, row, out[:, row])
                            mm.then_inc(scores_in.sem, 1)

                        def mix_values(b):
                            k = blocks[b]
                            w = rows_of(e[:, b % 2], k)
                            pe.wait_ge(weights_in.sem, weights_in.at(b + 1))
                            for n, h0, per, chunks in rounds[b]:
                                wait(pe, w_copied.sem, w_copied.at(n) if n else 0)
                                for j in range(per):
                                    for c in range(chunks):
                                        m = j * chunks + c
                                        tr = pe.transpose(banks[:, 4 + m // 4, P * (m % 4):P * (m % 4) + P],
                                                          w[:, h0 + j, T * c:T * c + T], ident)
                                tr.then_inc(w_turned.sem, 1)
                                pe.wait_ge(w_copied.sem, w_copied.at(n + 1))
                                wait(pe, mixed_out.sem, mixed_out.at(n) if n else 0)
                                for j in range(per):
                                    for c in range(chunks):
                                        mm = pe.matmul(banks[:, 6 + j // 4, P * (j % 4):P * (j % 4) + P],
                                                       k["value"](h0 + j, c), wt[:, n % 2, j * chunks + c],
                                                       start=c == 0, stop=c == chunks - 1)
                                mm.then_inc(mixed.sem, 1)
                        score(0)
                        for b in range(len(blocks)):
                            if b + 1 < len(blocks):
                                score(b + 1)
                            mix_values(b)

                    @block.vector
                    def _(dve):
                        def prepare(b):
                            k = blocks[b]
                            s, w = rows_of(scores, k), rows_of(e[:, b % 2], k)
                            dve.wait_ge(scores_in.sem, scores_in.at(b + 1))
                            top = mx[:, b % 2, 0:k["rows"]]
                            dve.tensor_reduce(top, s, X_AXIS, ALU.max).then_inc(row_max.sem, 1)
                            dve.wait_ge(row_max.sem, row_max.at(b + 1))
                            if b >= 2:
                                dve.wait_ge(w_turned.sem, w_turned.at(rounds[b - 2][-1][0] + 1))
                            dve.tensor_tensor(w, s, over(top, k["keys"]), ALU.subtract).then_inc(scores_out.sem, 1)

                        def normalise(b):
                            k = blocks[b]
                            w = rows_of(e[:, b % 2], k)
                            r = inv[:, b % 2, 0:k["rows"]]
                            dve.wait_ge(exped.sem, exped.at(b + 1))
                            dve.tensor_reduce(r, w, X_AXIS, ALU.add).then_inc(row_sum.sem, 1)
                            dve.wait_ge(row_sum.sem, row_sum.at(b + 1))
                            dve.reciprocal(r, r).then_inc(row_inv.sem, 1)
                            dve.wait_ge(row_inv.sem, row_inv.at(b + 1))
                            if k["diff"]:
                                second = r[:, k["rows"] // 2:]
                                dve.tensor_scalar(second, second, lam[:], -1.0, ALU.mult, ALU.mult
                                                  ).then_inc(inv_signed.sem, 1)
                                dve.wait_ge(inv_signed.sem, inv_signed.at(b + 1))
                                dve.tensor_tensor(w, w, over(r, k["keys"]), ALU.mult).then_inc(scaled.sem, 1)
                                dve.wait_ge(scaled.sem, scaled.at(b + 1))
                                w1, w2 = w[:, 0:k["rows"] // 2], w[:, k["rows"] // 2:]
                                dve.tensor_tensor(w1, w1, w2, ALU.add).then_inc(weights_in.sem, 1)
                            else:
                                dve.tensor_tensor(w, w, over(r, k["keys"]), ALU.mult).then_inc(weights_in.sem, 1)
                        prepare(0)
                        for b in range(len(blocks)):
                            if b + 1 < len(blocks):
                                prepare(b + 1)
                            normalise(b)

                    @block.scalar
                    def _(act):
                        def exponentials(b):
                            k = blocks[b]
                            w = rows_of(e[:, b % 2], k)
                            act.wait_ge(scores_out.sem, scores_out.at(b + 1))
                            act.activation(w, w, ACT.Exp, scale=k["scale"]).then_inc(exped.sem, 1)

                        def carry(b):
                            for n, h0, per, chunks in rounds[b]:
                                act.wait_ge(w_turned.sem, w_turned.at(n + 1))
                                if n >= 2:
                                    act.wait_ge(mixed.sem, mixed.at(n - 1))
                                act.activation(wt[:, n % 2], banks[:, 4:6].rearrange("p b (n t) -> p (b n) t", t=P),
                                               ACT.Copy).then_inc(w_copied.sem, 1)
                                act.wait_ge(mixed.sem, mixed.at(n + 1))
                                out = banks[:, 6:8].rearrange("p b (n t) -> p (b n) t", t=P)
                                act.activation(blocks[b]["dst"](h0, per), out[:, 0:per], ACT.Copy
                                               ).then_inc(mixed_out.sem, 1)
                        exponentials(0)
                        for b in range(len(blocks)):
                            if b + 1 < len(blocks):
                                exponentials(b + 1)
                            carry(b)
                diffs = sum(k["diff"] for k in blocks)
                assert all(k["diff"] for k in blocks[:diffs])
                for t in (scores_in, scores_out, row_max, exped, row_sum, row_inv, weights_in):
                    t.advance(len(blocks))
                for t in (inv_signed, scaled):
                    t.advance(diffs)
                for t in (w_turned, w_copied, mixed, mixed_out):
                    t.advance(at)

        def even_layer(l):
            with ExitStack() as outer:
                mix = sb("mix0", [P, 2 * HEADS, NT], scope=outer)
                with ExitStack() as scope:
                    qkv = sb("qkv", [P, EVEN_TILES, NT], scope=scope)
                    with ExitStack() as inner:
                        xs = sb("xs_even", [P, KD, 2 * NT], F32R, inner)
                        norm_of(l, 0, xs)
                        tb = sb("tb_even", [P, GROUP, NT], scope=inner)
                        a, b = ph["even_in"], ph["even_in_end"]
                        project([a, b], lambda s, k: xs[:, CHUNKS * k:CHUNKS * k + CHUNKS],
                                [[copy_part(tb)], [copy_part(tb)]],
                                [[add_parts(tb, qkv)], [add_parts(tb, qkv, GROUP * a.iters * a.groups)]])
                        resid_skip[0] += EVEN_TILES // GROUP
                    QA, KA, VA, QB, KB, VB = 0, 8, 16, 24, 32, 34
                    kv_cache = sb("kv_cache", [P, 2, 10, P], scope=scope)
                    turned = sb("turned0", [P, 40, P], scope=scope)
                    with nc.Block() as block:
                        @block.sync
                        def _(sp):
                            for c in range(2):
                                sp.dma_start(kv_cache[:, 0, 0:HEADS].rearrange("t h (c d) -> t h c d", c=2)[:, :, c],
                                             ins["cache_da_k"][0, 0, :, c].rearrange("h t d -> t h d")
                                             ).then_inc(small_in.sem, 16)
                            sp.dma_start(kv_cache[:, 1, 0:HEADS], ins["cache_da_v"][0, 0].rearrange("h t d -> t h d")
                                         ).then_inc(small_in.sem, 16)
                            for n, name in enumerate(("cache_gq_k", "cache_gq_v")):
                                sp.dma_start(kv_cache[:, n, HEADS:10], ins[name][0, 0].rearrange("h t d -> t h d")
                                             ).then_inc(small_in.sem, 16)
                            sp.wait_ge(small_in.sem, small_in.at(80))
                    small_in.advance(80)
                    with ExitStack() as inner:
                        work = sb("work0", [P, 10, NT], scope=inner)
                        feature_rms(qkv[:, QB:KB + KV_HEADS], work,
                                    [(slice(0, HEADS), par[:, PCOL["gq_q_norm_g"]:PCOL["gq_q_norm_g"] + 1], 1.0),
                                     (slice(HEADS, HEADS + KV_HEADS),
                                      par[:, PCOL["gq_k_norm_g"]:PCOL["gq_k_norm_g"] + 1], 1.0)])
                        rotate(qkv[:, 0:2 * HEADS, T:NT], C_ROT_SUB, C_COS_SUB, C_SIN_SUB, work)
                        rotate(qkv[:, QB:KB + KV_HEADS, T:NT], C_ROT_HD, C_COS_HD, C_SIN_HD, work)
                    prompt = [qkv[:, t, 0:T] for t in (*range(KA, KA + 8), *range(VA, VA + 8), 32, 33, 34, 35)]
                    sample = [qkv[:, t, T:NT] for t in (*range(VA, VA + 8), 34, 35)]
                    turn_tiles(prompt + sample + [kv_cache[:, 0, h] for h in range(10)], turned)
                    KA_P, VA_P, KB_P, VB_P, VA_S, VB_S, K_CACHE = 0, 8, 16, 18, 20, 28, 30
                    with nc.Block() as block:
                        @block.sync
                        def _(sp):
                            for c in range(2):
                                sp.dma_start(outs["new_da_k"][0, 0, :, c].rearrange("h t d -> t h d"),
                                             turned[:, KA_P:KA_P + 8].rearrange("t h (c d) -> t h c d", c=2)[:, :, c]
                                             ).then_inc(stored.sem, 16)
                            for name, t0, n in (("new_da_v", VA_P, 8), ("new_gq_k", KB_P, 2), ("new_gq_v", VB_P, 2)):
                                sp.dma_start(outs[name][0, 0].rearrange("h t d -> t h d"), turned[:, t0:t0 + n]
                                             ).then_inc(stored.sem, 16)
                    stored.advance(80)

                    def sub(c):
                        return slice(SUB * c, SUB * c + SUB)

                    def da_prompt(pe, row, out):
                        c, h = divmod(row, HEADS)
                        return pe.matmul(out, qkv[sub(c), QA + h, 0:T], qkv[sub(c), KA + h, 0:T], start=True, stop=True)

                    def da_sample(h0):
                        def score(pe, row, out):
                            c, h = row // 4, h0 + row % 4
                            q = qkv[sub(c), QA + h, T:NT]
                            pe.matmul(out[:, 0:T], q, turned[sub(c), K_CACHE + h], start=True, stop=True)
                            return pe.matmul(out[:, T:2 * T], q, qkv[sub(c), KA + h, T:NT], start=True, stop=True)
                        return score

                    def gq_prompt(pe, row, out):
                        return pe.matmul(out, qkv[:, QB + row, 0:T], qkv[:, KB + row // 4, 0:T], start=True, stop=True)

                    def gq_sample(pe, row, out):
                        g = row // 4
                        pe.matmul(out[:, 0:T], qkv[:, QB + row, T:NT], turned[:, K_CACHE + 8 + g], start=True, stop=True)
                        return pe.matmul(out[:, T:2 * T], qkv[:, QB + row, T:NT], qkv[:, KB + g, T:NT],
                                         start=True, stop=True)

                    def dst(first, stream):
                        return lambda h0, n: mix[:, first + h0:first + h0 + n, T * stream:T * stream + T]

                    def cached(v_cache, v_own, share=1):
                        return lambda h, c: kv_cache[:, 1, v_cache + h // share] if c == 0 else turned[:, v_own + h // share]

                    da = dict(diff=True, scale=SUB ** -0.5)
                    gq = dict(diff=False, scale=P ** -0.5)
                    attention([
                        dict(da, rows=16, keys=T, score=da_prompt, dst=dst(0, 0), value=lambda h, c: turned[:, VA_P + h]),
                        dict(da, rows=8, keys=2 * T, score=da_sample(0), dst=dst(0, 1), value=cached(0, VA_S)),
                        dict(da, rows=8, keys=2 * T, score=da_sample(4), dst=dst(4, 1), value=lambda h, c: cached(4, VA_S + 4)(h, c)),
                        dict(gq, rows=8, keys=T, score=gq_prompt, dst=dst(8, 0), value=lambda h, c: turned[:, VB_P + h // 4]),
                        dict(gq, rows=8, keys=2 * T, score=gq_sample, dst=dst(8, 1), value=cached(8, VB_S, 4)),
                    ], "even")
                    with ExitStack() as inner:
                        work = sb("work1", [P, HEADS, NT], scope=inner)
                        feature_rms(mix[:, 0:HEADS], work,
                                    [(slice(0, HEADS), par[:, PCOL["da_subln_g"]:PCOL["da_subln_g"] + 1], 1.0 - LAM_INIT)])
                out_projection(l, mix)
            ffn(l)

        VM, OM, QD, KV, PE_T = 0, 8, 16, 20, 22

        def mlstm(kq, prj, gates, mix):
            R = 2 * HEADS
            NEG_M, Z, A_, EM, WG = range(5)
            with ExitStack() as scope:
                ee = sb("ee", [P, 4 * HEADS, T], scope=scope)
                va = sb("va", [P, R, P + 1], scope=scope)
                c0 = sb("c0", [P, R, P + 1], scope=scope)
                k_tok = sb("k_tok", [P, HEADS, P], scope=scope)
                qa = sb("qa", [P, R, T], scope=scope)
                sc = sb("sc", [R, 5, 2, T], scope=scope)
                turned = sb("sc_turned", [P, 4, R], scope=scope)
                den = sb("den", [P, 2, HEADS], scope=scope)
                state_n = sb("state_n", [R, 1, P], scope=scope)
                hbuf = mix[:, HEADS:2 * HEADS].rearrange("p a (b t) -> p (a b) t", t=T)

                def ordered(kind, d):
                    return sc[:, kind, d, :] if d == 0 else sc[:, kind, d, ::-1]

                with ExitStack() as inner:
                    gs, ex, lf, bs = (qa[0:R, a:b] for a, b in ((0, 4), (4, 6), (6, 8), (8, 10)))
                    zz = sb("zz", [R, 2, T], scope=inner)
                    mm_ = sb("mm", [R, 2, T], scope=inner)
                    ms = sb("ms", [R, 2, T], scope=inner)
                    zero = sb("zero", [R, T], scope=inner)
                    n_end = sb("n_end", [R, 2], scope=inner)
                    f_rows = gs.rearrange("r (d k) t -> r d k t", k=2)[:, :, 1]
                    i_rows = gs.rearrange("r (d k) t -> r d k t", k=2)[:, :, 0]
                    with nc.Block() as block:
                        @block.sync
                        def _(sp):
                            for d in range(2):
                                sp.dma_start(c0[:, HEADS * d:HEADS * d + HEADS, 0:P],
                                             ins["state_ml_C"][0, 0, d].rearrange("h k v -> k h v")
                                             ).then_inc(small_in.sem, 16)
                            sp.wait_ge(V.sem, V.at(9))
                            sp.dma_start(outs["new_ml_m"][0, 0].rearrange("d h -> h d"), ms[0:HEADS, :, T - 1],
                                         allow_slow_non_contiguous=True).then_inc(stored.sem, 16)
                            sp.wait_ge(stored.sem, stored.at(16))

                        @block.gpsimd
                        def _(pool):
                            pool.memset(zero[:], 0.0).then_inc(pool_step.sem, 1)
                            pool.memset(va[:, :, P:P + 1], 1.0)

                        @block.vector
                        def _(dve):
                            dve.tensor_scalar(gates[:], gates[:], gate_b[:], None, ALU.add).then_inc(V.sem, 1)
                            dve.tensor_scalar(kq[:, 0:HEADS], kq[:, 0:HEADS], P ** -0.5, None, ALU.mult)
                            dve.tensor_copy(c0[:, :, P:P + 1],
                                            par[:, PCOL["state_ml_n"]:PCOL["state_ml_n"] + R].unsqueeze(2))
                            dve.wait_ge(E.sem, E.at(1))
                            dve.tensor_copy(gs, banks[0:R, 0, :].rearrange("r (k t) -> r k t", k=4)
                                            ).then_inc(V.sem, 1)
                            dve.wait_ge(V.sem, V.at(2))
                            dve.scalar_tensor_tensor(ex, f_rows, -1.0, f_rows, ALU.mult, ALU.min
                                                     ).then_inc(V.sem, 1)
                            dve.tensor_scalar(lf, f_rows, 0.0, None, ALU.min).then_inc(V.sem, 1)
                            dve.wait_ge(A.sem, A.at(2))
                            dve.wait_ge(V.sem, V.at(4))
                            dve.tensor_tensor(lf, lf, ex, ALU.subtract).then_inc(V.sem, 1)
                            dve.wait_ge(V.sem, V.at(5))
                            dve.wait_ge(pool_step.sem, pool_step.at(1))
                            for d in range(2):
                                sn = dve.tensor_tensor_scan(bs[:, d], lf[:, d], zero[:], 0.0, ALU.add, ALU.add)
                            sn.then_inc(V.sem, 1)
                            dve.wait_ge(V.sem, V.at(6))
                            dve.tensor_tensor(zz[:], i_rows, bs, ALU.subtract).then_inc(V.sem, 1)
                            dve.wait_ge(V.sem, V.at(7))
                            for d in range(2):
                                sn = dve.tensor_tensor_scan(mm_[:, d], zz[:, d], zz[:, d], m0[:, d:d + 1],
                                                            ALU.max, ALU.max)
                            sn.then_inc(V.sem, 1)
                            dve.wait_ge(V.sem, V.at(8))
                            dve.tensor_tensor(ms[:], bs, mm_[:], ALU.add).then_inc(V.sem, 1)
                            dve.tensor_scalar(n_end[:].unsqueeze(2), mm_[:, :, T - 1:T], -1.0, None, ALU.mult
                                              ).then_inc(V.sem, 1)
                            for d in range(2):
                                dve.tensor_scalar(ordered(NEG_M, d), mm_[:, d], -1.0, None, ALU.mult)
                                dve.tensor_copy(ordered(Z, d), zz[:, d])

                        @block.scalar
                        def _(act):
                            act.wait_ge(V.sem, V.at(3))
                            act.activation(ex, ex, ACT.Exp).then_inc(A.sem, 1)
                            act.wait_ge(A.sem, A.at(1))
                            act.activation(ex, ex, ACT.Ln, bias=1.0).then_inc(A.sem, 1)
                            act.wait_ge(V.sem, V.at(10))
                            for d in range(2):
                                act.activation(ordered(A_, d), mm_[:, d], ACT.Exp, bias=m0[:, d:d + 1], scale=-1.0)
                                act.activation(ordered(EM, d), ms[:, d], ACT.Exp, scale=-1.0)
                                act.activation(ordered(WG, d), zz[:, d], ACT.Exp, bias=n_end[:, d:d + 1])

                        @block.tensor
                        def _(pe):
                            pe.wait_ge(V.sem, V.at(1))
                            for d in range(2):
                                for kind in range(2):
                                    for s in range(2):
                                        tok = gates[:, T * s:T * s + T]
                                        col = C_SEL + 16 * (4 * d + 2 * kind + s)
                                        mm = pe.matmul(banks[0:R, 0, T * (2 * d + kind):T * (2 * d + kind) + T],
                                                       const[0:4 * HEADS, col:col + R], tok if d == 0 else tok[:, ::-1],
                                                       start=s == 0, stop=s == 1)
                            mm.then_inc(E.sem, 1)
                    V.advance(10)
                    A.advance(2)
                    E.advance(1)
                    pool_step.advance(1)
                    stored.advance(16)
                turn_tiles([prj[:, VM + h, T * s:T * s + T] for s in range(2) for h in range(HEADS)], va[:])
                turn_tiles([kq[:, HEADS + h, 0:T] for h in range(HEADS)], k_tok[:])
                turn_tiles([sc[:, kind, d, :] for kind in (EM, WG) for d in range(2)], turned[:])

                def row(n):
                    return const[0:R, C_IDENT + n:C_IDENT + n + 1].broadcast_to([R, P])
                with nc.Block() as block:
                    @block.sync
                    def _(sp):
                        sp.wait_ge(small_in.sem, small_in.at(32))

                    @block.tensor
                    def _(pe):
                        for j in range(8):
                            d = j // 4
                            pe.matmul(banks[:, j, :], ident, const[:, C_MASK + T * d:C_MASK + T * d + T]
                                      .unsqueeze(1).broadcast_to([P, 4, T]), start=True, stop=False)
                            for m in range(4):
                                n = (4 * j + m) % R
                                out = banks[:, j, T * m:T * m + T]
                                pe.matmul(out, row(n), sc[:, NEG_M, d, :], start=False, stop=False)
                                mm = pe.matmul(out, sc[:, Z, d, :], row(n), start=False, stop=m == 3)
                            mm.then_inc(E.sem, 1)
                        for b in range(4):
                            pe.wait_ge(A.sem, A.at(b + 1))
                            for m in range(4):
                                s, h = divmod(4 * b + m, HEADS)
                                mm = pe.matmul(banks[:, b, T * m:T * m + T], kq[:, HEADS + h, T * s:T * s + T],
                                               kq[:, h, T * s:T * s + T], start=True, stop=True)
                        mm.then_inc(E.sem, 1)
                        for b in range(4):
                            pe.wait_ge(A.sem, A.at(b + 5))
                            for m in range(4):
                                d, h = divmod(4 * b + m, HEADS)
                                mm = pe.matmul(banks[:, 4 + b, T * m:T * m + T], row(HEADS + h), sc[:, A_, d, :],
                                               start=True, stop=True)
                        mm.then_inc(E.sem, 1)

                    @block.scalar
                    def _(act):
                        for j in range(8):
                            act.wait_ge(E.sem, E.at(1 + j))
                            act.activation(ee[:, 4 * j:4 * j + 4], banks[:, j, :].rearrange("p (m t) -> p m t", m=4),
                                           ACT.Exp).then_inc(A.sem, 1)

                    @block.vector
                    def _(dve):
                        dve.wait_ge(E.sem, E.at(9))
                        dve.wait_ge(A.sem, A.at(8))
                        for d in range(2):
                            part = ee[:, R * d:R * d + R]
                            dve.tensor_tensor(part, banks[:, 0:4].rearrange("p b (m t) -> p (b m) t", t=T), part, ALU.mult)
                        dve.wait_ge(E.sem, E.at(10))
                        for d in range(2):
                            dve.tensor_tensor(qa[:, HEADS * d:HEADS * d + HEADS],
                                              banks[:, 4 + 2 * d:6 + 2 * d].rearrange("p b (m t) -> p (b m) t", t=T),
                                              kq[:, 0:HEADS, T:NT], ALU.mult)
                small_in.advance(32)
                E.advance(10)
                A.advance(8)

                def pair_banks(n):
                    return banks[:, 4 * (n % 2):4 * (n % 2) + 4].rearrange("p b (j w) -> p (b j) w", j=2)
                with nc.Block() as block:
                    @block.tensor
                    def _(pe):
                        for n in range(4):
                            d, s = divmod(n, 2)
                            wait(pe, V.sem, V.at(3 * (n - 2) + 3) if n >= 2 else 0)
                            for h in range(HEADS):
                                out = pair_banks(n)[:, h, 0:P + 1]
                                mm = pe.matmul(out, ee[:, R * d + HEADS * s + h], va[:, HEADS * s + h],
                                               start=True, stop=s == 0)
                                if s == 1:
                                    mm = pe.matmul(out, qa[:, HEADS * d + h], c0[:, HEADS * d + h],
                                                   start=False, stop=True)
                            mm.then_inc(E.sem, 1)

                    @block.scalar
                    def _(act):
                        for n in range(4):
                            act.wait_ge(E.sem, E.at(n + 1))
                            if n >= 2:
                                act.wait_ge(V.sem, V.at(3 * (n - 2) + 3))
                            act.activation(den[:, n % 2].unsqueeze(2), pair_banks(n)[:, :, P:P + 1], ACT.Abs
                                           ).then_inc(A.sem, 1)

                    @block.vector
                    def _(dve):
                        for n in range(4):
                            d, s = divmod(n, 2)
                            dn = den[:, n % 2]
                            dve.wait_ge(A.sem, A.at(n + 1))
                            dve.tensor_tensor(dn, dn, turned[:, d, HEADS * s:HEADS * s + HEADS], ALU.max
                                              ).then_inc(V.sem, 1)
                            dve.wait_ge(V.sem, V.at(3 * n + 1))
                            dve.reciprocal(dn, dn).then_inc(V.sem, 1)
                            dve.wait_ge(V.sem, V.at(3 * n + 2))
                            hs = hbuf[:, HEADS * s:HEADS * s + HEADS]
                            dst = hs if d == 0 else ee[:, HEADS * s:HEADS * s + HEADS]
                            dve.tensor_tensor(dst, pair_banks(n)[:, :, 0:P], over(dn, P), ALU.mult
                                              ).then_inc(V.sem, 1)
                        for s in range(2):
                            dve.wait_ge(V.sem, V.at(9 + 3 * s))
                            hs = hbuf[:, HEADS * s:HEADS * s + HEADS]
                            dve.tensor_tensor(hs, hs, ee[:, HEADS * s:HEADS * s + HEADS], ALU.add)
                V.advance(12)
                A.advance(4)
                E.advance(4)

                kw = ee[:, 0:R]
                new_c = c0
                with nc.Block() as block:
                    @block.vector
                    def _(dve):
                        for d in range(2):
                            dve.tensor_tensor(kw[:, HEADS * d:HEADS * d + HEADS], k_tok[:],
                                              over(turned[:, 2 + d, 0:HEADS], P), ALU.mult).then_inc(V.sem, 1)
                        for d in range(2):
                            dve.wait_ge(E.sem, E.at(d + 1))
                            dve.tensor_copy(new_c[:, HEADS * d:HEADS * d + HEADS], pair_banks(d)[:, :, 0:P + 1]
                                            ).then_inc(V.sem, 1)
                        dve.wait_ge(A.sem, A.at(1))
                        r = den[:].rearrange("p a b -> p (a b)")
                        dve.tensor_reduce(r, qa[:], X_AXIS, ALU.add).then_inc(V.sem, 1)
                        dve.wait_ge(V.sem, V.at(5))
                        dve.tensor_scalar(r, r, 1.0 / P, EPS, ALU.mult, ALU.add).then_inc(V.sem, 1)
                        dve.wait_ge(A.sem, A.at(2))
                        dve.reciprocal(r, r).then_inc(V.sem, 1)
                        dve.wait_ge(V.sem, V.at(7))
                        dve.tensor_tensor(hbuf, hbuf, over(r, P), ALU.mult).then_inc(V.sem, 1)
                        for b in range(4):
                            dve.wait_ge(E.sem, E.at(3 + b))
                            s, h = divmod(4 * b, HEADS)
                            dve.scalar_tensor_tensor(
                                mix[:, h:h + 4, T * s:T * s + T], banks[:, b, :].rearrange("p (n t) -> p n t", t=T),
                                par[:, PCOL["ml_norm_g"]:PCOL["ml_norm_g"] + 1], prj[:, OM + h:OM + h + 4, T * s:T * s + T],
                                ALU.mult, ALU.mult)

                    @block.scalar
                    def _(act):
                        act.activation(qa[:], hbuf, ACT.Square).then_inc(A.sem, 1)
                        act.wait_ge(V.sem, V.at(6))
                        r = den[:].rearrange("p a b -> p (a b)")
                        act.activation(r, r, ACT.Sqrt).then_inc(A.sem, 1)
                        act.activation(prj[:, OM:OM + HEADS], prj[:, OM:OM + HEADS], ACT.Sigmoid).then_inc(A.sem, 1)

                    @block.tensor
                    def _(pe):
                        for d in range(2):
                            pe.wait_ge(V.sem, V.at(d + 1))
                            for h in range(HEADS):
                                mm = pe.matmul(pair_banks(d)[:, h, 0:P + 1], kw[:, HEADS * d + h], va[:, h],
                                               start=True, stop=True)
                            mm.then_inc(E.sem, 1)
                        pe.wait_ge(V.sem, V.at(8))
                        pe.wait_ge(A.sem, A.at(3))
                        for b in range(4):
                            for m in range(4):
                                tr = pe.transpose(banks[:, b, P * m:P * m + P], hbuf[:, 4 * b + m], ident)
                            tr.then_inc(E.sem, 1)
                V.advance(8)
                A.advance(3)
                E.advance(6)
                turn_tiles([new_c[:, :, P]], state_n[:])
                with nc.Block() as block:
                    @block.sync
                    def _(sp):
                        for d in range(2):
                            sp.dma_start(outs["new_ml_C"][0, 0, d].rearrange("h k v -> k h v"),
                                         new_c[:, HEADS * d:HEADS * d + HEADS, 0:P]).then_inc(stored.sem, 16)
                        sp.dma_start(outs["new_ml_n"][0, 0].rearrange("d h k -> (d h) k"), state_n[:, 0]
                                     ).then_inc(stored.sem, 16)
                        sp.wait_ge(stored.sem, stored.at(48))
                stored.advance(48)

        def latent_attention(prj, mix):
            KEYS = 3 * T
            with ExitStack() as scope:
                qn = sb("qn", [P, HEADS, NT], scope=scope)
                qp = sb("qp", [SUB, HEADS, NT], scope=scope)
                kn = sb("kn", [P, HEADS, KEYS], scope=scope)
                vt = sb("vt", [P, 3, HEADS, P], scope=scope)
                kp = sb("kp", [SUB, KEYS], scope=scope)
                with ExitStack() as inner:
                    work = sb("work2", [P, 4, NT], scope=inner)
                    cached = sb("cached", [P, 2, P], scope=inner)
                    cached_kpe = sb("cached_kpe", [P, SUB], scope=inner)
                    turned = sb("turned1", [P, 4, P], scope=inner)
                    kpe_turned = sb("kpe_turned", [SUB, 1, P], scope=inner)
                    kpe_tok = sb("kpe_tok", [P, 1, SUB], scope=inner)
                    cq = sb("cq", [P, Q_RANK // P, 2 * NT], F32R, inner)
                    ckv_hi = sb("ckv_hi", [P, 2, KEYS], F32R, inner)
                    ckv_lo = sb("ckv_lo", [P, 2, KEYS], F32R, inner)
                    tb = sb("tb_uq", [P, 4, NT], scope=inner)
                    with nc.Block() as block:
                        @block.sync
                        def _(sp):
                            sp.dma_start(cached[:, 0:2].rearrange("t a b -> t (a b)"), ins["cache_mla_ckv"][0, 0]
                                         ).then_inc(small_in.sem, 16)
                            sp.dma_start(cached_kpe[:], ins["cache_mla_kpe"][0, 0]).then_inc(small_in.sem, 16)
                            sp.wait_ge(small_in.sem, small_in.at(32))
                    small_in.advance(32)
                    for first, n, name in ((QD, 4, "mla_q_norm_g"), (KV, 2, "mla_kv_norm_g")):
                        feature_rms(prj[:, first:first + n], work,
                                    [(slice(k, k + 1), par[:, PCOL[name] + k:PCOL[name] + k + 1], 1.0)
                                     for k in range(n)], together=True)
                    turn_tiles([prj[:, KV, 0:T], prj[:, KV + 1, 0:T], cached[:, 0], cached[:, 1]],
                               turned[:])
                    turn_tiles([cached_kpe[:]], kpe_turned[:])
                    turn_tiles([prj[0:SUB, PE_T, 0:T]], kpe_tok[:])
                    rotate(prj[0:SUB, PE_T:PE_T + 1, T:NT], C_ROT_SUB, C_COS_SUB, C_SIN_SUB, work)
                    with nc.Block() as block:
                        @block.sync
                        def _(sp):
                            sp.dma_start(outs["new_mla_ckv"][0, 0], turned[:, 0:2].rearrange("t a b -> t (a b)")
                                         ).then_inc(stored.sem, 16)
                            sp.dma_start(outs["new_mla_kpe"][0, 0], kpe_tok[:, 0]).then_inc(stored.sem, 16)
                            sp.wait_ge(stored.sem, stored.at(32))

                        @block.scalar
                        def _(act):
                            act.activation(cq[:, :, 0:NT], prj[:, QD:QD + 4], ACT.Copy).then_inc(A.sem, 1)
                            act.activation(ckv_hi[:, :, 0:NT], prj[:, KV:KV + 2], ACT.Copy).then_inc(A.sem, 1)
                            act.activation(ckv_hi[:, :, NT:KEYS], turned[:, 2:4], ACT.Copy).then_inc(A.sem, 1)

                        @block.vector
                        def _(dve):
                            dve.tensor_copy(kp[:, 0:NT], prj[0:SUB, PE_T])
                            dve.tensor_copy(kp[:, NT:KEYS], kpe_turned[:, 0])
                            dve.wait_ge(A.sem, A.at(3))
                            dve.tensor_tensor(cq[:, :, NT:2 * NT], prj[:, QD:QD + 4], cq[:, :, 0:NT].bitcast(F32),
                                              ALU.subtract)
                            dve.tensor_tensor(ckv_lo[:, :, 0:NT], prj[:, KV:KV + 2], ckv_hi[:, :, 0:NT].bitcast(F32),
                                              ALU.subtract)
                            dve.tensor_tensor(ckv_lo[:, :, NT:KEYS], turned[:, 2:4],
                                              ckv_hi[:, :, NT:KEYS].bitcast(F32), ALU.subtract)
                    A.advance(3)
                    stored.advance(32)

                    def uq_products(pe, f, i, s, g, k):
                        def tile(half, c, t):
                            first = (NOPE + SUB) * (t % 2) + (0 if t < 2 else NOPE)
                            return half[:, s % SPLIT, c, first:first + (NOPE if t < 2 else SUB)]
                        for c in range(CHUNKS):
                            n = CHUNKS * k + c
                            for t in range(4):
                                bank = banks[0:NOPE if t < 2 else SUB, GROUP * (g % 2) + t]
                                pe.matmul(bank, tile(w_hi, c, t), cq[:, n], start=n == 0, stop=False)
                                mm = pe.matmul(bank[:, 0:NT], tile(w_lo, c, t), cq[:, n, 0:NT], start=False,
                                               stop=n == Q_RANK // P - 1)
                        return mm

                    def uq_copy(act, f, i, g):
                        act.wait_ge(slab_used.sem, group_used(f, i, g))
                        wait(act, summed.sem, f.group(i, g))
                        b = GROUP * (g % 2)
                        act.activation(tb[0:SUB, 2:4], banks[0:SUB, b + 2:b + 4, NT:2 * NT], ACT.Copy)
                        act.activation(tb[:, 0:2], banks[:, b:b + 2, NT:2 * NT], ACT.Copy).then_inc(part_copied.sem, 1)

                    def uq_add(dve, f, i, g):
                        dve.wait_ge(part_copied.sem, f.group(i, g) + 1)
                        b = GROUP * (g % 2)
                        dve.tensor_tensor(qp[:, 2 * g:2 * g + 2], banks[0:SUB, b + 2:b + 4, 0:NT], tb[0:SUB, 2:4], ALU.add)
                        dve.tensor_tensor(qn[:, 2 * g:2 * g + 2], banks[:, b:b + 2, 0:NT], tb[:, 0:2], ALU.add
                                          ).then_inc(summed.sem, 1)

                    def ukv_products(pe, f, i, s, g, k):
                        if k == 0:
                            wait(pe, summed.sem, f.group(i, g))
                        hi2, lo2 = (w[:, s % SPLIT].rearrange("p c (h n) -> p c h n", h=2) for w in (w_hi, w_lo))
                        for c in range(2):
                            for h in range(2):
                                for n, (w, a) in enumerate(((hi2, ckv_hi), (hi2, ckv_lo), (lo2, ckv_hi))):
                                    pe.matmul(banks[:, 2 * k + h, 0:KEYS], w[:, c, h, 0:NOPE], a[:, c, :],
                                              start=c == 0 and n == 0, stop=c == 1 and n == 2)
                        for t in range(3):
                            for c in range(2):
                                for n, (w, a) in enumerate(((hi2, ckv_hi), (hi2, ckv_lo), (lo2, ckv_hi))):
                                    mm = pe.matmul(banks[:, 4 + t, 2 * P * k:2 * P * k + 2 * P], a[:, c, T * t:T * t + T],
                                                   w[:, c, :, NOPE:NOPE + P],
                                                   start=c == 0 and n == 0, stop=c == 1 and n == 2)
                        return mm

                    def ukv_keys(act, f, i, g):
                        act.wait_ge(slab_used.sem, group_used(f, i, g))
                        act.activation(kn[:, 4 * g:4 * g + 4], banks[:, 0:4, 0:KEYS], ACT.Copy).then_inc(part_copied.sem, 1)

                    def ukv_values(dve, f, i, g):
                        dve.wait_ge(part_copied.sem, f.group(i, g) + 1)
                        dve.tensor_copy(vt[:, :, 4 * g:4 * g + 4], banks[:, 4:7, :].rearrange("p t (h n) -> p t h n", h=4)
                                        ).then_inc(summed.sem, 1)

                    project([ph["uq"], ph["ukv"]], None, [[uq_copy], [ukv_keys]], [[uq_add], [ukv_values]],
                            products=[uq_products, ukv_products])
                    resid_skip[0] += 6
                    rotate(qp[:, :, T:NT], C_ROT_SUB, C_COS_SUB, C_SIN_SUB, work)

                def score(stream):
                    cols = slice(0, T) if stream == 0 else slice(T, KEYS)

                    def one(pe, h, out):
                        tok = slice(T * stream, T * stream + T)
                        pe.matmul(out, qn[:, h, tok], kn[:, h, cols], start=True, stop=False)
                        return pe.matmul(out, qp[:, h, tok], kp[:, cols], start=False, stop=True)
                    return one

                common = dict(diff=False, rows=HEADS, scale=(NOPE + SUB) ** -0.5)
                attention([
                    dict(common, keys=T, score=score(0), value=lambda h, c: vt[:, 0, h],
                         dst=lambda h0, n: mix[:, HEADS + h0:HEADS + h0 + n, 0:T]),
                    dict(common, keys=2 * T, score=score(1), value=lambda h, c: vt[:, 1 + c, h],
                         dst=lambda h0, n: mix[:, HEADS + h0:HEADS + h0 + n, T:NT]),
                ], "odd")

        def odd_layer(l):
            with ExitStack() as outer:
                mix = sb("mix1", [P, 2 * HEADS, NT], scope=outer)
                with ExitStack() as scope:
                    prj = sb("prj", [P, 23, NT], scope=scope)
                    gates = sb("gates", [4 * HEADS, NT], scope=scope)
                    with ExitStack() as rec:
                        kq = sb("kq", [P, 2 * HEADS, NT], scope=rec)
                        with ExitStack() as inner:
                            xs = sb("xs_odd", [P, KD, 2 * NT], F32R, inner)
                            norm_of(l, 0, xs)
                            tb = sb("tb_odd", [P, GROUP, NT], scope=inner)
                            u = sb("u_odd", [P, GROUP, NT], scope=inner)
                            y = sb("y_odd", [P, 2, GROUP, NT], scope=inner)
                            fq = ph["odd_qk"]

                            def column(base):
                                return lambda f, i, g, t: par[:, tiles_at(base + GROUP * (i * f.groups + g) + t, 1)]

                            def weight(f, i, g, which, t):
                                return column(PCOL["ml_conv_w"] + which * 2 * HEADS)(f, i, g, t)

                            def count(f, i, g):
                                return f.group(i, g) - fq.group0

                            def y_free(act, f, i, g):
                                wait(act, silu_done.sem, silu_done.at(count(f, i, g) - 1))

                            def silu(act, f, i, g):
                                n = count(f, i, g)
                                act.wait_ge(tap[2].sem, tap[2].at(n + 1))
                                act.activation(kq[:, GROUP * n:GROUP * n + GROUP], y[:, g % 2], ACT.Silu
                                               ).then_inc(silu_done.sem, 1)

                            def tail_products(pe, f, i, s, g, k):
                                spans = ((0, 32), (32, 160), (160, 288), (288, 416)) if g == 0 else \
                                    ((0, 128), (128, 256), (256, 384), (384, 448))
                                for c in range(CHUNKS):
                                    n = CHUNKS * k + c
                                    for t, (a, b) in enumerate(spans):
                                        hi, lo = w_hi[:, s % SPLIT, c, a:b], w_lo[:, s % SPLIT, c, a:b]
                                        bank = banks[0:b - a, GROUP * (g % 2) + t]
                                        pe.matmul(bank, hi, xs[:, n], start=n == 0, stop=False)
                                        mm = pe.matmul(bank[:, 0:NT], lo, xs[:, n, 0:NT], start=False, stop=n == KD - 1)
                                return mm

                            def tail_copy(act, f, i, g):
                                act.wait_ge(slab_used.sem, group_used(f, i, g))
                                wait(act, summed.sem, f.group(i, g))
                                if g == 0:
                                    act.activation(tb[0:32, 0], banks[0:32, 0, NT:2 * NT], ACT.Copy)
                                    act.activation(tb[:, 1:4], banks[:, 1:4, NT:2 * NT], ACT.Copy).then_inc(part_copied.sem, 1)
                                else:
                                    act.activation(tb[0:SUB, 3], banks[0:SUB, 7, NT:2 * NT], ACT.Copy)
                                    act.activation(tb[:, 0:3], banks[:, 4:7, NT:2 * NT], ACT.Copy).then_inc(part_copied.sem, 1)

                            def tail_add(dve, f, i, g):
                                dve.wait_ge(part_copied.sem, f.group(i, g) + 1)
                                if g == 0:
                                    dve.tensor_tensor(gates[:], banks[0:32, 0, 0:NT], tb[0:32, 0], ALU.add)
                                    dve.tensor_tensor(prj[:, QD:QD + 3], banks[:, 1:4, 0:NT], tb[:, 1:4], ALU.add
                                                      ).then_inc(summed.sem, 1)
                                else:
                                    dve.tensor_tensor(prj[0:SUB, PE_T], banks[0:SUB, 7, 0:NT], tb[0:SUB, 3], ALU.add)
                                    dve.tensor_tensor(prj[:, QD + 3:QD + 6], banks[:, 4:7, 0:NT], tb[:, 0:3], ALU.add
                                                      ).then_inc(summed.sem, 1)

                            act_pieces, dve_pieces = convolution(tb, u, y, weight, column(PCOL["ml_conv_b"]), count,
                                                                 y_free)
                            project([fq, ph["odd_vo"], ph["odd_tail"]],
                                    lambda s, k: xs[:, CHUNKS * k:CHUNKS * k + CHUNKS],
                                    [[*act_pieces, None, None, silu], [copy_part(tb)], [tail_copy]],
                                    [dve_pieces, [add_parts(tb, prj)], [tail_add]],
                                    products=[None, None, tail_products])
                            for t in (*tap, silu_done):
                                t.advance(4)
                            resid_skip[0] += 10
                        mlstm(kq, prj, gates, mix)
                    latent_attention(prj, mix)
                out_projection(l, mix)
            ffn(l)

        even_layer(0)
        odd_layer(1)

        with ExitStack() as scope:
            work = sb("work_end", [P, KD, NT], scope=scope)
            y_tok = sb("y_tok", [P, 2 * KD, P], scope=scope)
            g0 = PCOL["final_norm_g"]
            feature_rms(x[:], work, [(slice(k, k + 1), par[:, g0 + k:g0 + k + 1], 1.0) for k in range(KD)], together=True)
            turn_tiles([x[:, k, T * s:T * s + T] for s in range(2) for k in range(KD)], y_tok[:])
            with nc.Block() as block:
                @block.sync
                def _(sp):
                    for s, name in enumerate(("y_prompt", "y_sample")):
                        sp.dma_start(outs[name][0], y_tok[:, KD * s:KD * s + KD].rearrange("t k p -> t (k p)")
                                     ).then_inc(stored.sem, 16)
                    sp.wait_ge(stored.sem, stored.at(32))


INPUTS = ("x_prompt", "x_sample", "cache_da_k", "cache_da_v", "cache_gq_k", "cache_gq_v", "cache_mla_ckv",
          "cache_mla_kpe", "state_ml_C", "state_ml_n", "state_ml_m", "c", "c_ctx", "norm1_g", "norm2_g", "w_mod",
          "b_mod", "even_w_in", "even_w_out", "da_lambda", "da_subln_g", "gq_q_norm_g", "gq_k_norm_g", "odd_w_in",
          "odd_w_out", "ml_conv_w", "ml_conv_b", "ml_gate_b", "ml_norm_g", "mla_q_norm_g", "mla_w_uq",
          "mla_kv_norm_g", "mla_w_ukv", "ffn_w_up", "ffn_conv_w", "ffn_conv_b", "ffn_w_down", "final_norm_g")
OUTPUTS = (("y_prompt", (1, T, D)), ("y_sample", (1, T, D)), ("new_da_k", (1, 1, HEADS, 2, T, SUB)),
           ("new_da_v", (1, 1, HEADS, T, P)), ("new_gq_k", (1, 1, KV_HEADS, T, P)),
           ("new_gq_v", (1, 1, KV_HEADS, T, P)), ("new_mla_ckv", (1, 1, T, KV_RANK)),
           ("new_mla_kpe", (1, 1, T, SUB)), ("new_ml_C", (1, 1, 2, HEADS, P, P)), ("new_ml_n", (1, 1, 2, HEADS, P)),
           ("new_ml_m", (1, 1, 2, HEADS)))


def kernel(**inputs):
    import concourse.bacc as bacc
    from concourse.bass_utils import run_bass_kernel_spmd

    nc = bacc.Bacc("TRN2", target_bir_lowering=False, num_devices=1)
    arrays, ins, outs = {}, {}, {}
    given = {name: np.ascontiguousarray(inputs[name]) for name in INPUTS}
    given["constants"] = constants()
    for name, a in given.items():
        arrays[f"in_{name}"] = a
        ins[name] = nc.dram_tensor(f"in_{name}", a.shape, mybir.dt.from_np(a.dtype), kind="ExternalInput").ap()
    for name, shape in OUTPUTS:
        outs[name] = nc.dram_tensor(f"out_{name}", shape, F32, kind="ExternalOutput").ap()
    trunk(nc, ins, outs)
    r = run_bass_kernel_spmd(nc, [arrays], core_ids=[0])
    return tuple(r.results[0][f"out_{name}"] for name, _ in OUTPUTS)
```

```python
from contextlib import ExitStack

import concourse.bass as bass
import numpy as np
from concourse import mybir

F32 = mybir.dt.float32
F32R = mybir.dt.float32r
ALU = mybir.AluOpType
ACT = mybir.ActivationFunctionType
X_AXIS = mybir.AxisListType.X

P = 128
D = 2048
KD = D // P
T = 128
NT = 2 * T
DEPTH = 2
GRID_W = 64
EPS = 1e-6
HEADS = 8
KV_HEADS = 2
SUB = 64
Q_RANK, KV_RANK = 512, 256
NOPE = 128
D_FF = 5632
KF = D_FF // P
EVEN_TILES = 36
LAM_INIT = 0.8 - 0.6
MASKED = -1.0e30

RAW = 8
SPLIT = 4
CHUNKS = 2
SLABW = 512
GROUP = SLABW // P
MOD_SLABS = KD // CHUNKS
MOD_GROUPS = 6 * D // SLABW
MOD_ROWS, MOD_COLS = 4, 6

C_IDENT, C_ONES, C_ROT_SUB, C_ROT_HD = 0, 128, 256, 384
C_COS_SUB, C_SIN_SUB, C_COS_HD, C_SIN_HD = 512, 640, 768, 896
C_MASK = 1024
C_SEL = 1280
C_SUM = 1408
C_COLUMN = 1410
NCONST = 1441


def constants():
    c = np.zeros((P, NCONST), np.float32)
    c[:, C_IDENT:C_IDENT + P] = np.eye(P)
    c[:, C_ONES:C_ONES + P] = 1.0
    t = np.arange(T)
    for width, rot, cos, sin in ((SUB, C_ROT_SUB, C_COS_SUB, C_SIN_SUB), (P, C_ROT_HD, C_COS_HD, C_SIN_HD)):
        quarter = width // 4
        inv = np.float32(10000.0) ** (-np.arange(quarter, dtype=np.float32) / quarter)
        for f in range(P):
            g = f % width
            axis, half, j = g // (2 * quarter), (g // quarter) % 2, g % quarter
            pos = (t // GRID_W if axis == 0 else t % GRID_W).astype(np.float32)
            angle = pos * inv[j]
            c[f, cos:cos + T] = np.cos(angle)
            c[f, sin:sin + T] = np.sin(angle)
            if half == 0:
                c[f + quarter, rot + f] = -1.0
            else:
                c[f - quarter, rot + f] = 1.0
    c[:, C_MASK:C_MASK + T] = np.where(t[:, None] <= t[None, :], 0.0, MASKED)
    c[:, C_MASK + T:C_MASK + 2 * T] = np.where(t[:, None] >= t[None, :], 0.0, MASKED)
    for direction in range(2):
        for kind in range(2):
            for stream in range(2):
                for h in range(HEADS):
                    col = C_SEL + 16 * (4 * direction + 2 * kind + stream) + 8 * stream + h
                    c[16 * direction + 8 * kind + h, col] = 1.0
    for stream in range(2):
        c[stream, C_SUM + stream] = 1.0
        c[2 + stream, C_SUM + stream] = 1.0
    c[:, C_COLUMN + 15] = 1.0
    return c


PARAMS = (
    ("b_mod", DEPTH * 6 * KD), ("norm1_g", DEPTH * KD), ("norm2_g", DEPTH * KD), ("final_norm_g", KD),
    ("ffn_conv_w", DEPTH * 3 * 2 * KF), ("ffn_conv_b", DEPTH * 2 * KF), ("ml_conv_w", 3 * 2 * HEADS),
    ("ml_conv_b", 2 * HEADS), ("c_ctx", KD), ("c", KD), ("da_subln_g", 1), ("gq_q_norm_g", 1),
    ("gq_k_norm_g", 1), ("ml_norm_g", 1), ("mla_q_norm_g", Q_RANK // P), ("mla_kv_norm_g", KV_RANK // P),
    ("state_ml_n", 2 * HEADS),
)
PCOL = {}
_at = 0
for _name, _rows in PARAMS:
    PCOL[_name] = _at
    _at += _rows
NPAR = _at
PAR_TILES = -(-NPAR // P)


class Tally:

    def __init__(self, sem):
        self.sem, self.base = sem, 0

    def at(self, n):
        return self.base + n

    def advance(self, n):
        self.base += n


def wait(eng, sem, value):
    if not isinstance(value, int) or value > 0:
        eng.wait_ge(sem, value)


class Phase:

    def __init__(self, load, iters, groups, per_group, mods=0, iter0=0, by_halves=True):
        self.load, self.iters, self.groups, self.per_group, self.mods, self.iter0 = \
            load, iters, groups, per_group, mods, iter0
        self.seq = []
        for g in range(max(groups, mods)):
            own = [("own", g, k) for k in range(per_group)] if g < groups else []
            mod = [("mod", g, k) for k in range(MOD_SLABS)] if g < mods else []
            if own and mod:
                self.seq += [own[0], *(slab for pair in zip(own[1:], mod) for slab in pair), mod[-1]]
            else:
                self.seq += own + mod
        self.slabs = len(self.seq)
        self.ends = [self.seq.index(("own", g, per_group - 1)) for g in range(groups)]
        self.mod_ends = [self.seq.index(("mod", j, MOD_SLABS - 1)) for j in range(mods)]
        self.by_halves = by_halves
        self.slab0 = self.group0 = self.mod0 = self.half0 = 0
        self.slot0 = [0] * RAW
        self.before = [0] * RAW
        self.next = None
        self.continues = False

    def slab(self, i, s):
        return self.slab0 + i * self.slabs + s

    def group(self, i, g):
        return self.group0 + i * self.groups + g

    def half(self, i, g):
        return self.half0 + i * self.groups + g

    def mod_group(self, i, j):
        return self.mod0 + i * self.mods + j

    def loads_of(self, slot):
        return (self.slabs - slot + RAW - 1) // RAW if self.slabs > slot else 0

    def first_bank(self, g):
        return 0 if self.mods else GROUP * (g % 2)


def plan(phases):
    slab = group = mod = half = 0
    held, last = [0] * RAW, [0] * RAW
    for n, ph in enumerate(phases):
        ph.slab0, ph.group0, ph.mod0, ph.half0 = slab, group, mod, half
        ph.slot0, ph.before = list(held), list(last)
        ph.continues = n > 0 and not phases[n - 1].mods and phases[n - 1].groups % 2 == 0
        for slot in range(RAW):
            k = ph.loads_of(slot)
            held[slot] += k * ph.iters
            if k:
                last[slot] = slab + (ph.iters - 1) * ph.slabs + slot + RAW * (k - 1) + 1
        slab += ph.iters * ph.slabs
        group += ph.iters * ph.groups
        mod += ph.iters * ph.mods
        half += ph.iters * ph.groups if ph.by_halves else 0
        ph.next = phases[n + 1] if n + 1 < len(phases) else None
    assert mod == DEPTH * MOD_GROUPS


def rolled(eng, iters, body):
    if iters == 1:
        body(0, True, True)
        return
    body(0, True, False)
    if iters > 2:
        with eng.Fori(1, iters - 1) as i:
            body(i, False, False)
    body(iters - 1, False, True)


def over(ap, n):
    return ap.unsqueeze(len(ap.shape)).broadcast_to([*ap.shape, n])


def trunk(nc, ins, outs):
    ctx = ExitStack()
    with ctx:
        def sb(name, shape, dt=F32, scope=ctx):
            return scope.enter_context(nc.sbuf_tensor(name, shape, dt))

        def tally(name):
            return Tally(ctx.enter_context(nc.semaphore(name)))

        raw = sb("raw", [P, RAW, CHUNKS, SLABW])
        w_hi = sb("w_hi", [P, SPLIT, CHUNKS, SLABW], F32R)
        w_lo = sb("w_lo", [P, SPLIT, CHUNKS, SLABW], F32R)
        x = sb("x", [P, KD, NT])
        const = sb("const", [P, NCONST])
        par = sb("par", [P, NPAR])
        mod = sb("mod", [P, DEPTH, 6 * KD, 2])
        norm_gain = sb("norm_gain", [P, DEPTH, 2, KD, 2])
        cond_split = sb("cond_split", [P, KD, 4], F32R)
        mod_rows = sb("mod_rows", [4, 2, SLABW])
        lam = sb("lam", [P, 1])
        gate_b = sb("gate_b", [4 * HEADS, 1])
        m0 = sb("m0", [2 * HEADS, 2])
        banks = ctx.enter_context(nc.psum_tensor("banks", [P, 8, 512], F32))

        ident = const[:, C_IDENT:C_IDENT + P]
        ones = const[:, C_ONES:C_ONES + P]

        landed = [tally(f"landed{s}") for s in range(RAW)]
        hi_done = tally("hi_done")
        lo_done = tally("lo_done")
        slab_used = tally("slab_used")
        half_ready = tally("half_ready")
        part_copied = tally("part_copied")
        summed = tally("summed")
        gated = tally("gated")
        resid = tally("resid")
        rows_out = tally("rows_out")
        rows_turned = tally("rows_turned")
        mod_done = tally("mod_done")
        tap = [tally(f"tap{n}") for n in range(3)]
        silu_done = tally("silu_done")
        act_done = tally("act_done")
        mov_hi = tally("mov_hi")
        mov_lo = tally("mov_lo")
        small_in = tally("small_in")
        tokens_in = tally("tokens_in")
        lam_in = tally("lam_in")
        state_in = tally("state_in")
        pool_step = tally("pool_step")
        stored = tally("stored")
        pe_step = tally("pe_step")
        act_step = tally("act_step")
        dve_step = tally("dve_step")

        def columns(w, first, width=SLABW):
            v = w.rearrange("(s c p) n -> s p c n", c=CHUNKS, p=P)
            return lambda s, n0: v[s, :, :, bass.ds(n0, width) if not isinstance(n0, int) else slice(n0, n0 + width)]

        def plain(w, first, groups_per_iter):
            get = columns(w, first)

            def load(sp, slot, i, g, k):
                return sp.dma_start(raw[:, slot], get(k, first + SLABW * (i * groups_per_iter + g)))
            return load

        def ffn_up_load(w, iter0):
            get = columns(w, 0)

            def load(sp, slot, i, g, k):
                return sp.dma_start(raw[:, slot], get(k, SLABW * (i + iter0) + D_FF * g))
            return load

        def odd_tail_load(w):
            def load(sp, slot, i, g, k):
                n0, width = ((4 * D // 2, 416), (4 * D // 2 + 416, 448))[g]
                v = w.rearrange("(s c p) n -> s p c n", c=CHUNKS, p=P)
                return sp.dma_start(raw[:, slot, :, 0:width], v[k, :, :, n0:n0 + width])
            return load

        def uq_load(sp, slot, i, g, k):
            v = ins["mla_w_uq"][0].rearrange("(s c p) n -> s p c n", c=CHUNKS, p=P)
            return sp.dma_start(raw[:, slot, :, 0:384], v[k, :, :, 384 * g:384 * g + 384])

        def ukv_load(sp, slot, i, g, k):
            v = ins["mla_w_ukv"][0].rearrange("(c p) n -> p c n", p=P)
            return sp.dma_start(raw[:, slot], v[:, :, SLABW * (2 * g + k):SLABW * (2 * g + k + 1)])

        KS = KD // CHUNKS
        ph = {
            "mod": Phase(None, 4, 0, 0, mods=2),
            "even_in": Phase(plain(ins["even_w_in"][0], 0, 2), 4, 2, KS, mods=2),
            "even_in_end": Phase(plain(ins["even_w_in"][0], 8 * SLABW, 1), 1, 1, KS),
            ("out", 0): Phase(plain(ins["even_w_out"][0], 0, 2), 2, 2, KS, mods=2),
            ("up", 0): Phase(ffn_up_load(ins["ffn_w_up"][0], 0), 2, 2, KS, mods=2),
            ("up_end", 0): Phase(ffn_up_load(ins["ffn_w_up"][0], 2), 9, 2, KS, mods=2, iter0=2),
            "odd_qk": Phase(plain(ins["odd_w_in"][0], 0, 2), 2, 2, KS, mods=2),
            "odd_vo": Phase(plain(ins["odd_w_in"][0], 4 * SLABW, 4), 1, 4, KS, mods=2),
            "odd_tail": Phase(odd_tail_load(ins["odd_w_in"][0]), 1, 2, KS, by_halves=False),
            "uq": Phase(uq_load, 1, 4, Q_RANK // (P * CHUNKS), by_halves=False),
            "ukv": Phase(ukv_load, 1, 2, 2, by_halves=False),
            ("out", 1): Phase(plain(ins["odd_w_out"][0], 0, 2), 2, 2, KS),
            ("up", 1): Phase(ffn_up_load(ins["ffn_w_up"][1], 0), 11, 2, KS),
        }
        for l in range(DEPTH):
            ph["down", l] = Phase(plain(ins["ffn_w_down"][l], 0, 2), 2, 2, KF // CHUNKS)
        order = ["mod", "even_in", "even_in_end", ("out", 0), ("up", 0), ("up_end", 0), ("down", 0),
                 "odd_qk", "odd_vo", "odd_tail", "uq", "ukv", ("out", 1), ("up", 1), ("down", 1)]
        plan([ph[k] for k in order])

        def mod_columns(f, i, j):
            l = f.mod0 // MOD_GROUPS
            return l, GROUP * (f.mod_group(i, j) - l * MOD_GROUPS)

        def mod_load(sp, f, slot, i, j, k):
            l, tile = mod_columns(f, i, j)
            return sp.dma_start(raw[:, slot], columns(ins["w_mod"][l], 0)(k, P * tile))

        def load_slab(sp, f, i, s, in_slot_before):
            slot = s % RAW
            wait(sp, hi_done.sem, in_slot_before)
            wait(sp, lo_done.sem, in_slot_before)
            kind, g, k = f.seq[s]
            dma = f.load(sp, slot, i, g, k) if kind == "own" else mod_load(sp, f, slot, i, g, k)
            dma.then_inc(landed[slot].sem, 16)

        def sp_first(sp, f):
            if f is not None:
                for s in range(min(RAW, f.slabs)):
                    load_slab(sp, f, 0, s, f.before[s])

        def sp_stream(sp, f):
            def body(i, first, last):
                for s in range(RAW, f.slabs):
                    load_slab(sp, f, i, s, f.slab(i, s - RAW) + 1)
                if last:
                    sp_first(sp, f.next)
                else:
                    for s in range(RAW):
                        newest = s + RAW * (f.loads_of(s) - 1)
                        load_slab(sp, f, i + 1, s, f.slab(i, newest) + 1)
            rolled(sp, f.iters, body)

        def slab_landed(f, i, s):
            slot = s % RAW
            return landed[slot].sem, 16 * (f.slot0[slot] + i * f.loads_of(slot) + s // RAW + 1)

        def split_hi(act, f, i, s):
            q = f.slab(i, s)
            act.wait_ge(*slab_landed(f, i, s))
            wait(act, slab_used.sem, q - SPLIT + 1)
            act.activation(w_hi[:, s % SPLIT], raw[:, s % RAW], ACT.Copy).then_inc(hi_done.sem, 1)

        def split_lo(dve, f, i, s):
            q = f.slab(i, s)
            dve.wait_ge(hi_done.sem, q + 1)
            wait(dve, slab_used.sem, q - SPLIT + 1)
            dve.tensor_tensor(w_lo[:, s % SPLIT], raw[:, s % RAW], w_hi[:, s % SPLIT].bitcast(F32),
                              ALU.subtract).then_inc(lo_done.sem, 1)

        def split_stream(eng, f, split, places, also=None, left=()):
            def body(i, first, last):
                for s in range(f.slabs):
                    run_pieces(f, places, i, s, first, left)
                    ahead = s + SPLIT
                    if ahead < f.slabs:
                        due = f, i, ahead
                    elif not last:
                        due = f, i + 1, ahead - f.slabs
                    else:
                        due = f.next, 0, ahead - f.slabs
                    if due[0] is not None:
                        split(eng, *due)
                        if also:
                            also(eng, *due)
            rolled(eng, f.iters, body)
            return left_over(f, places)

        def placed(f, pieces, mod_pieces):
            return [(end + d, piece, g)
                    for ends, all_ in ((f.ends, pieces), (f.mod_ends, mod_pieces))
                    for g, end in enumerate(ends) for d, piece in enumerate(all_) if piece is not None]

        def run_pieces(f, places, i, s, first, left=()):
            if first:
                for at, call in left:
                    if at == s or (s == f.slabs - 1 and at > s):
                        call()
            for at, piece, g in places:
                if at == s:
                    piece(i, g)
                elif at == s + f.slabs and not first:
                    piece(i - 1, g)

        def left_over(f, places):
            return [(s - f.slabs, lambda piece=piece, g=g: piece(f.iters - 1, g))
                    for s in range(f.slabs, 2 * f.slabs) for at, piece, g in places if at == s]

        def product_stream(pe, f, slab_products, left):
            places = placed(f, [], [None] * 3 + [lambda i, j: turn_mod(pe, f, i, j)])

            def body(i, first, last):
                for s, (kind, g, k) in enumerate(f.seq):
                    pe.wait_ge(lo_done.sem, f.slab(i, s) + 1)
                    if kind == "mod":
                        products = mod_products(pe, f, i, s, g, k)
                    else:
                        if k == 0:
                            alternating = not f.mods and (f.continues or not (first and g == 0))
                            out = 2 * (f.group(i, g) - (1 if alternating else 0))
                            wait(pe, summed.sem, out - 1 if f.by_halves else out)
                            if first and g == 1 and not f.mods:
                                wait(pe, mod_done.sem, f.mod0)
                        if f.by_halves:
                            products = slab_products(i, s, g, k, out if k == 0 else 0)
                        else:
                            products = slab_products(i, s, g, k)
                    products.then_inc(slab_used.sem, 1)
                    run_pieces(f, places, i, s, first, left)
            rolled(pe, f.iters, body)
            return left_over(f, places)

        def mod_products(pe, f, i, s, j, k):
            if k == 0:
                wait(pe, rows_out.sem, f.mod_group(i, j) - 1)
            for c in range(CHUNKS):
                for n, half in enumerate((w_hi, w_lo)):
                    mm = pe.matmul(banks[0:4, MOD_ROWS + j % 2, :], cond_split[:, CHUNKS * k + c, :],
                                   half[:, s % SPLIT, c, :], start=(k == 0 and c == 0 and n == 0),
                                   stop=(k == MOD_SLABS - 1 and c == CHUNKS - 1 and n == 1))
            return mm

        def copy_mod_rows(act, f, i, j):
            n = f.mod_group(i, j)
            act.wait_ge(slab_used.sem, f.slab(i, f.mod_ends[j]) + 1)
            wait(act, rows_turned.sem, n - 1)
            act.activation(mod_rows[:, j % 2, :], banks[0:4, MOD_ROWS + j % 2, :], ACT.Copy).then_inc(rows_out.sem, 1)

        def turn_mod(pe, f, i, j):
            n = f.mod_group(i, j)
            pe.wait_ge(rows_out.sem, n + 1)
            wait(pe, mod_done.sem, n - 1)
            for t in range(GROUP):
                mm = pe.matmul(banks[:, MOD_COLS + j % 2, 2 * t:2 * t + 2], mod_rows[:, j % 2, P * t:P * t + P],
                               const[0:4, C_SUM:C_SUM + 2], start=True, stop=True)
            mm.then_inc(rows_turned.sem, 1)

        def add_mod_bias(dve, f, i, j):
            dve.wait_ge(rows_turned.sem, f.mod_group(i, j) + 1)
            l, tile = mod_columns(f, i, j)
            bias = par[:, PCOL["b_mod"] + l * 6 * KD:PCOL["b_mod"] + (l + 1) * 6 * KD]
            dve.tensor_tensor(mod[:, l, tiles_at(tile, GROUP), :],
                              banks[:, MOD_COLS + j % 2, 0:2 * GROUP].rearrange("p (t s) -> p t s", s=2),
                              over(bias[:, tiles_at(tile, GROUP)], 2), ALU.add).then_inc(mod_done.sem, 1)

        def tiles_at(n, k):
            return slice(n, n + k) if isinstance(n, int) else bass.ds(n, k)

        def tile_products(pe, slot, first_bank, moving, start, stop, out):
            for t in range(GROUP):
                bank = banks[:, first_bank + t]
                cols = slice(P * t, P * t + P)
                if t == GROUP // 2:
                    wait(pe, summed.sem, out)
                for c in range(CHUNKS):
                    pe.matmul(bank, w_hi[:, slot, c, cols], moving[:, c, :], start=start and c == 0, stop=False)
                    mm = pe.matmul(bank[:, 0:NT], w_lo[:, slot, c, cols], moving[:, c, 0:NT],
                                   start=False, stop=stop and c == CHUNKS - 1)
                if stop and t == GROUP // 2 - 1:
                    mm.then_inc(half_ready.sem, 1)
            return mm

        def split_products(pe, f, operand, ready, left):
            def one(i, s, g, k, out):
                ready(i, s)
                return tile_products(pe, s % SPLIT, f.first_bank(g), operand(s, k), k == 0, k == f.per_group - 1, out)
            return product_stream(pe, f, one, left)

        with ExitStack() as scope:
            rows = sb("rows", [P, PAR_TILES, P], scope=scope)
            tokens = sb("tokens", [P, 2, D], scope=scope)
            cond_f = sb("cond_f", [P, KD, 2], scope=scope)
            lam_rows = sb("lam_rows", [P, 4 * SUB], scope=scope)
            lam_prod = sb("lam_prod", [P, 2 * SUB], scope=scope)
            lam_sum = sb("lam_sum", [P, 2], scope=scope)
            first = ph[order[0]]

            pieces_in = []
            for name, n in PARAMS:
                flat = ins[name].rearrange(
                    {1: "(n p) -> n p", 2: "a (n p) -> (a n) p", 3: "a b (n p) -> (a b n) p",
                     4: "a b c (n p) -> (a b c n) p", 5: "a b c d (n p) -> (a b c d n) p"}[len(ins[name].shape)], p=P)
                r = 0
                while r < n:
                    tile, row = divmod(PCOL[name] + r, P)
                    k = min(n - r, P - row)
                    pieces_in.append((rows[row:row + k, tile, :], flat[r:r + k, :]))
                    r += k
            with nc.Block() as block:
                @block.sync
                def _(sp):
                    sp.dma_start(const[:], ins["constants"]).then_inc(small_in.sem, 16)
                    for dst, src in pieces_in:
                        sp.dma_start(dst, src).then_inc(small_in.sem, 16)
                    sp_first(sp, first)

                @block.gpsimd
                def _(pool):
                    pool.memset(m0[:], 0.0).then_inc(pool_step.sem, 1)
                    pool.wait_ge(pool_step.sem, 1)
                    pool.dma_start(m0[HEADS:2 * HEADS, :], ins["state_ml_m"][0, 0].rearrange("d h -> h d"),
                                   allow_slow_non_contiguous=True).then_inc(state_in.sem, 16)
                    pool.dma_start(gate_b[:], ins["ml_gate_b"].rearrange("a n -> n a"),
                                   allow_slow_non_contiguous=True).then_inc(state_in.sem, 16)
                    pool.wait_ge(state_in.sem, 32)

                @block.scalar
                def _(act):
                    act.dma_start(tokens[:, 0, :], ins["x_prompt"][0]).then_inc(tokens_in.sem, 16)
                    act.dma_start(tokens[:, 1, :], ins["x_sample"][0]).then_inc(tokens_in.sem, 16)
                    act.dma_start(lam_rows[:], ins["da_lambda"].rearrange("a b c -> a (b c)")
                                  .broadcast_to([P, 4 * SUB])).then_inc(lam_in.sem, 16)
                    act.wait_ge(dve_step.sem, 1)
                    act.activation(cond_f[:], par[:, PCOL["c_ctx"]:PCOL["c_ctx"] + 2 * KD]
                                   .rearrange("p (s k) -> p k s", s=2), ACT.Silu).then_inc(act_step.sem, 1)
                    act.wait_ge(act_step.sem, 1)
                    act.activation(cond_split[:, :, 0:2], cond_f[:], ACT.Copy).then_inc(act_step.sem, 1)
                    act.wait_ge(dve_step.sem, 4)
                    act.activation(lam_sum[:], lam_sum[:], ACT.Exp).then_inc(act_step.sem, 1)
                    for s in range(SPLIT):
                        split_hi(act, first, 0, s)

                @block.vector
                def _(dve):
                    dve.wait_ge(pe_step.sem, 1)
                    for b in range(0, PAR_TILES, 4):
                        k = min(4, PAR_TILES - b) * P
                        k = min(k, NPAR - b * P)
                        cp = dve.tensor_copy(par[:, b * P:b * P + k], banks[:, b // 4, 0:k])
                    cp.then_inc(dve_step.sem, 1)
                    dve.wait_ge(act_step.sem, 2)
                    dve.tensor_tensor(cond_split[:, :, 2:4], cond_f[:], cond_split[:, :, 0:2].bitcast(F32),
                                      ALU.subtract).then_inc(dve_step.sem, 1)
                    dve.wait_ge(lam_in.sem, 16)
                    lr = lam_rows[:].rearrange("p (a b c) -> p a b c", a=2, b=2)
                    dve.tensor_tensor(lam_prod[:].rearrange("p (a c) -> p a c", a=2), lr[:, :, 0], lr[:, :, 1],
                                      ALU.mult).then_inc(dve_step.sem, 1)
                    dve.wait_ge(dve_step.sem, 3)
                    dve.tensor_reduce(lam_sum[:], lam_prod[:].rearrange("p (a c) -> p a c", a=2), X_AXIS,
                                      ALU.add).then_inc(dve_step.sem, 1)
                    for s in range(2):
                        for b in range(4):
                            dve.wait_ge(pe_step.sem, 2 + 4 * s + b)
                            dve.tensor_copy(x[:, 4 * b:4 * b + 4, T * s:T * s + T],
                                            banks[:, 3 + (4 * s + b) % 4, :].rearrange("p (k t) -> p k t", k=4)
                                            ).then_inc(dve_step.sem, 1)
                    dve.wait_ge(act_step.sem, 3)
                    dve.tensor_tensor(lam[:], lam_sum[:, 0:1], lam_sum[:, 1:2], ALU.subtract
                                      ).then_inc(dve_step.sem, 1)
                    dve.wait_ge(dve_step.sem, 13)
                    dve.tensor_scalar(lam[:], lam[:], LAM_INIT, None, ALU.add).then_inc(dve_step.sem, 1)
                    for s in range(SPLIT):
                        split_lo(dve, first, 0, s)

                @block.tensor
                def _(pe):
                    pe.wait_ge(small_in.sem, 16 * (1 + len(pieces_in)))
                    for b in range(PAR_TILES):
                        k = min(P, NPAR - b * P)
                        tr = pe.transpose(banks[:, b // 4, P * (b % 4):P * (b % 4) + k], rows[0:k, b, :],
                                          ident[0:k, 0:k])
                    tr.then_inc(pe_step.sem, 1)
                    pe.wait_ge(tokens_in.sem, 32)
                    for s in range(2):
                        for b in range(4):
                            if s:
                                pe.wait_ge(dve_step.sem, 5 + b)
                            for k in range(4):
                                tr = pe.transpose(banks[:, 3 + (4 * s + b) % 4, P * k:P * k + P],
                                                  tokens[:, s, P * (4 * b + k):P * (4 * b + k) + P], ident)
                            tr.then_inc(pe_step.sem, 1)
            small_in.advance(16 * (1 + len(pieces_in)))
            pool_step.advance(1)
            pe_step.advance(9)
            act_step.advance(3)
            dve_step.advance(14)

        A, V, E = act_step, dve_step, pe_step

        def norm_before(l, n, xs, h, r, sums):
            gains, gain = norm_gain[:, l, n], par[:, PCOL[f"norm{n + 1}_g"] + l * KD:PCOL[f"norm{n + 1}_g"] + (l + 1) * KD]
            shifts, scales = mod[:, l, 3 * n * KD:(3 * n + 1) * KD, :], mod[:, l, (3 * n + 1) * KD:(3 * n + 2) * KD, :]
            PARTS = ((0, 2), (2, 4), (4, 8), (8, 12), (12, 16))
            MULTIPLIED, MODULATED, SPLIT_UP = (7, 9, 12, 15, 18), (8, 10, 13, 16, 19), (11, 14, 17, 20, 21)

            def four(buf, b):
                return buf[:, 4 * b:4 * b + 4]

            def part(buf, b):
                return buf[:, PARTS[b][0]:PARTS[b][1]]

            def four_sum(b):
                return sums[:, b]

            def on_act(act):
                for b in range(4):
                    act.activation(four(h, b), four(x, b), ACT.Square).then_inc(A.sem, 1)
                act.wait_ge(V.sem, V.at(5))
                act.activation(r[:], r[:], ACT.Sqrt).then_inc(A.sem, 1)
                for b in range(len(PARTS)):
                    act.wait_ge(V.sem, V.at(MODULATED[b]))
                    act.activation(part(xs, b)[:, :, 0:NT], part(h, b), ACT.Copy).then_inc(A.sem, 1)

            def on_pe(pe):
                for b in range(4):
                    pe.wait_ge(V.sem, V.at(1 + b))
                    mm = pe.matmul(banks[:, 0, 0:NT], ones, four_sum(b), start=b == 0, stop=b == 3)
                mm.then_inc(E.sem, 1)

            def on_dve(dve):
                for b in range(4):
                    dve.wait_ge(A.sem, A.at(1 + b))
                    dve.tensor_reduce(four_sum(b), four(h, b).rearrange("p k t -> p t k"), X_AXIS, ALU.add
                                      ).then_inc(V.sem, 1)
                dve.scalar_tensor_tensor(gains, scales, 1.0, over(gain, 2), ALU.add, ALU.mult)
                dve.wait_ge(E.sem, E.at(1))
                dve.tensor_scalar(r[:], banks[:, 0, 0:NT], 1.0 / D, EPS, ALU.mult, ALU.add).then_inc(V.sem, 1)
                dve.wait_ge(A.sem, A.at(5))
                dve.reciprocal(r[:], r[:]).then_inc(V.sem, 1)
                dve.wait_ge(V.sem, V.at(6))

                def low(b):
                    dve.wait_ge(A.sem, A.at(6 + b))
                    dve.tensor_tensor(part(xs, b)[:, :, NT:2 * NT], part(h, b), part(xs, b)[:, :, 0:NT].bitcast(F32),
                                      ALU.subtract).then_inc(V.sem, 1)
                for b, (k0, k1) in enumerate(PARTS):
                    dve.tensor_tensor(part(h, b), part(x, b), r[:].unsqueeze(1).broadcast_to([P, k1 - k0, NT]), ALU.mult
                                      ).then_inc(V.sem, 1)
                    dve.wait_ge(V.sem, V.at(MULTIPLIED[b]))
                    for k in range(k0, k1):
                        for st in range(2):
                            tile = h[:, k, T * st:T * st + T]
                            ts = dve.tensor_scalar(tile, tile, gains[:, k, st:st + 1], shifts[:, k, st:st + 1],
                                                   ALU.mult, ALU.add)
                    ts.then_inc(V.sem, 1)
                    if b:
                        low(b - 1)
                low(len(PARTS) - 1)

            def ready(pe, k):
                b = max(n for n, (k0, _) in enumerate(PARTS) if k0 <= CHUNKS * k)
                pe.wait_ge(V.sem, V.at(SPLIT_UP[b]))
            return dict(act=on_act, pe=on_pe, dve=on_dve, steps=(10, 21, 1), ready=ready)

        def split_before(src, xs):
            def on_act(act):
                for b in range(4):
                    act.activation(xs[:, 4 * b:4 * b + 4, 0:NT], src[:, 4 * b:4 * b + 4], ACT.Copy).then_inc(A.sem, 1)

            def on_dve(dve):
                for b in range(4):
                    dve.wait_ge(A.sem, A.at(1 + b))
                    dve.tensor_tensor(xs[:, 4 * b:4 * b + 4, NT:2 * NT], src[:, 4 * b:4 * b + 4],
                                      xs[:, 4 * b:4 * b + 4, 0:NT].bitcast(F32), ALU.subtract).then_inc(V.sem, 1)
            return dict(act=on_act, dve=on_dve, steps=(4, 4, 0),
                        ready=lambda pe, k: pe.wait_ge(V.sem, V.at(1 + CHUNKS * k // 4)))

        def project(phases, operands, act_pieces, dve_pieces, moving=(None, None, None, None), products=None,
                    before=None):
            before = before or {}

            def ahead(name, eng):
                if name in before:
                    before[name](eng)

            def ready(pe, f, i, s):
                kind, g, k = f.seq[s]
                if "ready" in before and f is phases[0] and isinstance(i, int) and i == 0 and g == 0:
                    before["ready"](pe, k)
                if f is moving[0]:
                    moving[3](pe, f, i, s)

            def also(split_moving):
                def split_if_due(eng, f, i, s):
                    if f is moving[0]:
                        split_moving(eng, f, i, s)
                return split_if_due if moving[0] is not None else None

            def bound(eng, f, pieces):
                return [p and (lambda i, g, p=p: p(eng, f, i, g)) for p in pieces]

            with nc.Block() as block:
                @block.sync
                def _(sp):
                    ahead("sp", sp)
                    for f in phases:
                        sp_stream(sp, f)

                @block.scalar
                def _(act):
                    ahead("act", act)
                    left = []
                    for n, f in enumerate(phases):
                        left = split_stream(act, f, split_hi, placed(f, bound(act, f, act_pieces[n]),
                                                              bound(act, f, [copy_mod_rows])),
                                            also=also(moving[1]),
                                            left=left)
                    for _, call in left:
                        call()

                @block.vector
                def _(dve):
                    ahead("dve", dve)
                    left = []
                    for n, f in enumerate(phases):
                        left = split_stream(dve, f, split_lo, placed(f, bound(dve, f, dve_pieces[n]),
                                                              bound(dve, f, [None] * 5 + [add_mod_bias])),
                                            also=also(moving[2]),
                                            left=left)
                    for _, call in left:
                        call()

                @block.tensor
                def _(pe):
                    ahead("pe", pe)
                    left = []
                    for n, f in enumerate(phases):
                        own = products and products[n]
                        if own:
                            left = product_stream(pe, f, lambda i, s, g, k, f=f, own=own: own(pe, f, i, s, g, k), left)
                        else:
                            left = split_products(pe, f, operands[n], lambda i, s, f=f: ready(pe, f, i, s), left)
                    for _, call in left:
                        call()
            for counted, n in zip((A, V, E), before.get("steps", (0, 0, 0))):
                counted.advance(n)

        def group_used(f, i, g):
            return f.slab(i, f.ends[g]) + 1

        def half_banks(f, g, n):
            return slice(f.first_bank(g) + 2 * n, f.first_bank(g) + 2 * n + 2)

        def products_done(eng, f, i, g, n):
            if n == 0:
                eng.wait_ge(half_ready.sem, f.half(i, g) + 1)
            else:
                eng.wait_ge(slab_used.sem, group_used(f, i, g))

        def copy_part(tb):
            def piece(act, f, i, g):
                wait(act, summed.sem, 2 * f.group(i, g))
                for n in range(2):
                    products_done(act, f, i, g, n)
                    act.activation(tb[:, 2 * n:2 * n + 2], banks[:, half_banks(f, g, n), NT:2 * NT], ACT.Copy
                                   ).then_inc(part_copied.sem, 1)
            return piece

        def sum_halves(dve, f, i, g, tb, dst):
            for n in range(2):
                dve.wait_ge(part_copied.sem, 2 * f.group(i, g) + n + 1)
                dve.tensor_tensor(dst(n), banks[:, half_banks(f, g, n), 0:NT], tb[:, 2 * n:2 * n + 2], ALU.add
                                  ).then_inc(summed.sem, 1)

        def add_parts(tb, dst, first=0):
            def piece(dve, f, i, g):
                tile0 = first + GROUP * (i * f.groups + g)
                sum_halves(dve, f, i, g, tb, lambda n: dst[:, tiles_at(tile0 + 2 * n, 2), :])
            return piece

        def residual_pieces(tb, gate):
            def act_piece(act, f, i, g):
                wait(act, resid.sem, f.group(i, g) - resid_skip[0])
                for n in range(2):
                    products_done(act, f, i, g, n)
                    act.activation(tb[:, 2 * n:2 * n + 2], banks[:, half_banks(f, g, n), NT:2 * NT], ACT.Copy
                                   ).then_inc(part_copied.sem, 1)

            def add(dve, f, i, g):
                sum_halves(dve, f, i, g, tb, lambda n: tb[:, 2 * n:2 * n + 2])

            def multiply(dve, f, i, g):
                dve.wait_ge(summed.sem, 2 * f.group(i, g) + 2)
                tile0 = GROUP * (i * f.groups + g)
                four = tb[:].rearrange("p t (s n) -> p (t s) n", s=2)
                dve.tensor_tensor(four, four, over(gate[:, tiles_at(tile0, GROUP), :].rearrange("p t s -> p (t s)"), T),
                                  ALU.mult).then_inc(gated.sem, 1)

            def update(dve, f, i, g):
                dve.wait_ge(gated.sem, f.group(i, g) - resid_skip[0] + 1)
                xt = x[:, tiles_at(GROUP * (i * f.groups + g), GROUP), :]
                dve.tensor_tensor(xt, xt, tb[:], ALU.add).then_inc(resid.sem, 1)
            return [act_piece], [add, multiply, update]

        resid_skip = [0]

        def convolution(tb, u, y, weight, bias, count, y_free):
            def add(dve, f, i, g):
                wait(dve, tap[2].sem, tap[2].at(count(f, i, g)))
                sum_halves(dve, f, i, g, tb, lambda n: u[:, 2 * n:2 * n + 2])

            def middle(act, f, i, g):
                act.wait_ge(summed.sem, 2 * f.group(i, g) + 2)
                y_free(act, f, i, g)
                for t in range(GROUP):
                    mid = act.activation(y[:, g % 2, t], u[:, t], ACT.Identity, bias=bias(f, i, g, t),
                                         scale=weight(f, i, g, 1, t))
                mid.then_inc(tap[0].sem, 1)

            def neighbour(which):
                to, frm = ((1, 0), None, (0, 1))[which]
                before, after = (tap[0], tap[1]) if which == 0 else (tap[1], tap[2])

                def piece(dve, f, i, g):
                    dve.wait_ge(before.sem, before.at(count(f, i, g) + 1))
                    for t in range(GROUP):
                        yt = y[:, g % 2, t].rearrange("p (s n) -> p s n", s=2)[:, :, to:to + T - 1]
                        ut = u[:, t].rearrange("p (s n) -> p s n", s=2)[:, :, frm:frm + T - 1]
                        added = dve.scalar_tensor_tensor(yt, ut, weight(f, i, g, which, t), yt, ALU.mult, ALU.add)
                    added.then_inc(after.sem, 1)
                return piece
            return [copy_part(tb), None, middle], [add, None, None, neighbour(0), None, neighbour(2)]

        project([ph["mod"]], [None], [[]], [[]])

        def ffn(l):
            ups, down = [ph[k, l] for k in ("up", "up_end") if (k, l) in ph], ph["down", l]
            with ExitStack() as scope:
                acts = sb(f"acts{l}", [P, KF, NT], scope=scope)
                xs = sb(f"xs_ffn{l}", [P, KD, 2 * NT], F32R, scope)
                r = sb(f"r_ffn{l}", [P, NT], scope=scope)
                tb = sb(f"tb{l}", [P, GROUP, NT], scope=scope)
                u = sb(f"u{l}", [P, GROUP, NT], scope=scope)
                y = sb(f"y{l}", [P, 2, GROUP, NT], scope=scope)
                conv_col = PCOL["ffn_conv_w"] + l * 3 * 2 * KF
                bias_col = PCOL["ffn_conv_b"] + l * 2 * KF

                def column(base):
                    return lambda f, i, g, t: par[:, tiles_at(base + g * KF + t + GROUP * (i + f.iter0), 1)]

                def weight(f, i, g, which, t):
                    return column(conv_col + which * 2 * KF)(f, i, g, t)

                def y_free(act, f, i, g):
                    wait(act, act_done.sem, act_done.at(i + f.iter0))

                def silu(act, f, i, g):
                    if g == 0:
                        act.wait_ge(tap[2].sem, tap[2].at(f.group(i, g) - ups[0].group0 + 1))
                        act.activation(y[:, 0], y[:, 0], ACT.Silu).then_inc(silu_done.sem, 1)

                def multiply(dve, f, i, g):
                    if g == 1:
                        dve.wait_ge(tap[2].sem, tap[2].at(f.group(i, g) - ups[0].group0 + 1))
                        dve.wait_ge(silu_done.sem, silu_done.at(i + f.iter0 + 1))
                        dve.tensor_tensor(acts[:, tiles_at(GROUP * (i + f.iter0), GROUP), :], y[:, 0], y[:, 1], ALU.mult
                                          ).then_inc(act_done.sem, 1)

                act_pieces, dve_pieces = convolution(tb, u, y, weight, column(bias_col),
                                                     lambda f, i, g: f.group(i, g) - ups[0].group0, y_free)
                def chunk0(s):
                    return CHUNKS * (s % down.per_group)

                def slot_of(s):
                    return slice(CHUNKS * (s % SPLIT), CHUNKS * (s % SPLIT) + CHUNKS)

                def moving_hi(act, f, i, s):
                    if s < f.per_group and isinstance(i, int) and i == 0:
                        act.wait_ge(act_done.sem, act_done.at(chunk0(s) // GROUP + 1))
                    act.activation(xs[:, slot_of(s), 0:NT], acts[:, chunk0(s):chunk0(s) + CHUNKS], ACT.Copy
                                   ).then_inc(mov_hi.sem, 1)

                def moving_lo(dve, f, i, s):
                    dve.wait_ge(mov_hi.sem, mov_hi.at(i * f.slabs + s + 1))
                    dve.tensor_tensor(xs[:, slot_of(s), NT:2 * NT], acts[:, chunk0(s):chunk0(s) + CHUNKS],
                                      xs[:, slot_of(s), 0:NT].bitcast(F32), ALU.subtract).then_inc(mov_lo.sem, 1)

                iters = sum(f.iters for f in ups)
                resid_skip[0] += 2 * iters
                act_resid, dve_resid = residual_pieces(tb, mod[:, l, 5 * KD:6 * KD, :])
                project([*ups, down], [lambda s, k: xs[:, CHUNKS * k:CHUNKS * k + CHUNKS]] * len(ups)
                        + [lambda s, k: xs[:, slot_of(s)]],
                        [[*act_pieces, None, None, None, silu]] * len(ups) + [act_resid],
                        [[*dve_pieces, multiply]] * len(ups) + [dve_resid],
                        moving=(down, moving_hi, moving_lo,
                                lambda pe, f, i, s: pe.wait_ge(mov_lo.sem, mov_lo.at(i * f.slabs + s + 1))),
                        before=norm_before(l, 1, xs, acts[:, 0:KD], r, tb))
                for t in tap:
                    t.advance(2 * iters)
                for t in (silu_done, act_done):
                    t.advance(iters)
                mov_hi.advance(down.iters * down.slabs)
                mov_lo.advance(down.iters * down.slabs)

        def out_projection(l, mix):
            f = ph["out", l]
            with ExitStack() as scope:
                xs = sb(f"xs_out{l}", [P, KD, 2 * NT], F32R, scope)
                tb = sb(f"tb_out{l}", [P, GROUP, NT], scope=scope)
                act_pieces, dve_pieces = residual_pieces(tb, mod[:, l, 2 * KD:3 * KD, :])
                project([f], [lambda s, k: xs[:, CHUNKS * k:CHUNKS * k + CHUNKS]], [act_pieces], [dve_pieces],
                        before=split_before(mix, xs))

        def feature_rms(src, work, gains, together=False, loads=None):
            n = src.shape[1]
            flat = work.rearrange("p n t -> p (n t)")
            sq = flat[:, 0:n * NT].rearrange("p (n t) -> p n t", n=n)
            rows = P if together else n
            r = flat[0:rows, 0:NT]
            parts = range(0, n, 2)
            with nc.Block() as block:
                @block.sync
                def _(sp):
                    if loads:
                        loads(sp)

                @block.scalar
                def _(act):
                    for b in parts:
                        act.activation(sq[:, b:b + 2], src[:, b:b + 2], ACT.Square).then_inc(A.sem, 1)
                    act.wait_ge(V.sem, V.at(1))
                    act.activation(r, r, ACT.Sqrt).then_inc(A.sem, 1)

                @block.tensor
                def _(pe):
                    for k in range(n):
                        if k % 2 == 0:
                            pe.wait_ge(A.sem, A.at(k // 2 + 1))
                        lhs = ones if together else const[:, C_COLUMN + 15 - k:C_COLUMN + 15 - k + n]
                        mm = pe.matmul(banks[0:rows, 0, 0:NT], lhs, sq[:, k], start=k == 0, stop=k == n - 1)
                    mm.then_inc(E.sem, 1)
                    if not together:
                        pe.wait_ge(V.sem, V.at(2))
                        for k in range(n):
                            mm = pe.matmul(banks[:, 1 + k // 2, NT * (k % 2):NT * (k % 2) + NT],
                                           const[0:n, C_IDENT + k:C_IDENT + k + 1].broadcast_to([n, P]), r,
                                           start=True, stop=True)
                            if k % 2:
                                mm.then_inc(E.sem, 1)

                @block.vector
                def _(dve):
                    dve.wait_ge(E.sem, E.at(1))
                    dve.tensor_scalar(r, banks[0:rows, 0, 0:NT], 1.0 / (P * n if together else P), EPS, ALU.mult, ALU.add
                                      ).then_inc(V.sem, 1)
                    dve.wait_ge(A.sem, A.at(len(parts) + 1))
                    dve.reciprocal(r, r).then_inc(V.sem, 1)
                    dve.wait_ge(V.sem, V.at(2))
                    for b in parts:
                        if not together:
                            dve.wait_ge(E.sem, E.at(b // 2 + 2))
                        scale = (r.unsqueeze(1).broadcast_to([P, 2, NT]) if together
                                 else banks[:, 1 + b // 2, :].rearrange("p (n t) -> p n t", n=2))
                        ts = dve.tensor_tensor(src[:, b:b + 2], src[:, b:b + 2], scale, ALU.mult)
                    ts.then_inc(V.sem, 1)
                    dve.wait_ge(V.sem, V.at(3))
                    for tiles, gain, factor in gains:
                        dve.tensor_scalar(src[:, tiles], src[:, tiles], gain, factor, ALU.mult, ALU.mult)
            A.advance(len(parts) + 1)
            V.advance(3)
            E.advance(1 if together else 1 + len(parts))

        def rotate(src, rot_col, cos_col, sin_col, work):
            R, n = src.shape[0:2]
            tmp = work.rearrange("p n t -> p (n t)")[0:R, 0:n * T].rearrange("p (n t) -> p n t", n=n)
            with nc.Block() as block:
                @block.tensor
                def _(pe):
                    for b in range(0, n, 4):
                        k = min(4, n - b)
                        mm = pe.matmul(banks[0:R, b // 4, 0:k * T], const[0:R, rot_col:rot_col + R], src[:, b:b + k, :],
                                       start=True, stop=True)
                    mm.then_inc(E.sem, 1)

                @block.vector
                def _(dve):
                    def table(c):
                        return const[0:R, c:c + T].unsqueeze(1).broadcast_to([R, n, T])
                    dve.wait_ge(E.sem, E.at(1))
                    turned = banks[0:R].rearrange("p b n -> p (b n)")[:, 0:n * T].rearrange("p (n t) -> p n t", n=n)
                    dve.tensor_tensor(tmp, turned, table(sin_col), ALU.mult)
                    dve.tensor_tensor(src, src, table(cos_col), ALU.mult).then_inc(V.sem, 1)
                    dve.wait_ge(V.sem, V.at(1))
                    dve.tensor_tensor(src, src, tmp, ALU.add)
            V.advance(1)
            E.advance(1)

        def turn_tiles(srcs, dst, loaded=0):
            with nc.Block() as block:
                batches = [srcs[b:b + 4] for b in range(0, len(srcs), 4)]

                @block.tensor
                def _(pe):
                    wait(pe, small_in.sem, loaded)
                    for b, batch in enumerate(batches):
                        wait(pe, A.sem, A.at(b - 7) if b >= 8 else 0)
                        for j, s in enumerate(batch):
                            rows, cols = s.shape
                            tr = pe.transpose(banks[0:cols, b % 8, P * j:P * j + rows], s, ident[0:rows, 0:rows])
                        tr.then_inc(E.sem, 1)

                @block.scalar
                def _(act):
                    for b, batch in enumerate(batches):
                        act.wait_ge(E.sem, E.at(b + 1))
                        cols, rows = batch[0].shape[1], batch[0].shape[0]
                        act.activation(dst[0:cols, 4 * b:4 * b + len(batch), 0:rows],
                                       banks[0:cols, b % 8, 0:P * len(batch)].rearrange("p (n r) -> p n r", r=P)[:, :, 0:rows],
                                       ACT.Copy).then_inc(A.sem, 1)
            A.advance(len(batches))
            E.advance(len(batches))

        scores_in = tally("scores_in")
        scores_out = tally("scores_out")
        row_max = tally("row_max")
        exped = tally("exped")
        row_sum = tally("row_sum")
        row_inv = tally("row_inv")
        inv_signed = tally("inv_signed")
        scaled = tally("scaled")
        weights_in = tally("weights_in")
        w_turned = tally("w_turned")
        w_copied = tally("w_copied")
        mixed = tally("mixed")
        mixed_out = tally("mixed_out")

        def attention(blocks, tag, stores=None):
            with ExitStack() as scope:
                e = sb(f"e_{tag}", [P, 2, 2048], scope=scope)
                wt = sb(f"wt_{tag}", [P, 2, 8, P], scope=scope)
                mx = sb(f"mx_{tag}", [P, 2, 16], scope=scope)
                inv = sb(f"inv_{tag}", [P, 2, 16], scope=scope)
                scores = banks[:, 0:4].rearrange("p b n -> p (b n)")
                rounds, at = [], 0
                for b, k in enumerate(blocks):
                    heads = k["rows"] // (2 if k["diff"] else 1)
                    chunks = k["keys"] // T
                    per = 8 // chunks
                    rounds.append([(at + j, per * j, per, chunks) for j in range(heads // per)])
                    at += heads // per

                def rows_of(buf, k):
                    return buf[:, 0:k["rows"] * k["keys"]].rearrange("p (r l) -> p r l", r=k["rows"])

                with nc.Block() as block:
                    @block.sync
                    def _(sp):
                        if stores:
                            stores(sp)

                    @block.tensor
                    def _(pe):
                        def score(b):
                            k = blocks[b]
                            wait(pe, scores_out.sem, scores_out.at(b) if b else 0)
                            out = rows_of(scores, k)
                            for row in range(k["rows"]):
                                mm = k["score"](pe, row, out[:, row])
                            mm.then_inc(scores_in.sem, 1)

                        def mix_values(b):
                            k = blocks[b]
                            w = rows_of(e[:, b % 2], k)
                            pe.wait_ge(weights_in.sem, weights_in.at(b + 1))
                            for n, h0, per, chunks in rounds[b]:
                                wait(pe, w_copied.sem, w_copied.at(n) if n else 0)
                                for j in range(per):
                                    for c in range(chunks):
                                        m = j * chunks + c
                                        tr = pe.transpose(banks[:, 4 + m // 4, P * (m % 4):P * (m % 4) + P],
                                                          w[:, h0 + j, T * c:T * c + T], ident)
                                tr.then_inc(w_turned.sem, 1)
                                pe.wait_ge(w_copied.sem, w_copied.at(n + 1))
                                wait(pe, mixed_out.sem, mixed_out.at(n) if n else 0)
                                for j in range(per):
                                    for c in range(chunks):
                                        mm = pe.matmul(banks[:, 6 + j // 4, P * (j % 4):P * (j % 4) + P],
                                                       k["value"](h0 + j, c), wt[:, n % 2, j * chunks + c],
                                                       start=c == 0, stop=c == chunks - 1)
                                mm.then_inc(mixed.sem, 1)
                        score(0)
                        for b in range(len(blocks)):
                            if b + 1 < len(blocks):
                                score(b + 1)
                            mix_values(b)

                    @block.vector
                    def _(dve):
                        def prepare(b):
                            k = blocks[b]
                            s, w = rows_of(scores, k), rows_of(e[:, b % 2], k)
                            dve.wait_ge(scores_in.sem, scores_in.at(b + 1))
                            top = mx[:, b % 2, 0:k["rows"]]
                            dve.tensor_reduce(top, s, X_AXIS, ALU.max).then_inc(row_max.sem, 1)
                            dve.wait_ge(row_max.sem, row_max.at(b + 1))
                            if b >= 2:
                                dve.wait_ge(w_turned.sem, w_turned.at(rounds[b - 2][-1][0] + 1))
                            dve.tensor_tensor(w, s, over(top, k["keys"]), ALU.subtract).then_inc(scores_out.sem, 1)

                        def normalise(b):
                            k = blocks[b]
                            w = rows_of(e[:, b % 2], k)
                            r = inv[:, b % 2, 0:k["rows"]]
                            dve.wait_ge(exped.sem, exped.at(b + 1))
                            dve.tensor_reduce(r, w, X_AXIS, ALU.add).then_inc(row_sum.sem, 1)
                            dve.wait_ge(row_sum.sem, row_sum.at(b + 1))
                            dve.reciprocal(r, r).then_inc(row_inv.sem, 1)
                            dve.wait_ge(row_inv.sem, row_inv.at(b + 1))
                            if k["diff"]:
                                second = r[:, k["rows"] // 2:]
                                dve.tensor_scalar(second, second, lam[:], -1.0, ALU.mult, ALU.mult
                                                  ).then_inc(inv_signed.sem, 1)
                                dve.wait_ge(inv_signed.sem, inv_signed.at(b + 1))
                                dve.tensor_tensor(w, w, over(r, k["keys"]), ALU.mult).then_inc(scaled.sem, 1)
                                dve.wait_ge(scaled.sem, scaled.at(b + 1))
                                w1, w2 = w[:, 0:k["rows"] // 2], w[:, k["rows"] // 2:]
                                dve.tensor_tensor(w1, w1, w2, ALU.add).then_inc(weights_in.sem, 1)
                            else:
                                dve.tensor_tensor(w, w, over(r, k["keys"]), ALU.mult).then_inc(weights_in.sem, 1)
                        prepare(0)
                        for b in range(len(blocks)):
                            normalise(b)
                            if b + 1 < len(blocks):
                                prepare(b + 1)

                    @block.scalar
                    def _(act):
                        def exponentials(b):
                            k = blocks[b]
                            w = rows_of(e[:, b % 2], k)
                            act.wait_ge(scores_out.sem, scores_out.at(b + 1))
                            act.activation(w, w, ACT.Exp, scale=k["scale"]).then_inc(exped.sem, 1)

                        def carry(b):
                            for n, h0, per, chunks in rounds[b]:
                                act.wait_ge(w_turned.sem, w_turned.at(n + 1))
                                if n >= 2:
                                    act.wait_ge(mixed.sem, mixed.at(n - 1))
                                act.activation(wt[:, n % 2], banks[:, 4:6].rearrange("p b (n t) -> p (b n) t", t=P),
                                               ACT.Copy).then_inc(w_copied.sem, 1)
                                if n == rounds[b][0][0] and b + 1 < len(blocks):
                                    exponentials(b + 1)
                                act.wait_ge(mixed.sem, mixed.at(n + 1))
                                out = banks[:, 6:8].rearrange("p b (n t) -> p (b n) t", t=P)
                                act.activation(blocks[b]["dst"](h0, per), out[:, 0:per], ACT.Copy
                                               ).then_inc(mixed_out.sem, 1)
                        exponentials(0)
                        for b in range(len(blocks)):
                            carry(b)
                diffs = sum(k["diff"] for k in blocks)
                assert all(k["diff"] for k in blocks[:diffs])
                for t in (scores_in, scores_out, row_max, exped, row_sum, row_inv, weights_in):
                    t.advance(len(blocks))
                for t in (inv_signed, scaled):
                    t.advance(diffs)
                for t in (w_turned, w_copied, mixed, mixed_out):
                    t.advance(at)

        def even_layer(l):
            with ExitStack() as outer:
                mix = sb("mix0", [P, 2 * HEADS, NT], scope=outer)
                with ExitStack() as scope:
                    qkv = sb("qkv", [P, EVEN_TILES, NT], scope=scope)
                    kv_cache = sb("kv_cache", [P, 2, 10, P], scope=scope)

                    def load_cache(sp):
                        for c in range(2):
                            sp.dma_start(kv_cache[:, 0, 0:HEADS].rearrange("t h (c d) -> t h c d", c=2)[:, :, c],
                                         ins["cache_da_k"][0, 0, :, c].rearrange("h t d -> t h d")
                                         ).then_inc(small_in.sem, 16)
                        sp.dma_start(kv_cache[:, 1, 0:HEADS], ins["cache_da_v"][0, 0].rearrange("h t d -> t h d")
                                     ).then_inc(small_in.sem, 16)
                        for n, name in enumerate(("cache_gq_k", "cache_gq_v")):
                            sp.dma_start(kv_cache[:, n, HEADS:10], ins[name][0, 0].rearrange("h t d -> t h d")
                                         ).then_inc(small_in.sem, 16)

                    with ExitStack() as inner:
                        xs = sb("xs_even", [P, KD, 2 * NT], F32R, inner)
                        r = sb("r_even", [P, NT], scope=inner)
                        tb = sb("tb_even", [P, GROUP, NT], scope=inner)
                        a, b = ph["even_in"], ph["even_in_end"]
                        project([a, b], [lambda s, k: xs[:, CHUNKS * k:CHUNKS * k + CHUNKS]] * 2,
                                [[copy_part(tb)], [copy_part(tb)]],
                                [[add_parts(tb, qkv)], [add_parts(tb, qkv, GROUP * a.iters * a.groups)]],
                                before=dict(norm_before(l, 0, xs, qkv[:, 0:KD], r, tb), sp=load_cache))
                        resid_skip[0] += EVEN_TILES // GROUP
                    QA, KA, VA, QB, KB, VB = 0, 8, 16, 24, 32, 34
                    turned = sb("turned0", [P, 40, P], scope=scope)
                    with ExitStack() as inner:
                        work = sb("work0", [P, 10, NT], scope=inner)
                        feature_rms(qkv[:, QB:KB + KV_HEADS], work,
                                    [(slice(0, HEADS), par[:, PCOL["gq_q_norm_g"]:PCOL["gq_q_norm_g"] + 1], 1.0),
                                     (slice(HEADS, HEADS + KV_HEADS),
                                      par[:, PCOL["gq_k_norm_g"]:PCOL["gq_k_norm_g"] + 1], 1.0)])
                        rotate(qkv[:, 0:2 * HEADS, T:NT], C_ROT_SUB, C_COS_SUB, C_SIN_SUB, work)
                        rotate(qkv[:, QB:KB + KV_HEADS, T:NT], C_ROT_HD, C_COS_HD, C_SIN_HD, work)
                    prompt = [qkv[:, t, 0:T] for t in (*range(KA, KA + 8), *range(VA, VA + 8), 32, 33, 34, 35)]
                    sample = [qkv[:, t, T:NT] for t in (*range(VA, VA + 8), 34, 35)]
                    turn_tiles(prompt + sample + [kv_cache[:, 0, h] for h in range(10)], turned, small_in.at(80))
                    small_in.advance(80)
                    KA_P, VA_P, KB_P, VB_P, VA_S, VB_S, K_CACHE = 0, 8, 16, 18, 20, 28, 30

                    def store_new(sp):
                        for c in range(2):
                            sp.dma_start(outs["new_da_k"][0, 0, :, c].rearrange("h t d -> t h d"),
                                         turned[:, KA_P:KA_P + 8].rearrange("t h (c d) -> t h c d", c=2)[:, :, c]
                                         ).then_inc(stored.sem, 16)
                        for name, t0, n in (("new_da_v", VA_P, 8), ("new_gq_k", KB_P, 2), ("new_gq_v", VB_P, 2)):
                            sp.dma_start(outs[name][0, 0].rearrange("h t d -> t h d"), turned[:, t0:t0 + n]
                                         ).then_inc(stored.sem, 16)
                        sp.wait_ge(stored.sem, stored.at(80))

                    def sub(c):
                        return slice(SUB * c, SUB * c + SUB)

                    def da_prompt(pe, row, out):
                        c, h = divmod(row, HEADS)
                        return pe.matmul(out, qkv[sub(c), QA + h, 0:T], qkv[sub(c), KA + h, 0:T], start=True, stop=True)

                    def da_sample(h0):
                        def score(pe, row, out):
                            c, h = row // 4, h0 + row % 4
                            q = qkv[sub(c), QA + h, T:NT]
                            pe.matmul(out[:, 0:T], q, turned[sub(c), K_CACHE + h], start=True, stop=True)
                            return pe.matmul(out[:, T:2 * T], q, qkv[sub(c), KA + h, T:NT], start=True, stop=True)
                        return score

                    def gq_prompt(pe, row, out):
                        return pe.matmul(out, qkv[:, QB + row, 0:T], qkv[:, KB + row // 4, 0:T], start=True, stop=True)

                    def gq_sample(pe, row, out):
                        g = row // 4
                        pe.matmul(out[:, 0:T], qkv[:, QB + row, T:NT], turned[:, K_CACHE + 8 + g], start=True, stop=True)
                        return pe.matmul(out[:, T:2 * T], qkv[:, QB + row, T:NT], qkv[:, KB + g, T:NT],
                                         start=True, stop=True)

                    def dst(first, stream):
                        return lambda h0, n: mix[:, first + h0:first + h0 + n, T * stream:T * stream + T]

                    def cached(v_cache, v_own, share=1):
                        return lambda h, c: kv_cache[:, 1, v_cache + h // share] if c == 0 else turned[:, v_own + h // share]

                    da = dict(diff=True, scale=SUB ** -0.5)
                    gq = dict(diff=False, scale=P ** -0.5)
                    attention([
                        dict(da, rows=16, keys=T, score=da_prompt, dst=dst(0, 0), value=lambda h, c: turned[:, VA_P + h]),
                        dict(da, rows=8, keys=2 * T, score=da_sample(0), dst=dst(0, 1), value=cached(0, VA_S)),
                        dict(da, rows=8, keys=2 * T, score=da_sample(4), dst=dst(4, 1), value=lambda h, c: cached(4, VA_S + 4)(h, c)),
                        dict(gq, rows=8, keys=T, score=gq_prompt, dst=dst(8, 0), value=lambda h, c: turned[:, VB_P + h // 4]),
                        dict(gq, rows=8, keys=2 * T, score=gq_sample, dst=dst(8, 1), value=cached(8, VB_S, 4)),
                    ], "even", store_new)
                    stored.advance(80)
                    with ExitStack() as inner:
                        work = sb("work1", [P, HEADS, NT], scope=inner)
                        feature_rms(mix[:, 0:HEADS], work,
                                    [(slice(0, HEADS), par[:, PCOL["da_subln_g"]:PCOL["da_subln_g"] + 1], 1.0 - LAM_INIT)])
                out_projection(l, mix)
            ffn(l)

        VM, OM, QD, KV, PE_T = 0, 8, 16, 20, 22

        def mlstm(kq, prj, gates, mix):
            R = 2 * HEADS
            NEG_M, Z, A_, EM, WG = range(5)
            with ExitStack() as scope:
                ee = sb("ee", [P, 4 * HEADS, T], scope=scope)
                va = sb("va", [P, R, P + 1], scope=scope)
                c0 = sb("c0", [P, R, P + 1], scope=scope)
                k_tok = sb("k_tok", [P, HEADS, P], scope=scope)
                qa = sb("qa", [P, R, T], scope=scope)
                sc = sb("sc", [R, 5, 2, T], scope=scope)
                turned = sb("sc_turned", [P, 4, R], scope=scope)
                den = sb("den", [P, 2, HEADS], scope=scope)
                state_n = sb("state_n", [R, 1, P], scope=scope)
                hbuf = mix[:, HEADS:2 * HEADS].rearrange("p a (b t) -> p (a b) t", t=T)

                def ordered(kind, d):
                    return sc[:, kind, d, :] if d == 0 else sc[:, kind, d, ::-1]

                with ExitStack() as inner:
                    gs, ex, lf, bs = (qa[0:R, a:b] for a, b in ((0, 4), (4, 6), (6, 8), (8, 10)))
                    zz = sb("zz", [R, 2, T], scope=inner)
                    mm_ = sb("mm", [R, 2, T], scope=inner)
                    ms = sb("ms", [R, 2, T], scope=inner)
                    zero = sb("zero", [R, T], scope=inner)
                    n_end = sb("n_end", [R, 2], scope=inner)
                    f_rows = gs.rearrange("r (d k) t -> r d k t", k=2)[:, :, 1]
                    i_rows = gs.rearrange("r (d k) t -> r d k t", k=2)[:, :, 0]
                    with nc.Block() as block:
                        @block.sync
                        def _(sp):
                            for d in range(2):
                                sp.dma_start(c0[:, HEADS * d:HEADS * d + HEADS, 0:P],
                                             ins["state_ml_C"][0, 0, d].rearrange("h k v -> k h v")
                                             ).then_inc(small_in.sem, 16)
                            sp.wait_ge(V.sem, V.at(9))
                            sp.dma_start(outs["new_ml_m"][0, 0].rearrange("d h -> h d"), ms[0:HEADS, :, T - 1],
                                         allow_slow_non_contiguous=True).then_inc(stored.sem, 16)
                            sp.wait_ge(stored.sem, stored.at(16))

                        @block.gpsimd
                        def _(pool):
                            pool.memset(zero[:], 0.0).then_inc(pool_step.sem, 1)
                            pool.memset(va[:, :, P:P + 1], 1.0)

                        @block.vector
                        def _(dve):
                            dve.tensor_scalar(gates[:], gates[:], gate_b[:], None, ALU.add).then_inc(V.sem, 1)
                            dve.tensor_scalar(kq[:, 0:HEADS], kq[:, 0:HEADS], P ** -0.5, None, ALU.mult)
                            dve.tensor_copy(c0[:, :, P:P + 1],
                                            par[:, PCOL["state_ml_n"]:PCOL["state_ml_n"] + R].unsqueeze(2))
                            dve.wait_ge(E.sem, E.at(1))
                            dve.tensor_copy(gs, banks[0:R, 0, :].rearrange("r (k t) -> r k t", k=4)
                                            ).then_inc(V.sem, 1)
                            dve.wait_ge(V.sem, V.at(2))
                            dve.scalar_tensor_tensor(ex, f_rows, -1.0, f_rows, ALU.mult, ALU.min
                                                     ).then_inc(V.sem, 1)
                            dve.tensor_scalar(lf, f_rows, 0.0, None, ALU.min).then_inc(V.sem, 1)
                            dve.wait_ge(A.sem, A.at(2))
                            dve.wait_ge(V.sem, V.at(4))
                            dve.tensor_tensor(lf, lf, ex, ALU.subtract).then_inc(V.sem, 1)
                            dve.wait_ge(V.sem, V.at(5))
                            dve.wait_ge(pool_step.sem, pool_step.at(1))
                            for d in range(2):
                                sn = dve.tensor_tensor_scan(bs[:, d], lf[:, d], zero[:], 0.0, ALU.add, ALU.add)
                            sn.then_inc(V.sem, 1)
                            dve.wait_ge(V.sem, V.at(6))
                            dve.tensor_tensor(zz[:], i_rows, bs, ALU.subtract).then_inc(V.sem, 1)
                            dve.wait_ge(V.sem, V.at(7))
                            for d in range(2):
                                sn = dve.tensor_tensor_scan(mm_[:, d], zz[:, d], zz[:, d], m0[:, d:d + 1],
                                                            ALU.max, ALU.max)
                            sn.then_inc(V.sem, 1)
                            dve.wait_ge(V.sem, V.at(8))
                            dve.tensor_tensor(ms[:], bs, mm_[:], ALU.add).then_inc(V.sem, 1)
                            dve.tensor_scalar(n_end[:].unsqueeze(2), mm_[:, :, T - 1:T], -1.0, None, ALU.mult
                                              ).then_inc(V.sem, 1)
                            for d in range(2):
                                dve.tensor_scalar(ordered(NEG_M, d), mm_[:, d], -1.0, None, ALU.mult)
                                dve.tensor_copy(ordered(Z, d), zz[:, d])

                        @block.scalar
                        def _(act):
                            act.wait_ge(V.sem, V.at(3))
                            act.activation(ex, ex, ACT.Exp).then_inc(A.sem, 1)
                            act.wait_ge(A.sem, A.at(1))
                            act.activation(ex, ex, ACT.Ln, bias=1.0).then_inc(A.sem, 1)
                            for b in range(6):
                                act.wait_ge(E.sem, E.at(2 + b))
                                dst = va[:, 4 * b:4 * b + 4, 0:P] if b < 4 else k_tok[:, 4 * b - R:4 * b - R + 4]
                                act.activation(dst, banks[:, 1 + b, :].rearrange("p (n t) -> p n t", t=P), ACT.Copy)
                            act.wait_ge(V.sem, V.at(10))
                            for d in range(2):
                                act.activation(ordered(A_, d), mm_[:, d], ACT.Exp, bias=m0[:, d:d + 1], scale=-1.0)
                                act.activation(ordered(EM, d), ms[:, d], ACT.Exp, scale=-1.0)
                                act.activation(ordered(WG, d), zz[:, d], ACT.Exp, bias=n_end[:, d:d + 1])

                        @block.tensor
                        def _(pe):
                            pe.wait_ge(V.sem, V.at(1))
                            for d in range(2):
                                for kind in range(2):
                                    for s in range(2):
                                        tok = gates[:, T * s:T * s + T]
                                        col = C_SEL + 16 * (4 * d + 2 * kind + s)
                                        mm = pe.matmul(banks[0:R, 0, T * (2 * d + kind):T * (2 * d + kind) + T],
                                                       const[0:4 * HEADS, col:col + R], tok if d == 0 else tok[:, ::-1],
                                                       start=s == 0, stop=s == 1)
                            mm.then_inc(E.sem, 1)
                            tiles = [prj[:, VM + h, T * s:T * s + T] for s in range(2) for h in range(HEADS)]
                            tiles += [kq[:, HEADS + h, 0:T] for h in range(HEADS)]
                            for n, tile in enumerate(tiles):
                                tr = pe.transpose(banks[:, 1 + n // 4, P * (n % 4):P * (n % 4) + P], tile, ident)
                                if n % 4 == 3:
                                    tr.then_inc(E.sem, 1)
                    V.advance(10)
                    A.advance(2)
                    E.advance(7)
                    pool_step.advance(1)
                    stored.advance(16)
                turn_tiles([sc[:, kind, d, :] for kind in (EM, WG) for d in range(2)], turned[:])

                def row(n):
                    return const[0:R, C_IDENT + n:C_IDENT + n + 1].broadcast_to([R, P])
                with nc.Block() as block:
                    @block.sync
                    def _(sp):
                        sp.wait_ge(small_in.sem, small_in.at(32))

                    @block.tensor
                    def _(pe):
                        for j in range(8):
                            d = j // 4
                            pe.matmul(banks[:, j, :], ident, const[:, C_MASK + T * d:C_MASK + T * d + T]
                                      .unsqueeze(1).broadcast_to([P, 4, T]), start=True, stop=False)
                            n0 = (4 * j) % R
                            for m in range(4):
                                pe.matmul(banks[:, j, T * m:T * m + T], row(n0 + m), sc[:, NEG_M, d, :],
                                          start=False, stop=False)
                            mm = pe.matmul(banks[:, j, :], sc[:, Z, d, :],
                                           over(const[0:R, C_IDENT + n0:C_IDENT + n0 + 4], T), start=False, stop=True)
                            mm.then_inc(E.sem, 1)
                        for b in range(4):
                            pe.wait_ge(A.sem, A.at(b + 1))
                            for m in range(4):
                                s, h = divmod(4 * b + m, HEADS)
                                mm = pe.matmul(banks[:, b, T * m:T * m + T], kq[:, HEADS + h, T * s:T * s + T],
                                               kq[:, h, T * s:T * s + T], start=True, stop=True)
                        mm.then_inc(E.sem, 1)
                        for b in range(4):
                            pe.wait_ge(A.sem, A.at(b + 5))
                            for m in range(4):
                                d, h = divmod(4 * b + m, HEADS)
                                mm = pe.matmul(banks[:, 4 + b, T * m:T * m + T], row(HEADS + h), sc[:, A_, d, :],
                                               start=True, stop=True)
                        mm.then_inc(E.sem, 1)

                    @block.scalar
                    def _(act):
                        for j in range(8):
                            act.wait_ge(E.sem, E.at(1 + j))
                            act.activation(ee[:, 4 * j:4 * j + 4], banks[:, j, :].rearrange("p (m t) -> p m t", m=4),
                                           ACT.Exp).then_inc(A.sem, 1)

                    @block.vector
                    def _(dve):
                        dve.wait_ge(E.sem, E.at(9))
                        dve.wait_ge(A.sem, A.at(8))
                        for d in range(2):
                            part = ee[:, R * d:R * d + R]
                            dve.tensor_tensor(part, banks[:, 0:4].rearrange("p b (m t) -> p (b m) t", t=T), part, ALU.mult)
                        dve.wait_ge(E.sem, E.at(10))
                        for d in range(2):
                            dve.tensor_tensor(qa[:, HEADS * d:HEADS * d + HEADS],
                                              banks[:, 4 + 2 * d:6 + 2 * d].rearrange("p b (m t) -> p (b m) t", t=T),
                                              kq[:, 0:HEADS, T:NT], ALU.mult)
                small_in.advance(32)
                E.advance(10)
                A.advance(8)

                def pair_banks(n):
                    return banks[:, 4 * (n % 2):4 * (n % 2) + 4].rearrange("p b (j w) -> p (b j) w", j=2)
                with nc.Block() as block:
                    @block.tensor
                    def _(pe):
                        for n in range(4):
                            d, s = divmod(n, 2)
                            wait(pe, V.sem, V.at(3 * (n - 2) + 3) if n >= 2 else 0)
                            for h in range(HEADS):
                                out = pair_banks(n)[:, h, 0:P + 1]
                                mm = pe.matmul(out, ee[:, R * d + HEADS * s + h], va[:, HEADS * s + h],
                                               start=True, stop=s == 0)
                                if s == 1:
                                    mm = pe.matmul(out, qa[:, HEADS * d + h], c0[:, HEADS * d + h],
                                                   start=False, stop=True)
                            mm.then_inc(E.sem, 1)

                    @block.scalar
                    def _(act):
                        for n in range(4):
                            act.wait_ge(E.sem, E.at(n + 1))
                            if n >= 2:
                                act.wait_ge(V.sem, V.at(3 * (n - 2) + 3))
                            act.activation(den[:, n % 2].unsqueeze(2), pair_banks(n)[:, :, P:P + 1], ACT.Abs
                                           ).then_inc(A.sem, 1)

                    @block.vector
                    def _(dve):
                        for n in range(4):
                            d, s = divmod(n, 2)
                            dn = den[:, n % 2]
                            dve.wait_ge(A.sem, A.at(n + 1))
                            dve.tensor_tensor(dn, dn, turned[:, d, HEADS * s:HEADS * s + HEADS], ALU.max
                                              ).then_inc(V.sem, 1)
                            dve.wait_ge(V.sem, V.at(3 * n + 1))
                            dve.reciprocal(dn, dn).then_inc(V.sem, 1)
                            dve.wait_ge(V.sem, V.at(3 * n + 2))
                            hs = hbuf[:, HEADS * s:HEADS * s + HEADS]
                            dst = hs if d == 0 else ee[:, HEADS * s:HEADS * s + HEADS]
                            dve.tensor_tensor(dst, pair_banks(n)[:, :, 0:P], over(dn, P), ALU.mult
                                              ).then_inc(V.sem, 1)
                        for s in range(2):
                            dve.wait_ge(V.sem, V.at(9 + 3 * s))
                            hs = hbuf[:, HEADS * s:HEADS * s + HEADS]
                            dve.tensor_tensor(hs, hs, ee[:, HEADS * s:HEADS * s + HEADS], ALU.add)
                V.advance(12)
                A.advance(4)
                E.advance(4)

                kw = ee[:, 0:R]
                new_c = c0
                with nc.Block() as block:
                    @block.sync
                    def _(sp):
                        for d in range(2):
                            sp.wait_ge(V.sem, V.at(3 + d))
                            sp.dma_start(outs["new_ml_C"][0, 0, d].rearrange("h k v -> k h v"),
                                         new_c[:, HEADS * d:HEADS * d + HEADS, 0:P]).then_inc(stored.sem, 16)

                    @block.vector
                    def _(dve):
                        for d in range(2):
                            dve.tensor_tensor(kw[:, HEADS * d:HEADS * d + HEADS], k_tok[:],
                                              over(turned[:, 2 + d, 0:HEADS], P), ALU.mult).then_inc(V.sem, 1)
                        for d in range(2):
                            dve.wait_ge(E.sem, E.at(d + 1))
                            dve.tensor_copy(new_c[:, HEADS * d:HEADS * d + HEADS], pair_banks(d)[:, :, 0:P + 1]
                                            ).then_inc(V.sem, 1)
                        dve.wait_ge(A.sem, A.at(1))
                        r = den[:].rearrange("p a b -> p (a b)")
                        dve.tensor_reduce(r, qa[:], X_AXIS, ALU.add).then_inc(V.sem, 1)
                        dve.wait_ge(V.sem, V.at(5))
                        dve.tensor_scalar(r, r, 1.0 / P, EPS, ALU.mult, ALU.add).then_inc(V.sem, 1)
                        dve.wait_ge(A.sem, A.at(2))
                        dve.reciprocal(r, r).then_inc(V.sem, 1)
                        dve.wait_ge(V.sem, V.at(7))
                        dve.tensor_tensor(hbuf, hbuf, over(r, P), ALU.mult).then_inc(V.sem, 1)
                        for b in range(4):
                            dve.wait_ge(E.sem, E.at(3 + b))
                            s, h = divmod(4 * b, HEADS)
                            dve.scalar_tensor_tensor(
                                mix[:, h:h + 4, T * s:T * s + T], banks[:, b, :].rearrange("p (n t) -> p n t", t=T),
                                par[:, PCOL["ml_norm_g"]:PCOL["ml_norm_g"] + 1], prj[:, OM + h:OM + h + 4, T * s:T * s + T],
                                ALU.mult, ALU.mult)

                    @block.scalar
                    def _(act):
                        act.activation(qa[:], hbuf, ACT.Square).then_inc(A.sem, 1)
                        act.wait_ge(V.sem, V.at(6))
                        r = den[:].rearrange("p a b -> p (a b)")
                        act.activation(r, r, ACT.Sqrt).then_inc(A.sem, 1)
                        act.activation(prj[:, OM:OM + HEADS], prj[:, OM:OM + HEADS], ACT.Sigmoid).then_inc(A.sem, 1)

                    @block.tensor
                    def _(pe):
                        for d in range(2):
                            pe.wait_ge(V.sem, V.at(d + 1))
                            for h in range(HEADS):
                                mm = pe.matmul(pair_banks(d)[:, h, 0:P + 1], kw[:, HEADS * d + h], va[:, h],
                                               start=True, stop=True)
                            mm.then_inc(E.sem, 1)
                        pe.wait_ge(V.sem, V.at(8))
                        pe.wait_ge(A.sem, A.at(3))
                        for b in range(4):
                            for m in range(4):
                                tr = pe.transpose(banks[:, b, P * m:P * m + P], hbuf[:, 4 * b + m], ident)
                            tr.then_inc(E.sem, 1)
                V.advance(8)
                A.advance(3)
                E.advance(6)
                turn_tiles([new_c[:, :, P]], state_n[:])
                with nc.Block() as block:
                    @block.sync
                    def _(sp):
                        sp.dma_start(outs["new_ml_n"][0, 0].rearrange("d h k -> (d h) k"), state_n[:, 0]
                                     ).then_inc(stored.sem, 16)
                        sp.wait_ge(stored.sem, stored.at(48))
                stored.advance(48)

        def latent_attention(prj, mix):
            KEYS = 3 * T
            with ExitStack() as scope:
                qn = sb("qn", [P, HEADS, NT], scope=scope)
                qp = sb("qp", [SUB, HEADS, NT], scope=scope)
                kn = sb("kn", [P, HEADS, KEYS], scope=scope)
                vt = sb("vt", [P, 3, HEADS, P], scope=scope)
                kp = sb("kp", [SUB, KEYS], scope=scope)
                with ExitStack() as inner:
                    work = sb("work2", [P, 4, NT], scope=inner)
                    cached = sb("cached", [P, 2, P], scope=inner)
                    cached_kpe = sb("cached_kpe", [P, SUB], scope=inner)
                    turned = sb("turned1", [P, 4, P], scope=inner)
                    kpe_turned = sb("kpe_turned", [SUB, 1, P], scope=inner)
                    kpe_tok = sb("kpe_tok", [P, 1, SUB], scope=inner)
                    cq = sb("cq", [P, Q_RANK // P, 2 * NT], F32R, inner)
                    ckv_hi = sb("ckv_hi", [P, 2, KEYS], F32R, inner)
                    ckv_lo = sb("ckv_lo", [P, 2, KEYS], F32R, inner)
                    tb = sb("tb_uq", [P, 4, NT], scope=inner)

                    def load_cache(sp):
                        sp.dma_start(cached[:, 0:2].rearrange("t a b -> t (a b)"), ins["cache_mla_ckv"][0, 0]
                                     ).then_inc(small_in.sem, 16)
                        sp.dma_start(cached_kpe[:], ins["cache_mla_kpe"][0, 0]).then_inc(small_in.sem, 16)

                    for first, n, name in ((QD, 4, "mla_q_norm_g"), (KV, 2, "mla_kv_norm_g")):
                        feature_rms(prj[:, first:first + n], work,
                                    [(slice(k, k + 1), par[:, PCOL[name] + k:PCOL[name] + k + 1], 1.0)
                                     for k in range(n)], together=True, loads=load_cache if first == QD else None)
                    turn_tiles([prj[:, KV, 0:T], prj[:, KV + 1, 0:T], cached[:, 0], cached[:, 1]],
                               turned[:], small_in.at(32))
                    small_in.advance(32)
                    turn_tiles([cached_kpe[:]], kpe_turned[:])
                    turn_tiles([prj[0:SUB, PE_T, 0:T]], kpe_tok[:])
                    rotate(prj[0:SUB, PE_T:PE_T + 1, T:NT], C_ROT_SUB, C_COS_SUB, C_SIN_SUB, work)
                    with nc.Block() as block:
                        @block.sync
                        def _(sp):
                            sp.dma_start(outs["new_mla_ckv"][0, 0], turned[:, 0:2].rearrange("t a b -> t (a b)")
                                         ).then_inc(stored.sem, 16)
                            sp.dma_start(outs["new_mla_kpe"][0, 0], kpe_tok[:, 0]).then_inc(stored.sem, 16)

                        @block.scalar
                        def _(act):
                            act.activation(cq[:, :, 0:NT], prj[:, QD:QD + 4], ACT.Copy).then_inc(A.sem, 1)
                            act.activation(ckv_hi[:, :, 0:NT], prj[:, KV:KV + 2], ACT.Copy).then_inc(A.sem, 1)
                            act.activation(ckv_hi[:, :, NT:KEYS], turned[:, 2:4], ACT.Copy).then_inc(A.sem, 1)

                        @block.vector
                        def _(dve):
                            dve.tensor_copy(kp[:, 0:NT], prj[0:SUB, PE_T])
                            dve.tensor_copy(kp[:, NT:KEYS], kpe_turned[:, 0])
                            dve.wait_ge(A.sem, A.at(3))
                            dve.tensor_tensor(cq[:, :, NT:2 * NT], prj[:, QD:QD + 4], cq[:, :, 0:NT].bitcast(F32),
                                              ALU.subtract)
                            dve.tensor_tensor(ckv_lo[:, :, 0:NT], prj[:, KV:KV + 2], ckv_hi[:, :, 0:NT].bitcast(F32),
                                              ALU.subtract)
                            dve.tensor_tensor(ckv_lo[:, :, NT:KEYS], turned[:, 2:4],
                                              ckv_hi[:, :, NT:KEYS].bitcast(F32), ALU.subtract)
                    A.advance(3)
                    stored.advance(32)

                    def uq_products(pe, f, i, s, g, k):
                        def tile(half, c, t):
                            first = (NOPE + SUB) * (t % 2) + (0 if t < 2 else NOPE)
                            return half[:, s % SPLIT, c, first:first + (NOPE if t < 2 else SUB)]
                        for c in range(CHUNKS):
                            n = CHUNKS * k + c
                            for t in range(4):
                                bank = banks[0:NOPE if t < 2 else SUB, GROUP * (g % 2) + t]
                                pe.matmul(bank, tile(w_hi, c, t), cq[:, n], start=n == 0, stop=False)
                                mm = pe.matmul(bank[:, 0:NT], tile(w_lo, c, t), cq[:, n, 0:NT], start=False,
                                               stop=n == Q_RANK // P - 1)
                        return mm

                    def uq_copy(act, f, i, g):
                        act.wait_ge(slab_used.sem, group_used(f, i, g))
                        wait(act, summed.sem, 2 * f.group(i, g))
                        b = GROUP * (g % 2)
                        act.activation(tb[0:SUB, 2:4], banks[0:SUB, b + 2:b + 4, NT:2 * NT], ACT.Copy)
                        act.activation(tb[:, 0:2], banks[:, b:b + 2, NT:2 * NT], ACT.Copy).then_inc(part_copied.sem, 2)

                    def uq_add(dve, f, i, g):
                        dve.wait_ge(part_copied.sem, 2 * f.group(i, g) + 2)
                        b = GROUP * (g % 2)
                        dve.tensor_tensor(qp[:, 2 * g:2 * g + 2], banks[0:SUB, b + 2:b + 4, 0:NT], tb[0:SUB, 2:4], ALU.add)
                        dve.tensor_tensor(qn[:, 2 * g:2 * g + 2], banks[:, b:b + 2, 0:NT], tb[:, 0:2], ALU.add
                                          ).then_inc(summed.sem, 2)

                    def ukv_products(pe, f, i, s, g, k):
                        if k == 0:
                            wait(pe, summed.sem, 2 * f.group(i, g))
                        hi2, lo2 = (w[:, s % SPLIT].rearrange("p c (h n) -> p c h n", h=2) for w in (w_hi, w_lo))
                        for c in range(2):
                            for h in range(2):
                                for n, (w, a) in enumerate(((hi2, ckv_hi), (hi2, ckv_lo), (lo2, ckv_hi))):
                                    pe.matmul(banks[:, 2 * k + h, 0:KEYS], w[:, c, h, 0:NOPE], a[:, c, :],
                                              start=c == 0 and n == 0, stop=c == 1 and n == 2)
                        for t in range(3):
                            for c in range(2):
                                for n, (w, a) in enumerate(((hi2, ckv_hi), (hi2, ckv_lo), (lo2, ckv_hi))):
                                    mm = pe.matmul(banks[:, 4 + t, 2 * P * k:2 * P * k + 2 * P], a[:, c, T * t:T * t + T],
                                                   w[:, c, :, NOPE:NOPE + P],
                                                   start=c == 0 and n == 0, stop=c == 1 and n == 2)
                        return mm

                    def ukv_keys(act, f, i, g):
                        act.wait_ge(slab_used.sem, group_used(f, i, g))
                        act.activation(kn[:, 4 * g:4 * g + 4], banks[:, 0:4, 0:KEYS], ACT.Copy).then_inc(part_copied.sem, 2)

                    def ukv_values(dve, f, i, g):
                        dve.wait_ge(part_copied.sem, 2 * f.group(i, g) + 2)
                        dve.tensor_copy(vt[:, :, 4 * g:4 * g + 4], banks[:, 4:7, :].rearrange("p t (h n) -> p t h n", h=4)
                                        ).then_inc(summed.sem, 2)

                    project([ph["uq"], ph["ukv"]], [None] * 2, [[uq_copy], [ukv_keys]], [[uq_add], [ukv_values]],
                            products=[uq_products, ukv_products],
                            before=dict(sp=lambda sp: sp.wait_ge(stored.sem, stored.at(0))))
                    resid_skip[0] += 6
                    rotate(qp[:, :, T:NT], C_ROT_SUB, C_COS_SUB, C_SIN_SUB, work)

                def score(stream):
                    cols = slice(0, T) if stream == 0 else slice(T, KEYS)

                    def one(pe, h, out):
                        tok = slice(T * stream, T * stream + T)
                        pe.matmul(out, qn[:, h, tok], kn[:, h, cols], start=True, stop=False)
                        return pe.matmul(out, qp[:, h, tok], kp[:, cols], start=False, stop=True)
                    return one

                common = dict(diff=False, rows=HEADS, scale=(NOPE + SUB) ** -0.5)
                attention([
                    dict(common, keys=T, score=score(0), value=lambda h, c: vt[:, 0, h],
                         dst=lambda h0, n: mix[:, HEADS + h0:HEADS + h0 + n, 0:T]),
                    dict(common, keys=2 * T, score=score(1), value=lambda h, c: vt[:, 1 + c, h],
                         dst=lambda h0, n: mix[:, HEADS + h0:HEADS + h0 + n, T:NT]),
                ], "odd")

        def odd_layer(l):
            with ExitStack() as outer:
                mix = sb("mix1", [P, 2 * HEADS, NT], scope=outer)
                with ExitStack() as scope:
                    prj = sb("prj", [P, 23, NT], scope=scope)
                    gates = sb("gates", [4 * HEADS, NT], scope=scope)
                    with ExitStack() as rec:
                        kq = sb("kq", [P, 2 * HEADS, NT], scope=rec)
                        with ExitStack() as inner:
                            xs = sb("xs_odd", [P, KD, 2 * NT], F32R, inner)
                            r = sb("r_odd", [P, NT], scope=inner)
                            tb = sb("tb_odd", [P, GROUP, NT], scope=inner)
                            u = sb("u_odd", [P, GROUP, NT], scope=inner)
                            y = sb("y_odd", [P, 2, GROUP, NT], scope=inner)
                            fq = ph["odd_qk"]

                            def column(base):
                                return lambda f, i, g, t: par[:, tiles_at(base + GROUP * (i * f.groups + g) + t, 1)]

                            def weight(f, i, g, which, t):
                                return column(PCOL["ml_conv_w"] + which * 2 * HEADS)(f, i, g, t)

                            def count(f, i, g):
                                return f.group(i, g) - fq.group0

                            def y_free(act, f, i, g):
                                wait(act, silu_done.sem, silu_done.at(count(f, i, g) - 1))

                            def silu(act, f, i, g):
                                n = count(f, i, g)
                                act.wait_ge(tap[2].sem, tap[2].at(n + 1))
                                act.activation(kq[:, GROUP * n:GROUP * n + GROUP], y[:, g % 2], ACT.Silu
                                               ).then_inc(silu_done.sem, 1)

                            def tail_products(pe, f, i, s, g, k):
                                spans = ((0, 32), (32, 160), (160, 288), (288, 416)) if g == 0 else \
                                    ((0, 128), (128, 256), (256, 384), (384, 448))
                                for c in range(CHUNKS):
                                    n = CHUNKS * k + c
                                    for t, (a, b) in enumerate(spans):
                                        hi, lo = w_hi[:, s % SPLIT, c, a:b], w_lo[:, s % SPLIT, c, a:b]
                                        bank = banks[0:b - a, GROUP * (g % 2) + t]
                                        pe.matmul(bank, hi, xs[:, n], start=n == 0, stop=False)
                                        mm = pe.matmul(bank[:, 0:NT], lo, xs[:, n, 0:NT], start=False, stop=n == KD - 1)
                                return mm

                            def tail_copy(act, f, i, g):
                                act.wait_ge(slab_used.sem, group_used(f, i, g))
                                wait(act, summed.sem, 2 * f.group(i, g))
                                if g == 0:
                                    act.activation(tb[0:32, 0], banks[0:32, 0, NT:2 * NT], ACT.Copy)
                                    act.activation(tb[:, 1:4], banks[:, 1:4, NT:2 * NT], ACT.Copy).then_inc(part_copied.sem, 2)
                                else:
                                    act.activation(tb[0:SUB, 3], banks[0:SUB, 7, NT:2 * NT], ACT.Copy)
                                    act.activation(tb[:, 0:3], banks[:, 4:7, NT:2 * NT], ACT.Copy).then_inc(part_copied.sem, 2)

                            def tail_add(dve, f, i, g):
                                dve.wait_ge(part_copied.sem, 2 * f.group(i, g) + 2)
                                if g == 0:
                                    dve.tensor_tensor(gates[:], banks[0:32, 0, 0:NT], tb[0:32, 0], ALU.add)
                                    dve.tensor_tensor(prj[:, QD:QD + 3], banks[:, 1:4, 0:NT], tb[:, 1:4], ALU.add
                                                      ).then_inc(summed.sem, 2)
                                else:
                                    dve.tensor_tensor(prj[0:SUB, PE_T], banks[0:SUB, 7, 0:NT], tb[0:SUB, 3], ALU.add)
                                    dve.tensor_tensor(prj[:, QD + 3:QD + 6], banks[:, 4:7, 0:NT], tb[:, 0:3], ALU.add
                                                      ).then_inc(summed.sem, 2)

                            act_pieces, dve_pieces = convolution(tb, u, y, weight, column(PCOL["ml_conv_b"]), count,
                                                                 y_free)
                            project([fq, ph["odd_vo"], ph["odd_tail"]],
                                    [lambda s, k: xs[:, CHUNKS * k:CHUNKS * k + CHUNKS]] * 3,
                                    [[*act_pieces, None, None, None, silu], [copy_part(tb)], [tail_copy]],
                                    [dve_pieces, [add_parts(tb, prj)], [tail_add]],
                                    products=[None, None, tail_products],
                                    before=norm_before(l, 0, xs, prj[:, 0:KD], r, tb))
                            for t in (*tap, silu_done):
                                t.advance(4)
                            resid_skip[0] += 10
                        mlstm(kq, prj, gates, mix)
                    latent_attention(prj, mix)
                out_projection(l, mix)
            ffn(l)

        even_layer(0)
        odd_layer(1)

        with ExitStack() as scope:
            xg = sb("xg", [P, KD, NT], scope=scope)
            sq = sb("sq", [P, KD, NT], scope=scope)
            inv = sb("inv_end", [P, 2], scope=scope)
            y_tok = sb("y_tok", [P, 2, KD, P], scope=scope)
            g0 = PCOL["final_norm_g"]
            batches = [(n // 2, n % 2, n % 7) for n in range(8)]
            turned_at = (1, 2, 3, 4, 5, 6, 7, 9)

            def taken_out(eng, n):
                eng.wait_ge(*((A.sem, A.at(6 + n // 2)) if n % 2 == 0 else (V.sem, V.at(7 + n // 2))))

            with nc.Block() as block:
                @block.sync
                def _(sp):
                    for n, (b, st, _bank) in enumerate(batches):
                        taken_out(sp, n)
                        sp.dma_start(outs[("y_prompt", "y_sample")[st]][0, :, 4 * P * b:4 * P * b + 4 * P],
                                     y_tok[:, st, 4 * b:4 * b + 4].rearrange("t k p -> t (k p)")
                                     ).then_inc(stored.sem, 16)
                    sp.wait_ge(stored.sem, stored.at(128))

                @block.scalar
                def _(act):
                    for b in range(4):
                        act.activation(sq[:, 4 * b:4 * b + 4], x[:, 4 * b:4 * b + 4], ACT.Square).then_inc(A.sem, 1)
                    act.wait_ge(V.sem, V.at(5))
                    act.activation(inv[:], inv[:], ACT.Sqrt).then_inc(A.sem, 1)
                    act.wait_ge(V.sem, V.at(6))
                    for n, (b, st, bank) in enumerate(batches):
                        if n % 2 == 0:
                            act.wait_ge(E.sem, E.at(turned_at[n]))
                            act.activation(y_tok[:, st, 4 * b:4 * b + 4], banks[:, bank, :].rearrange("t (k p) -> t k p", p=P),
                                           ACT.Identity, scale=inv[:, st:st + 1]).then_inc(A.sem, 1)

                @block.vector
                def _(dve):
                    for b in range(4):
                        for k in range(4 * b, 4 * b + 4):
                            ts = dve.tensor_scalar(xg[:, k], x[:, k], par[:, g0 + k:g0 + k + 1], None, ALU.mult)
                        ts.then_inc(V.sem, 1)
                    dve.wait_ge(E.sem, E.at(8))
                    dve.tensor_scalar(inv[:], banks[:, 7, 0:2], 1.0 / D, EPS, ALU.mult, ALU.add).then_inc(V.sem, 1)
                    dve.wait_ge(A.sem, A.at(5))
                    dve.reciprocal(inv[:], inv[:]).then_inc(V.sem, 1)
                    dve.wait_ge(V.sem, V.at(6))
                    for n, (b, st, bank) in enumerate(batches):
                        if n % 2:
                            dve.wait_ge(E.sem, E.at(turned_at[n]))
                            dve.tensor_scalar(y_tok[:, st, 4 * b:4 * b + 4], banks[:, bank, :].rearrange("t (k p) -> t k p", p=P),
                                              inv[:, st:st + 1], None, ALU.mult).then_inc(V.sem, 1)

                @block.tensor
                def _(pe):
                    for n, (b, st, bank) in enumerate(batches):
                        pe.wait_ge(V.sem, V.at(1 + b))
                        if n == 7:
                            taken_out(pe, 0)
                        for m in range(4):
                            tr = pe.transpose(banks[:, bank, P * m:P * m + P], xg[:, 4 * b + m, T * st:T * st + T], ident)
                        tr.then_inc(E.sem, 1)
                        if n == 6:
                            pe.wait_ge(A.sem, A.at(4))
                            for stream in range(2):
                                for k in range(KD):
                                    mm = pe.matmul(banks[:, 7, stream:stream + 1], sq[:, k, T * stream:T * stream + T],
                                                   ones[:, 0:1], start=k == 0, stop=k == KD - 1)
                            mm.then_inc(E.sem, 1)


INPUTS = ("x_prompt", "x_sample", "cache_da_k", "cache_da_v", "cache_gq_k", "cache_gq_v", "cache_mla_ckv",
          "cache_mla_kpe", "state_ml_C", "state_ml_n", "state_ml_m", "c", "c_ctx", "norm1_g", "norm2_g", "w_mod",
          "b_mod", "even_w_in", "even_w_out", "da_lambda", "da_subln_g", "gq_q_norm_g", "gq_k_norm_g", "odd_w_in",
          "odd_w_out", "ml_conv_w", "ml_conv_b", "ml_gate_b", "ml_norm_g", "mla_q_norm_g", "mla_w_uq",
          "mla_kv_norm_g", "mla_w_ukv", "ffn_w_up", "ffn_conv_w", "ffn_conv_b", "ffn_w_down", "final_norm_g")
OUTPUTS = (("y_prompt", (1, T, D)), ("y_sample", (1, T, D)), ("new_da_k", (1, 1, HEADS, 2, T, SUB)),
           ("new_da_v", (1, 1, HEADS, T, P)), ("new_gq_k", (1, 1, KV_HEADS, T, P)),
           ("new_gq_v", (1, 1, KV_HEADS, T, P)), ("new_mla_ckv", (1, 1, T, KV_RANK)),
           ("new_mla_kpe", (1, 1, T, SUB)), ("new_ml_C", (1, 1, 2, HEADS, P, P)), ("new_ml_n", (1, 1, 2, HEADS, P)),
           ("new_ml_m", (1, 1, 2, HEADS)))


def kernel(**inputs):
    import concourse.bacc as bacc
    from concourse.bass_utils import run_bass_kernel_spmd

    nc = bacc.Bacc("TRN2", target_bir_lowering=False, num_devices=1)
    arrays, ins, outs = {}, {}, {}
    given = {name: np.ascontiguousarray(inputs[name]) for name in INPUTS}
    given["constants"] = constants()
    for name, a in given.items():
        arrays[f"in_{name}"] = a
        ins[name] = nc.dram_tensor(f"in_{name}", a.shape, mybir.dt.from_np(a.dtype), kind="ExternalInput").ap()
    for name, shape in OUTPUTS:
        outs[name] = nc.dram_tensor(f"out_{name}", shape, F32, kind="ExternalOutput").ap()
    trunk(nc, ins, outs)
    r = run_bass_kernel_spmd(nc, [arrays], core_ids=[0])
    return tuple(r.results[0][f"out_{name}"] for name, _ in OUTPUTS)
```
